# Optimizing a Trainium2 kernel written in Bass

```python
import math
import jax, jax.numpy as jnp
from jax import lax
import numpy as np

D_MODEL = 1024
BATCH = 1
SEQ = 512
DEPTH = 1

CONV_CH = D_MODEL // 2
CONV_WIDTH = 31
MLA_HEADS = 8
QK_NOPE = D_MODEL // 16
QK_ROPE = D_MODEL // 32
V_DIM = D_MODEL // 16
Q_LORA = 3 * D_MODEL // 8
KV_LORA = D_MODEL // 4
N_BRANCH = 2
IN_COLS = 2 * CONV_CH + Q_LORA + KV_LORA + QK_ROPE + N_BRANCH * D_MODEL
MEM_LEN = 256
X_HEADS = 4
X_HEAD_DIM = D_MODEL // 8
D_FF = 4 * D_MODEL
Q_BLOCK = 128
ROPE_THETA = 10000.0
EPS = 1e-6


def rms_norm(x, g):
    xf = x.astype(jnp.float32)
    y = xf * lax.rsqrt(jnp.mean(xf * xf, axis=-1, keepdims=True) + EPS)
    return (y * g.astype(jnp.float32)).astype(x.dtype)

def layer_norm(x, g, b):
    xf = x.astype(jnp.float32)
    mu = jnp.mean(xf, axis=-1, keepdims=True)
    var = jnp.mean(jnp.square(xf - mu), axis=-1, keepdims=True)
    y = (xf - mu) * lax.rsqrt(var + EPS)
    return (y * g.astype(jnp.float32) + b.astype(jnp.float32)).astype(x.dtype)

def rope_tables(positions):
    half = QK_ROPE // 2
    inv_freq = ROPE_THETA ** (-jnp.arange(half, dtype=jnp.float32) / half)
    ang = positions.astype(jnp.float32)[..., None] * inv_freq
    return jnp.cos(ang), jnp.sin(ang)

def apply_rope(t, cos, sin):
    half = t.shape[-1] // 2
    t1, t2 = t[..., :half], t[..., half:]
    c, s = cos.astype(t.dtype), sin.astype(t.dtype)
    return jnp.concatenate([t1 * c - t2 * s, t2 * c + t1 * s], axis=-1)

def conformer_conv(conv_in, conv_w, conv_b, ln_g, ln_b, w_conv_out):
    a, gt = jnp.split(conv_in, 2, axis=-1)
    z = a * jax.nn.sigmoid(gt)
    rhs = conv_w.astype(z.dtype).reshape(CONV_WIDTH, 1, CONV_CH)
    z = lax.conv_general_dilated(
        z, rhs, window_strides=(1,), padding=[(CONV_WIDTH - 1, 0)],
        dimension_numbers=("NWC", "WIO", "NWC"), feature_group_count=CONV_CH)
    z = z + conv_b
    z = layer_norm(z, ln_g, ln_b)
    z = jax.nn.silu(z)
    return z @ w_conv_out

def mla_attention(c_q, c_kv, k_rope_raw, cos, sin, q_norm_g, w_uq, kv_norm_g, w_ukv, w_mla_out):
    B, S, _ = c_q.shape
    q = rms_norm(c_q, q_norm_g) @ w_uq
    q = q.reshape(B, S, MLA_HEADS, QK_NOPE + QK_ROPE)
    q_nope, q_rope = q[..., :QK_NOPE], q[..., QK_NOPE:]
    q_rope = apply_rope(q_rope, cos[:, :, None, :], sin[:, :, None, :])
    kv = rms_norm(c_kv, kv_norm_g) @ w_ukv
    kv = kv.reshape(B, S, MLA_HEADS, QK_NOPE + V_DIM)
    k_nope, v = kv[..., :QK_NOPE], kv[..., QK_NOPE:]
    k_rope = apply_rope(k_rope_raw, cos, sin)

    scale = (QK_NOPE + QK_ROPE) ** -0.5
    n_blk = S // Q_BLOCK
    qn = (q_nope * scale).reshape(B, n_blk, Q_BLOCK, MLA_HEADS, QK_NOPE).transpose(1, 0, 2, 3, 4)
    qr = (q_rope * scale).reshape(B, n_blk, Q_BLOCK, MLA_HEADS, QK_ROPE).transpose(1, 0, 2, 3, 4)
    key_idx = jnp.arange(S)
    neg = jnp.finfo(jnp.float32).min

    def attend(args):
        qn_b, qr_b, blk = args
        s = jnp.einsum("bqhd,bkhd->bhqk", qn_b, k_nope, preferred_element_type=jnp.float32)
        s = s + jnp.einsum("bqhr,bkr->bhqk", qr_b, k_rope, preferred_element_type=jnp.float32)
        q_idx = blk * Q_BLOCK + jnp.arange(Q_BLOCK)
        mask = key_idx[None, :] <= q_idx[:, None]
        s = jnp.where(mask[None, None], s, neg)
        p = jax.nn.softmax(s, axis=-1).astype(v.dtype)
        return jnp.einsum("bhqk,bkhd->bqhd", p, v)

    o = lax.map(attend, (qn, qr, jnp.arange(n_blk)))
    o = o.transpose(1, 0, 2, 3, 4).reshape(B, S, MLA_HEADS * V_DIM)
    return o @ w_mla_out

def memory_cross_attention(u, mem_n, w_xq, w_xkv, w_xo):
    B, S, _ = u.shape
    q = (u @ w_xq).reshape(B, S, X_HEADS, X_HEAD_DIM) * (X_HEAD_DIM ** -0.5)
    kv = (mem_n @ w_xkv).reshape(B, MEM_LEN, 2, X_HEADS, X_HEAD_DIM)
    k, v = kv[:, :, 0], kv[:, :, 1]
    s = jnp.einsum("bqhd,bkhd->bhqk", q, k, preferred_element_type=jnp.float32)
    p = jax.nn.softmax(s, axis=-1).astype(v.dtype)
    o = jnp.einsum("bhqk,bkhd->bqhd", p, v).reshape(B, S, X_HEADS * X_HEAD_DIM)
    return o @ w_xo

def first_inputs(seed: int = 0) -> dict:
    key = jax.random.key(seed)
    ks = jax.random.split(key, 32)
    f32 = jnp.float32

    def w(k, shape, fan_in):
        return jax.random.normal(k, shape, f32) * (fan_in ** -0.5)

    def gain(k, shape):
        return 1.0 + 0.02 * jax.random.normal(k, shape, f32)

    L = DEPTH
    x = jax.random.normal(ks[0], (BATCH, SEQ, D_MODEL), f32)
    mem = jax.random.normal(ks[1], (BATCH, MEM_LEN, D_MODEL), f32)
    offsets = jax.random.randint(ks[2], (BATCH, 1), 0, 4096, dtype=jnp.int32)
    positions = offsets + jnp.arange(SEQ, dtype=jnp.int32)[None, :]
    return {
        "x": x,
        "mem": mem,
        "positions": positions,
        "norm_mix_g": gain(ks[3], (L, D_MODEL)),
        "w_in": w(ks[4], (L, D_MODEL, IN_COLS), D_MODEL),
        "conv_w": w(ks[5], (L, CONV_WIDTH, CONV_CH), CONV_WIDTH),
        "conv_b": 0.02 * jax.random.normal(ks[6], (L, CONV_CH), f32),
        "conv_ln_g": gain(ks[7], (L, CONV_CH)),
        "conv_ln_b": 0.02 * jax.random.normal(ks[8], (L, CONV_CH), f32),
        "w_conv_out": w(ks[9], (L, CONV_CH, D_MODEL), CONV_CH),
        "q_norm_g": gain(ks[10], (L, Q_LORA)),
        "w_uq": w(ks[11], (L, Q_LORA, MLA_HEADS * (QK_NOPE + QK_ROPE)), Q_LORA),
        "kv_norm_g": gain(ks[12], (L, KV_LORA)),
        "w_ukv": w(ks[13], (L, KV_LORA, MLA_HEADS * (QK_NOPE + V_DIM)), KV_LORA),
        "w_mla_out": w(ks[14], (L, MLA_HEADS * V_DIM, D_MODEL), MLA_HEADS * V_DIM),
        "w_out": w(ks[15], (L, D_MODEL, D_MODEL), D_MODEL),
        "norm_xattn_g": gain(ks[16], (L, D_MODEL)),
        "norm_mem_g": gain(ks[17], (L, D_MODEL)),
        "w_xq": w(ks[18], (L, D_MODEL, X_HEADS * X_HEAD_DIM), D_MODEL),
        "w_xkv": w(ks[19], (L, D_MODEL, 2 * X_HEADS * X_HEAD_DIM), D_MODEL),
        "w_xo": w(ks[20], (L, X_HEADS * X_HEAD_DIM, D_MODEL), X_HEADS * X_HEAD_DIM),
        "norm_mlp_g": gain(ks[21], (L, D_MODEL)),
        "w_mlp1": w(ks[22], (L, D_MODEL, D_FF), D_MODEL),
        "w_mlp2": w(ks[23], (L, D_FF, D_MODEL), D_FF),
        "final_norm_g": gain(ks[24], (D_MODEL,)),
    }

def first_block(x, mem, positions, norm_mix_g, w_in, conv_w, conv_b, conv_ln_g, conv_ln_b,
              w_conv_out, q_norm_g, w_uq, kv_norm_g, w_ukv, w_mla_out, w_out,
              norm_xattn_g, norm_mem_g, w_xq, w_xkv, w_xo, norm_mlp_g, w_mlp1, w_mlp2,
              final_norm_g):
    cos, sin = rope_tables(positions)
    B, S, _ = x.shape
    cut = np.cumsum([2 * CONV_CH, Q_LORA, KV_LORA, QK_ROPE]).tolist()
    h = x
    for l in range(DEPTH):
        u = rms_norm(h, norm_mix_g[l])
        proj = u @ w_in[l]
        conv_in, c_q, c_kv, k_rope_raw, gate_logits = jnp.split(proj, cut, axis=-1)
        conv_out = conformer_conv(conv_in, conv_w[l], conv_b[l], conv_ln_g[l], conv_ln_b[l],
                                  w_conv_out[l])
        mla_out = mla_attention(c_q, c_kv, k_rope_raw, cos, sin, q_norm_g[l], w_uq[l],
                                kv_norm_g[l], w_ukv[l], w_mla_out[l])
        gates = jax.nn.sigmoid(gate_logits).reshape(B, S, N_BRANCH, D_MODEL)
        merged = gates[:, :, 0] * conv_out + gates[:, :, 1] * mla_out
        h = h + merged @ w_out[l]
        u = rms_norm(h, norm_xattn_g[l])
        mem_n = rms_norm(mem, norm_mem_g[l])
        h = h + memory_cross_attention(u, mem_n, w_xq[l], w_xkv[l], w_xo[l])
        u = rms_norm(h, norm_mlp_g[l])
        h = h + jnp.square(jax.nn.relu(u @ w_mlp1[l])) @ w_mlp2[l]
    return rms_norm(h, final_norm_g)


CHUNK = 128
A_WIDTH = D_MODEL
A_GROUPS = 8
A_GROUP_DIM = A_WIDTH // A_GROUPS
N_HEADS = 16
HEAD_DIM = 64
B_WIDTH = N_HEADS * HEAD_DIM
DILATED_PATTERNS = ((128, 1), (512, 4), (2048, 16))
BLOCK = 128
N_BRANCHES = 2
NEG_INF = -1e30
IN_COLS_2 = 3 * A_WIDTH + 4 * B_WIDTH + N_BRANCHES * D_MODEL


def rmsnorm(x, g):
    xf = x.astype(jnp.float32)
    y = xf * lax.rsqrt(jnp.mean(xf * xf, axis=-1, keepdims=True) + EPS)
    return (y * g.astype(jnp.float32)).astype(x.dtype)

def chunked_spatial_gating(u, v, w_s, b_s, g_v):
    Bn, S, _ = v.shape
    v = rmsnorm(v, g_v)
    vc = v.reshape(Bn, S // CHUNK, CHUNK, A_GROUPS, A_GROUP_DIM)
    causal = jnp.tril(jnp.ones((CHUNK, CHUNK), dtype=bool))
    w = jnp.where(causal[None], w_s, 0).astype(v.dtype)
    mixed = jnp.einsum('gts,bcsgd->bctgd', w, vc) + b_s.T[None, None, :, :, None]
    return u * mixed.reshape(Bn, S, A_WIDTH)

def dilated_pattern(q, k, v, slopes, window, dilation):
    Bn, H, S, Dh = q.shape
    L = S // dilation
    nback = window // dilation
    nb = -(-L // BLOCK)
    pad = nb * BLOCK - L

    def to_blocks(t):
        t = t.reshape(Bn, H, L, dilation, Dh).transpose(0, 1, 3, 2, 4)
        t = jnp.pad(t, ((0, 0), (0, 0), (0, 0), (0, pad), (0, 0)))
        return t.reshape(Bn, H, dilation, nb, BLOCK, Dh)

    qb, kb, vb = to_blocks(q), to_blocks(k), to_blocks(v)

    def with_prev(t):
        prev = jnp.pad(t, ((0, 0), (0, 0), (0, 0), (1, 0), (0, 0), (0, 0)))[:, :, :, :-1]
        return jnp.concatenate([prev, t], axis=4)

    kw, vw = with_prev(kb), with_prev(vb)
    qpos = jnp.arange(BLOCK)[:, None] + BLOCK
    kpos = jnp.arange(2 * BLOCK)[None, :]
    dist = qpos - kpos
    key_idx = (jnp.arange(nb)[:, None, None] - 1) * BLOCK + kpos[None]
    valid = (dist >= 0) & (dist <= nback) & (key_idx >= 0)

    s = jnp.einsum('bhrnqd,bhrnkd->bhrnqk', qb, kw) * (Dh ** -0.5)
    s = s - slopes[None, :, None, None, None, None] * (dist * dilation).astype(jnp.float32)
    s = jnp.where(valid[None, None, None], s, NEG_INF)
    m = jnp.max(s, axis=-1)
    p = jnp.exp(s - m[..., None])
    l = jnp.sum(p, axis=-1)
    o = jnp.einsum('bhrnqk,bhrnkd->bhrnqd', p, vw) / l[..., None]

    def from_blocks(t):
        t = t.reshape(Bn, H, dilation, nb * BLOCK, *t.shape[5:])[:, :, :, :L]
        t = jnp.moveaxis(t, 2, 3)
        return t.reshape(Bn, H, S, *t.shape[4:])

    return from_blocks(o), from_blocks(m), from_blocks(l)

def dilated_attention(q, k, v):
    Bn, S, _ = q.shape
    heads = lambda t: t.astype(jnp.float32).reshape(Bn, S, N_HEADS, HEAD_DIM).transpose(0, 2, 1, 3)
    qh, kh, vh = heads(q), heads(k), heads(v)
    slopes = 2.0 ** (-8.0 * jnp.arange(1, N_HEADS + 1, dtype=jnp.float32) / N_HEADS)
    outs = [dilated_pattern(qh, kh, vh, slopes, w, d) for (w, d) in DILATED_PATTERNS]
    m_all = jnp.max(jnp.stack([m for (_, m, _) in outs]), axis=0)
    alphas = [l * jnp.exp(m - m_all) for (_, m, l) in outs]
    num = sum(a[..., None] * o for a, (o, _, _) in zip(alphas, outs))
    o = num / sum(alphas)[..., None]
    return o.transpose(0, 2, 1, 3).reshape(Bn, S, B_WIDTH).astype(q.dtype)

def second_inputs(seed: int = 0) -> dict:
    key = jax.random.key(seed)
    ks = jax.random.split(key, 10)
    f32 = jnp.float32
    x = jax.random.normal(ks[0], (BATCH, SEQ, D_MODEL), f32)
    g_norm = 1.0 + 0.05 * jax.random.normal(ks[1], (DEPTH, D_MODEL), f32)
    w_in = jax.random.normal(ks[2], (DEPTH, D_MODEL, IN_COLS_2), f32) * D_MODEL ** -0.5
    w_s = jax.random.normal(ks[3], (DEPTH, A_GROUPS, CHUNK, CHUNK), f32) * CHUNK ** -0.5
    b_s = 1.0 + 0.1 * jax.random.normal(ks[4], (DEPTH, A_GROUPS, CHUNK), f32)
    g_v = 1.0 + 0.05 * jax.random.normal(ks[5], (DEPTH, A_WIDTH), f32)
    w_proj_a = jax.random.normal(ks[6], (DEPTH, A_WIDTH, D_MODEL), f32) * A_WIDTH ** -0.5
    w_proj_b = jax.random.normal(ks[7], (DEPTH, B_WIDTH, D_MODEL), f32) * B_WIDTH ** -0.5
    w_out = jax.random.normal(ks[8], (DEPTH, D_MODEL, D_MODEL), f32) * D_MODEL ** -0.5
    g_final = 1.0 + 0.05 * jax.random.normal(ks[9], (D_MODEL,), f32)
    return {"x": x, "g_norm": g_norm, "w_in": w_in, "w_s": w_s, "b_s": b_s, "g_v": g_v,
            "w_proj_a": w_proj_a, "w_proj_b": w_proj_b, "w_out": w_out, "g_final": g_final}

def second_block(x, g_norm, w_in, w_s, b_s, g_v, w_proj_a, w_proj_b, w_out, g_final):
    splits = [A_WIDTH, 2 * A_WIDTH, 3 * A_WIDTH,
              3 * A_WIDTH + B_WIDTH, 3 * A_WIDTH + 2 * B_WIDTH,
              3 * A_WIDTH + 3 * B_WIDTH, 3 * A_WIDTH + 4 * B_WIDTH]
    for layer in range(DEPTH):
        h = rmsnorm(x, g_norm[layer])
        proj = h @ w_in[layer]
        a_u, a_v, a_gate, q, k, v, b_gate, gate_logits = jnp.split(proj, splits, axis=-1)
        y_a = chunked_spatial_gating(jax.nn.gelu(a_u), jax.nn.gelu(a_v),
                                     w_s[layer], b_s[layer], g_v[layer]) * jax.nn.silu(a_gate)
        y_b = dilated_attention(q, k, v) * jax.nn.silu(b_gate)
        g_a, g_b = jnp.split(jax.nn.sigmoid(gate_logits), N_BRANCHES, axis=-1)
        merged = g_a * (y_a @ w_proj_a[layer]) + g_b * (y_b @ w_proj_b[layer])
        x = x + merged @ w_out[layer]
    return rmsnorm(x, g_final)


def setup_inputs(seed=0):
    out = dict(first_inputs(seed))
    for name, value in second_inputs(seed + 1).items():
        if name != "x":
            out[name + "_2"] = value
    return out


def reference(
    x, mem, positions, norm_mix_g, w_in, conv_w, conv_b, conv_ln_g, conv_ln_b, w_conv_out,
    q_norm_g, w_uq, kv_norm_g, w_ukv, w_mla_out, w_out, norm_xattn_g, norm_mem_g, w_xq, w_xkv,
    w_xo, norm_mlp_g, w_mlp1, w_mlp2, final_norm_g, g_norm_2, w_in_2, w_s_2, b_s_2, g_v_2,
    w_proj_a_2, w_proj_b_2, w_out_2, g_final_2,
):
    x = first_block(
        x, mem, positions, norm_mix_g, w_in, conv_w, conv_b, conv_ln_g, conv_ln_b, w_conv_out,
        q_norm_g, w_uq, kv_norm_g, w_ukv, w_mla_out, w_out, norm_xattn_g, norm_mem_g, w_xq,
        w_xkv, w_xo, norm_mlp_g, w_mlp1, w_mlp2, final_norm_g,
    )
    return second_block(
        x, g_norm_2, w_in_2, w_s_2, b_s_2, g_v_2, w_proj_a_2, w_proj_b_2, w_out_2, g_final_2,
    )


_drawn_inputs = setup_inputs


def setup_inputs(seed=0):
    import zlib

    import numpy as np

    out = dict(_drawn_inputs(seed))
    spreads = {}
    factors = {'norm_mix_g': 6.6,
     'conv_b': 3.83,
     'conv_ln_g': 6.507,
     'conv_ln_b': 7.825,
     'q_norm_g': 8.0,
     'kv_norm_g': 8.0,
     'norm_xattn_g': 8.0,
     'norm_mem_g': 8.0,
     'norm_mlp_g': 8.065,
     'final_norm_g': 2.682,
     'b_s_2': 8.232,
     'g_v_2': 25.124}
    for name, (base, spread) in spreads.items():
        noise = np.random.default_rng([zlib.crc32(name.encode()), seed]).standard_normal(out[name].shape)
        drawn = base * np.exp(spread * noise) if base else spread * noise
        out[name] = __import__('jax').numpy.asarray(drawn.astype(out[name].dtype))
    for name, factor in factors.items():
        out[name] = (out[name] * factor).astype(out[name].dtype)
    return out
```

```python
from contextlib import ExitStack

import numpy as np

import concourse.bass as bass
from concourse import mybir

F32 = mybir.dt.float32
F32R = mybir.dt.float32r
I32 = mybir.dt.int32
ALU = mybir.AluOpType
ACT = mybir.ActivationFunctionType
AX_X = mybir.AxisListType.X

P = 128
S = 512
D = 1024
DT = D // P
QT = S // P
MEM = 256
CONV = 512
CT = CONV // P
TAPS = 31
PAD = TAPS - 1
HEADS = 8
NOPE, ROPE, VD = 64, 32, 64
QLORA, KVLORA = 384, 256
XH, XD = 4, 128
FF = 4096
EPS = 1e-6
BIG = 1e30
PAIRS = 8
GELU_A = 0.044715
GELU_C = 0.7978845608028654
LINEAR_Q_SCALE = -float((NOPE + ROPE) ** -0.5)
CROSS_Q_SCALE = -float(XD ** -0.5)
DILATED_Q_SCALE = -0.125

VECS = [("norm_mix_g", 8), ("conv_b", 4), ("conv_ln_g", 4), ("conv_ln_b", 4), ("q_norm_g", 3), ("kv_norm_g", 2),
        ("norm_xattn_g", 8), ("norm_mem_g", 8), ("norm_mlp_g", 8), ("final_norm_g", 8), ("g_norm_2", 8),
        ("g_v_2", 8), ("g_final_2", 8)]
COL, NVEC = {}, 0
for _name, _n in VECS:
    COL[_name] = NVEC
    NVEC += _n

PHASES = [("latent", 6, 6), ("conv", 8, 8), ("heads", 32, 32), ("mla_out", 4, 8), ("conv_out", 4, 8),
          ("w_out", 8, 8), ("xkv", 8, 8), ("xq", 4, 4), ("xo", 4, 8), ("up0", 16, 16), ("down0", 16, 8), ("up1", 16, 16),
          ("down1", 16, 8), ("av", 8, 8), ("pairs", 64, 64), ("proj_a", 8, 8), ("proj_b", 8, 8), ("w_out2", 8, 8)]
CHUNK0, JOB0, NCHUNKS, NJOBS = {}, {}, 0, 0
for _name, _c, _j in PHASES:
    CHUNK0[_name], JOB0[_name] = NCHUNKS, NJOBS
    NCHUNKS += _c
    NJOBS += _j

NORMS = [("mix", 8), ("q", 3), ("kv", 2), ("conv", 4), ("mem", 8), ("xattn", 8), ("mlp", 8), ("final", 8),
         ("second", 8), ("gate_v", 8), ("out", 8)]
NORM_NO = {n: k for k, (n, _) in enumerate(NORMS)}
SQ0, _t = {}, 0
for _name, _n in NORMS:
    SQ0[_name] = _t
    _t += _n
SPLIT_NORMS = [("mix", 8), ("q", 3), ("kv", 2), ("mem", 8), ("xattn", 8), ("mlp", 8), ("second", 8)]
U0, _t = {}, 0
for _name, _n in SPLIT_NORMS:
    U0[_name] = _t
    _t += _n


COUNTS = {n: (c, j) for n, c, j in PHASES}
NCONST = 4 + 16
SEL_MADE = 7
ROUND = 1.5 * 2.0 ** 23
TWO_PI = (6.28125, 0.00193500518798828125, 2 * np.pi - 6.28125 - 0.00193500518798828125)
TWO_PI = tuple(float(v) for v in TWO_PI)


def chunk_size(c):
    k = c - CHUNK0["heads"]
    return 1024 if not 0 <= k < COUNTS["heads"][0] else (3 * P, 2 * P, 1024, 1024)[k % 4]


class Idx:

    def __init__(self, static, per=0, i=None):
        self.static, self.per, self.i = static, per, i

    def __add__(self, k):
        return Idx(self.static + k, self.per, self.i)

    def times(self, m, k=0):
        v = self.static * m + k
        return v if self.i is None else v + (self.per * m) * self.i

    def v(self):
        return self.times(1)

    def half(self):
        assert self.per % 2 == 0
        return self.static // 2 if self.i is None else self.static // 2 + (self.per // 2) * self.i

    def slot(self, m):
        assert self.per % m == 0
        return self.static % m


def build(nc, a, out):
    ctx = ExitStack()
    with ctx:
        def sem(name):
            return ctx.enter_context(nc.semaphore(name))

        def sb(name, shape, dt=F32, stack=ctx):
            return stack.enter_context(nc.sbuf_tensor(name, shape, dt))

        def bank(name):
            return ctx.enter_context(nc.psum_tensor(name, [P, 512], F32))

        lin = [bank("lin0"), bank("lin1")]
        sc = [bank("sc0"), bank("sc1"), bank("sc2")]
        tr = [bank("tr0"), bank("tr1")]
        ob = bank("ob")

        h = sb("h", [P, DT, S])
        uh = sb("uh", [P, DT, S], F32R)
        ul = sb("ul", [P, DT, S], F32R)
        raw = sb("raw", [P, 2, 1024])
        wh = sb("wh", [P, 4, 1024], F32R)
        wl = sb("wl", [P, 4, 1024], F32R)
        ident = sb("ident", [P, P])
        ones = sb("ones", [P, P])
        cols = sb("cols", [P, NVEC])
        taps = sb("taps", [P, CT * TAPS])
        consts = sb("consts", [P, NCONST])
        small = sb("small", [P, 64])
        logit = sb("logit", [P, 1280])
        pt = sb("pt", [P, 896])
        qt = sb("qt", [P, S])
        kt = sb("kt", [P, S])
        vtok = sb("vtok", [P, QT, P])
        ta, tb, tc, td, te = (sb(n, [P, S]) for n in ("ta", "tb", "tc", "td", "te"))
        bias = sb("bias", [P, S])
        wst = sb("wst", [P, P])
        sel = wst
        trig = sb("trig", [P, S])
        dist = trig

        eps, eps4 = small[:, 0:1], small[:, 1:2]
        std, rstd = small[:, 4:8], small[:, 8:12]
        nmax = small[:, 12:16]
        den, rden = small[:, 16:20], small[:, 20:24]
        hb = small[:, 24:28]
        xnmax, xden, xrden = small[:, 32:40], small[:, 40:48], small[:, 48:56]

        st = ExitStack()
        gates = sb("gates", [P, 16, S], stack=st)
        acc = sb("acc", [P, CT, S], stack=st)
        otok = sb("otok", [P, QT, S], stack=st)
        s2 = ExitStack()
        cqh = sb("cqh", [P, 3, S], F32R, s2)
        cql = sb("cql", [P, 3, S], F32R, s2)
        ckh = sb("ckh", [P, 2, S], F32R, s2)
        ckl = sb("ckl", [P, 2, S], F32R, s2)
        z = sb("z", [P, CT, S + PAD], stack=s2)
        s2.close()
        yh = sb("yh", [P, CT, S], F32R, st)
        yl = sb("yl", [P, CT, S], F32R, st)
        oh = sb("oh", [P, 4, S], F32R, st)
        ol = sb("ol", [P, 4, S], F32R, st)
        st.close()
        st = ExitStack()
        xtok = sb("xtok", [P, QT, D], stack=st)
        vrows = sb("vrows", [P, P], stack=st)
        crows = sb("crows", [TAPS, CONV], stack=st)
        st.close()
        st = ExitStack()
        xq = sb("xq", [P, XH, S], stack=st)
        xp = sb("xp", [P, 2, QT, MEM], stack=st)
        xpt = sb("xpt", [P, 2, 2, S], stack=st)
        xoh = sb("xoh", [P, XH, S], F32R, st)
        xol = sb("xol", [P, XH, S], F32R, st)
        memtok = sb("memtok", [P, 2, D], stack=st)
        memt = sb("memt", [P, DT, MEM], stack=st)
        memh = sb("memh", [P, DT, MEM], F32R, st)
        meml = sb("meml", [P, DT, MEM], F32R, st)
        xk = sb("xk", [P, XH, MEM], stack=st)
        xv = sb("xv", [P, 2, XH * XD], stack=st)
        st.close()
        st = ExitStack()
        fh = sb("fh", [P, 16, S], F32R, st)
        fl = sb("fl", [P, 16, S], F32R, st)
        st.close()
        st = ExitStack()
        av = sb("av", [P, PAIRS, S], stack=st)
        gb = sb("gb", [P, PAIRS, S], stack=st)
        ya = sb("ya", [P, PAIRS, S], stack=st)
        ybh = sb("ybh", [P, PAIRS, S], F32R, st)
        ybl = sb("ybl", [P, PAIRS, S], F32R, st)
        otp = sb("otp", [P, QT, P], stack=st)
        rbc = sb("rbc", [P, S], stack=st)
        nlog = sb("nlog", [P, S], stack=st)
        atok = sb("atok", [P, QT, P], stack=st)
        st.close()
        cq = gates[:, 11:16, :]
        ws, bsb = ya[:, PAIRS - 1, 0:P], ya[:, PAIRS - 1, P:2 * P]

        x_landed, mem_landed, vecs_landed, taps_landed, consts_landed, pos_landed = (
            sem(n + "_landed") for n in ("x", "mem", "vecs", "taps", "consts", "pos"))
        raw_landed = [sem("raw0_landed"), sem("raw1_landed")]
        swapped_landed, gating_landed = sem("swapped_landed"), sem("gating_landed")
        hi_made, lo_made = sem("hi_made"), sem("lo_made")
        chunk_entered = sem("chunk_entered")
        lin_ready = sem("lin_ready")
        lin_freed = [sem("lin0_freed"), sem("lin1_freed")]
        pool_made, table_made = sem("pool_made"), sem("table_made")
        start_made = sem("start_made")
        xt_ready, xt_copied = sem("xt_ready"), sem("xt_copied")
        vec_ready, vec_copied = sem("vec_ready"), sem("vec_copied")
        trig_arg, trig_made = sem("trig_arg"), sem("trig_made")
        sq_made, sq_summed = sem("sq_made"), sem("sq_summed")
        std_made, rstd_made, diag_made, bc_ready = (sem(n) for n in ("std_made", "rstd_made", "diag_made", "bc_ready"))
        u_made, u_high, u_low = sem("u_made"), sem("u_high"), sem("u_low")
        kr_ready, kr_placed = sem("kr_ready"), sem("kr_placed")
        z_made, tap_done = sem("z_made"), sem("tap_done")
        vtr_ready, vtok_placed = sem("vtr_ready"), sem("vtok_placed")
        bias_made = sem("bias_made")
        scores_ready, logits_made, probs_made = sem("scores_ready"), sem("logits_made"), sem("probs_made")
        pt_ready, pt_act, pt_dve = sem("pt_ready"), sem("pt_copied_scalar"), sem("pt_copied_vector")
        rden_made, out_ready, out_copied = sem("rden_made"), sem("out_ready"), sem("out_copied")
        ot_ready, o_high, o_low = sem("ot_ready"), sem("o_high"), sem("o_low")
        mean_ready, centred = sem("mean_ready"), sem("centred")
        y_norm, y_half, y_tanh, y_made, y_high, y_low = (
            sem(n) for n in ("y_norm", "y_half", "y_tanh", "y_made", "y_high", "y_low"))
        m_made, m_high, m_low = sem("merged_made"), sem("merged_high"), sem("merged_low")
        mt_ready, mt_copied = sem("mt_ready"), sem("mt_copied")
        xvt_ready, xv_placed = sem("xvt_ready"), sem("xv_placed")
        xs_ready, xmax_made, xp_made, xrden_made, xp_scaled = (
            sem(n) for n in ("xs_ready", "xmax_made", "xp_made", "xrden_made", "xp_scaled"))
        xpt_ready, xpt_act, xpt_dve = sem("xpt_ready"), sem("xpt_copied_scalar"), sem("xpt_copied_vector")
        xo_ready, xo_high, xo_low = sem("xo_ready"), sem("xo_high"), sem("xo_low")
        f_sq, f_high, f_low = sem("f_sq"), sem("f_high"), sem("f_low")
        x1_made = sem("x1_made")
        g_square, g_poly, g_tanh = sem("gelu_square"), sem("gelu_poly"), sem("gelu_tanh")
        rbc_made = sem("rbc_made")
        gv_made, gvt_ready, atok_placed = sem("gv_made"), sem("gvt_ready"), sem("atok_placed")
        ws_masked, wst_ready, wst_placed = sem("ws_masked"), sem("wst_ready"), sem("wst_placed")
        mix_ready, mix_read, ya_made = sem("mix_ready"), sem("mix_read"), sem("ya_made")
        silu_tanh, gate_prod = sem("silu_tanh"), sem("gate_prod")
        ob_ready, yb_made, yb_high, yb_low = (sem(n) for n in ("ob_ready", "yb_made", "yb_high", "yb_low"))
        ya_high, ya_low = sem("ya_high"), sem("ya_low")
        fin_made, fin_ready, fin_copied, stored = (sem(n) for n in ("fin_made", "fin_ready", "fin_copied", "stored"))
        vector_steps, pool_steps = sem("vector_steps"), sem("pool_steps")

        def wait(eng, s, v):
            if not isinstance(v, int) or v > 0:
                eng.wait_ge(s, v)

        def now(eng, v):
            return v if isinstance(v, int) else eng.snap(eng.to_reg(v))

        def phase(name, per_c=0, per_j=0, i=None):
            return Idx(CHUNK0[name], per_c, i), Idx(JOB0[name], per_j, i)

        def col(name, k=0):
            return cols[:, COL[name] + k:COL[name] + k + 1]

        def evacuated(eng, j):
            eng.wait_ge(lin_freed[j.slot(2)], (j + 2).half())

        def chain(eng, s):
            done = [0]

            def step(ins):
                done[0] += 1
                ins.then_inc(s, 1)
                eng.wait_ge(s, done[0])
            return step

        BC_READ = {n: (u_made, U0[n] + k) for n, k in SPLIT_NORMS}
        BC_READ.update(conv=(y_norm, CT), final=(x1_made, DT), gate_v=(rbc_made, 1), out=(fin_made, DT))
        NTOK = {"mem": MEM}
        WIDTH = {"q": QLORA, "kv": KVLORA, "conv": CONV}
        NTILES = dict(NORMS)

        KEYS = [P * (q + 1) for q in range(QT)]
        LOFF = [0, 128, 384, 768]
        SBANK = [(0, 0), (0, 128), (1, 0), (2, 0)]
        PTBANK = [(0, 0), (0, 128), (1, 0), (0, 0)]
        PTOFF = [0, 128, 512, 0]
        SCORES_AT = [1, 1, 2, 3]

        block = ctx.enter_context(nc.Block())

        @block.sync
        def _(sp):
            def view(w):
                return w.rearrange("(k p) m -> p k m", p=P)

            def place(c, k, m):
                at = now(sp, (c + -1).v())
                if not isinstance(at, int):
                    sp.wait_ge(lo_made, 1)
                wait(sp, lo_made, at)
                return raw[:, c.slot(2), 0:k * m].rearrange("p (k m) -> p k m", k=k)

            def load(c, w, first, k, m):
                src = view(w)[:, :, bass.ds(now(sp, first), m)]
                sp.dma_start(place(c, k, m), src).then_inc(raw_landed[c.slot(2)], 16)

            def load_rope(c, w, first, rope, k):
                half = ROPE // 2
                src, second, front = (view(w)[:, :, bass.ds(now(sp, at), n)] for at, n in
                                      ((first, 96), (rope + half, half), (rope, half)))
                dst = place(c, k, P)
                sp.dma_start(dst[:, :, 0:96], src).then_inc(raw_landed[c.slot(2)], 16)
                sp.dma_start(dst[:, :, 96:96 + half], second).then_inc(swapped_landed, 16)
                sp.dma_start(dst[:, :, 96 + half:P], front).then_inc(swapped_landed, 16)

            def stream(name, w, first, k, m):
                with sp.Fori(0, COUNTS[name][0] // 4) as i:
                    c, _ = phase(name, 4, 0, i)
                    for n in range(4):
                        load(c + n, w, first + m * n + (m * 4) * i, k, m)

            w_in, w_in2 = a["w_in"][0], a["w_in_2"][0]
            c, _ = phase("latent")
            for m in range(5):
                load(c + m, w_in, 2 * CONV + P * m, DT, P)
            rope0 = 2 * CONV + QLORA + KVLORA
            load_rope(c + 5, w_in, rope0 - NOPE, rope0, DT)
            with sp.Fori(0, 2) as i:
                c, _ = phase("conv", 4, 0, i)
                for m in range(4):
                    load(c + m, w_in, (m % 2) * CONV + (m // 2) * P + (2 * P) * i, DT, P)
            with sp.Fori(0, HEADS) as i:
                c, _ = phase("heads", 4, 0, i)
                load_rope(c, a["w_uq"][0], 96 * i, 96 * i + NOPE, 3)
                load(c + 1, a["w_ukv"][0], P * i, 2, P)
                for m in range(2):
                    load(c + 2 + m, w_in, rope0 + ROPE + P * m + (2 * P) * i, DT, P)
            stream("mla_out", a["w_mla_out"][0], 0, 4, 256)
            stream("conv_out", a["w_conv_out"][0], 0, 4, 256)
            c, _ = phase("w_out")
            for m in range(DT):
                if m == 2:
                    sp.wait_ge(m_made, DT)
                    sp.dma_start(memtok[:], a["mem"][0].rearrange("(q p) n -> p q n", p=P)).then_inc(mem_landed, 16)
                load(c + m, a["w_out"][0], P * m, DT, P)
            stream("xkv", a["w_xkv"][0], 0, DT, P)
            stream("xq", a["w_xq"][0], 0, DT, P)
            stream("xo", a["w_xo"][0], 0, 4, 256)
            for half in range(2):
                stream(f"up{half}", a["w_mlp1"][0], half * FF // 2, DT, P)
                with sp.Fori(0, 4) as i:
                    c, _ = phase(f"down{half}", 4, 0, i)
                    for m in range(4):
                        first = half * FF // 2 + (m % 2) * D
                        load(c + m, a["w_mlp2"][0][first:first + D, :], (m // 2) * P + (2 * P) * i, DT, P)
            stream("av", w_in2, D, DT, P)
            with sp.Fori(0, PAIRS) as i:
                c, _ = phase("pairs", 8, 0, i)
                for m, first in enumerate((3, 4, 5, 0, 2, 6, 7, 8)):
                    load(c + m, w_in2, first * D + P * i, DT, P)
                    if m == 3:
                        weights, biases = a["w_s_2"][0][i], a["b_s_2"][0][i].partition_broadcast(P)
                        sp.wait_ge(mix_read, i)
                        sp.dma_start(ws, weights).then_inc(gating_landed, 16)
                        sp.dma_start(bsb, biases).then_inc(gating_landed, 16)
            stream("proj_a", a["w_proj_a_2"][0], 0, DT, P)
            stream("proj_b", a["w_proj_b_2"][0], 0, DT, P)
            stream("w_out2", a["w_out_2"][0], 0, DT, P)
            for f in range(DT):
                sp.wait_ge(fin_copied, f + 1)
                sp.dma_start(out[0].rearrange("(q p) n -> p q n", p=P)[:, :, f * P:(f + 1) * P],
                             ya[:, f, :].rearrange("p (q n) -> p q n", q=QT)).then_inc(stored, 16)
            sp.wait_ge(stored, 16 * DT)

        @block.gpsimd
        def _(pool):
            step = chain(pool, pool_steps)
            step(pool.memset(ident[:], 0.0))
            pool.affine_select(out=ident[:], in_=ident[:], compare_op=ALU.not_equal, fill=1.0, base=0,
                               pattern=[[-1, P]], channel_multiplier=1).then_inc(pool_made, 1)
            step(pool.memset(bias[:], 0.0))
            pool.affine_select(out=bias[:], in_=bias[:], compare_op=ALU.is_ge, fill=BIG, base=S - P,
                               pattern=[[-1, S]], channel_multiplier=1).then_inc(pool_made, 1)
            pool.wait_ge(xo_low, XH)
            dint = atok[:].rearrange("p a b -> p (a b)").bitcast(I32)
            step(pool.iota(dint, [[-1, S]], base=S - P, channel_multiplier=1))
            pool.tensor_copy(dist[:], dint).then_inc(pool_made, 1)
            pool.wait_ge(table_made, 1)
            pool.affine_select(out=nlog[:], in_=nlog[:], compare_op=ALU.is_ge, fill=BIG, base=S - P,
                               pattern=[[-1, S]], channel_multiplier=1).then_inc(pool_made, 1)
            with pool.Fori(0, PAIRS) as i:
                at = now(pool, 32 * i + 32)
                pool.wait_ge(table_made, 1)
                pool.wait_ge(gating_landed, at)
                pool.affine_select(out=ws, in_=ws, compare_op=ALU.is_ge, fill=0.0, base=0, pattern=[[-1, P]],
                                   channel_multiplier=1).then_inc(ws_masked, 1)

        @block.tensor
        def _(pe):
            def products(o, slot, k, m, xh_, xl_, start, stop, w, enter):
                at = slice(k * w + m * P, k * w + (m + 1) * P)
                ins = pe.matmul(o, wh[:, slot, at], xh_, start=start, stop=False)
                if enter:
                    ins.then_inc(chunk_entered, 1)
                pe.matmul(o, wh[:, slot, at], xl_, start=False, stop=False)
                return pe.matmul(o, wl[:, slot, at], xh_, start=False, stop=stop)

            def open_job(j):
                wait(pe, lin_freed[j.slot(2)], j.half())
                return lin[j.slot(2)]

            def job(c, j, rows, xh_, xl_, n=S, before=None):
                o = open_job(j)[:, 0:n]
                wait(pe, lo_made, (c + 1).v())
                for k in range(rows):
                    if before is not None:
                        before(k)
                    ins = products(o, c.slot(4), k, 0, xh_[:, k, :], xl_[:, k, :], k == 0, k == rows - 1, P, k == 0)
                ins.then_inc(lin_ready, 1)

            def two_jobs(c, j, xh_, xl_, before=None):
                wait(pe, lo_made, (c + 1).v())
                for m in range(2):
                    o = open_job(j + m)[:]
                    for k in range(4):
                        if before is not None and m == 0:
                            before(k)
                        ins = products(o, c.slot(4), k, m, xh_[:, k, :], xl_[:, k, :], k == 0, k == 3, 256,
                                       m == 0 and k == 0)
                    ins.then_inc(lin_ready, 1)

            def tiles_of(sem_, base):
                return lambda k: pe.wait_ge(sem_, base + k + 1)

            def turn_tile(dst, src, n=QT, idt=ident):
                for q in range(n):
                    ins = pe.transpose(dst[:, q * P:(q + 1) * P], src(q), idt[:])
                return ins

            def sum_squares(name, f):
                s, n = SQ0[name] + f, NTILES[name]
                if f == 0:
                    wait(pe, std_made, NORM_NO[name])
                pe.wait_ge(sq_made, s + 1)
                for q in range(NTOK.get(name, S) // P):
                    ins = pe.matmul(tr[1][:, q:q + 1], (ta, tb)[s % 2][:, q * P:(q + 1) * P], ones[:, 0:1],
                                    start=(f == 0 and q == 0), stop=(f == n - 1), skip_group_check=True)
                ins.then_inc(sq_summed, 1)

            def sums(name):
                for f in range(NTILES[name]):
                    sum_squares(name, f)

            def broadcast(name):
                k = NORM_NO[name]
                if k:
                    pe.wait_ge(*BC_READ[NORMS[k - 1][0]])
                pe.wait_ge(diag_made, k + 1)
                n = NTOK.get(name, S)
                pe.matmul(tr[0][:, 0:n], ones[:], te[:, 0:n], start=True, stop=True).then_inc(bc_ready, 1)

            def scores(n, rows):
                wait(pe, logits_made, n.times(4))
                for q in range(QT):
                    b, o = SBANK[q]
                    ins = pe.matmul(sc[b][:, o:o + KEYS[q]], qt[rows, q * P:(q + 1) * P], kt[rows, 0:KEYS[q]],
                                    start=True, stop=True)
                    if q:
                        ins.then_inc(scores_ready, 1)

            def turn(q):
                b, o = PTBANK[q]
                for kb in range(q + 1):
                    ins = pe.transpose(tr[b][:, o + kb * P:o + (kb + 1) * P],
                                       logit[:, LOFF[q] + kb * P:LOFF[q] + (kb + 1) * P], ident[:])
                return ins

            def weigh(q, v):
                for kb in range(q + 1):
                    ins = pe.matmul(ob[:, q * VD:(q + 1) * VD], pt[:, PTOFF[q] + kb * P:PTOFF[q] + (kb + 1) * P],
                                    v(kb), start=kb == 0, stop=kb == q)
                return ins

            def finish(n, v):
                wait(pe, probs_made, n.times(4, 2))
                wait(pe, pt_act, n.times(2))
                turn(0)
                turn(1).then_inc(pt_ready, 1)
                wait(pe, probs_made, n.times(4, 3))
                wait(pe, pt_dve, n.v())
                turn(2).then_inc(pt_ready, 1)
                wait(pe, pt_act, n.times(2, 1))
                wait(pe, out_copied, n.v())
                weigh(0, v)
                weigh(1, v)
                wait(pe, probs_made, n.times(4, 4))
                turn(3).then_inc(pt_ready, 1)
                wait(pe, pt_dve, n.times(1, 1))
                weigh(2, v)
                wait(pe, pt_act, n.times(2, 2))
                weigh(3, v).then_inc(out_ready, 1)

            pe.wait_ge(pool_made, 1)
            pe.wait_ge(vecs_landed, 16 * len(VECS))
            pe.transpose(tr[0][:, 0:NVEC], vrows[0:NVEC, :], ident[0:NVEC, 0:NVEC]).then_inc(vec_ready, 1)
            pe.wait_ge(taps_landed, 16)
            for t in range(CT):
                ins = pe.transpose(tr[1][:, t * 32:t * 32 + TAPS], crows[:, t * P:(t + 1) * P],
                                   ident[0:TAPS, 0:TAPS])
            ins.then_inc(vec_ready, 1)
            pe.wait_ge(start_made, 1)
            pe.wait_ge(vec_copied, 2)
            pe.wait_ge(x_landed, 16)
            for f in range(DT + 1):
                if f < DT:
                    if f >= 3:
                        pe.wait_ge(xt_copied, f - 2)
                    turn_tile(sc[f % 3], lambda q: xtok[:, q, f * P:(f + 1) * P]).then_inc(xt_ready, 1)
                if f:
                    sum_squares("mix", f - 1)
            broadcast("mix")

            c, j = phase("latent")
            for m in range(6):
                job(c + m, j + m, DT, uh, ul, before=tiles_of(u_low, U0["mix"]) if m == 0 else None)
                if m == 3:
                    sums("q")
                if m == 4:
                    broadcast("q")
            sums("kv")

            c, j = phase("conv")
            for m in range(8):
                job(c + m, j + m, DT, uh, ul)
                if m == 0:
                    evacuated(pe, Idx(JOB0["latent"] + 5))
                    pe.wait_ge(start_made, SEL_MADE)
                    pe.matmul(sc[0][:], sel[64:128, :], logit[64:128, 0:S], start=True, stop=True).then_inc(kr_ready, 1)
                if m == 1:
                    broadcast("kv")

            pe.wait_ge(u_low, U0["kv"] + 2)
            pe.wait_ge(kr_placed, 1)
            with pe.Fori(0, HEADS) as i:
                c, j = phase("heads", 4, 4, i)
                n = Idx(0, 1, i)
                job(c, j, 3, cqh, cql)
                job(c + 1, j + 1, 2, ckh, ckl)
                job(c + 2, j + 2, DT, uh, ul)
                pe.wait_ge(pool_made, 1)
                wait(pe, out_copied, n.v())
                evacuated(pe, j + 1)
                for kb in range(QT):
                    ins = pe.transpose(ob[:, 256 + kb * VD:256 + (kb + 1) * VD], td[64:128, kb * P:(kb + 1) * P],
                                       ident[64:128, 64:128])
                ins.then_inc(vtr_ready, 1)
                evacuated(pe, j)
                scores(n, slice(0, P))
                job(c + 3, j + 3, DT, uh, ul)
                pe.wait_ge(vtok_placed, n.times(1, 1))
                finish(n, lambda kb: vtok[:, kb, 0:VD])

            pe.wait_ge(tap_done, CT * TAPS)
            for t in range(CT):
                ins = pe.matmul(sc[0][:], ones[:], acc[:, t, :], start=t == 0, stop=t == CT - 1)
            ins.then_inc(mean_ready, 1)
            pe.wait_ge(out_copied, HEADS)
            for f in range(4):
                if f >= 2:
                    pe.wait_ge(o_low, f - 1)
                turn_tile(sc[1 + f % 2], lambda q: otok[:, q, f * P:(f + 1) * P]).then_inc(ot_ready, 1)
            c, j = phase("mla_out")
            for m in range(4):
                two_jobs(c + m, j + 2 * m, oh, ol, tiles_of(o_low, 0) if m == 0 else None)
                if m == 0:
                    sums("conv")
                if m == 1:
                    broadcast("conv")
            c, j = phase("conv_out")
            for m in range(4):
                two_jobs(c + m, j + 2 * m, yh, yl, tiles_of(y_low, 0) if m == 0 else None)

            c, j = phase("w_out")
            for m in range(DT):
                job(c + m, j + m, DT, uh, ul, before=tiles_of(m_low, 0) if m == 0 else None)
                if m == 0:
                    pe.wait_ge(mem_landed, 16)
                if m >= 3:
                    pe.wait_ge(mt_copied, m - 2)
                turn_tile(sc[m % 3], lambda q: memtok[:, q, m * P:(m + 1) * P], 2).then_inc(mt_ready, 1)
                if m:
                    sum_squares("mem", m - 1)
            sum_squares("mem", DT - 1)
            broadcast("mem")

            def turn_values(hd):
                evacuated(pe, Idx(JOB0["xkv"] + XH + hd))
                wait(pe, xv_placed, hd)
                turn_tile(ob, lambda q: (qt, kt)[hd % 2][:, q * P:(q + 1) * P], 2).then_inc(xvt_ready, 1)

            c, j = phase("xkv")
            for m in range(8):
                job(c + m, j + m, DT, memh, meml, MEM, tiles_of(u_low, U0["mem"]) if m == 0 else None)
                if m == 1:
                    sums("xattn")
                if m == 3:
                    broadcast("xattn")
                if m >= 5:
                    turn_values(m - 5)
            turn_values(3)
            c, j = phase("xq")
            for m in range(XH):
                job(c + m, j + m, DT, uh, ul, before=tiles_of(u_low, U0["xattn"]) if m == 0 else None)

            def x_scores(hd):
                evacuated(pe, Idx(JOB0["xq"] + hd))
                if hd >= 2:
                    pe.wait_ge(xo_low, hd - 1)
                for q in range(QT):
                    b = ((sc[0], sc[1]), (sc[2], ob))[hd % 2][q // 2]
                    ins = pe.matmul(b[:, (q % 2) * MEM:(q % 2 + 1) * MEM], xq[:, hd, q * P:(q + 1) * P], xk[:, hd, :],
                                    start=True, stop=True)
                    if q % 2:
                        ins.then_inc(xs_ready, 1)

            def x_finish(hd):
                for b in range(2):
                    pe.wait_ge(xp_scaled, 2 * hd + b + 1)
                    wait(pe, (xpt_act, xpt_dve)[b], hd)
                    for q in range(2):
                        for kb in range(2):
                            ins = pe.transpose(tr[b][:, kb * 256 + q * P:kb * 256 + (q + 1) * P],
                                               xp[:, hd % 2, 2 * b + q, kb * P:(kb + 1) * P], ident[:])
                    ins.then_inc(xpt_ready, 1)
                pe.wait_ge(xpt_act, hd + 1)
                pe.wait_ge(xpt_dve, hd + 1)
                for kb in range(2):
                    ins = pe.matmul(sc[2 * (hd % 2)][:], xv[:, kb, hd * XD:(hd + 1) * XD], xpt[:, hd % 2, kb, :],
                                    start=kb == 0, stop=kb == 1)
                ins.then_inc(xo_ready, 1)

            pe.wait_ge(xv_placed, XH)
            x_scores(0)
            for hd in range(XH):
                if hd + 1 < XH:
                    x_scores(hd + 1)
                x_finish(hd)
            c, j = phase("xo")
            for m in range(4):
                two_jobs(c + m, j + 2 * m, xoh, xol, tiles_of(xo_low, 0) if m == 0 else None)
                if m:
                    sum_squares("mlp", 2 * m - 2)
                    sum_squares("mlp", 2 * m - 1)
            sum_squares("mlp", 6)
            sum_squares("mlp", 7)
            broadcast("mlp")

            pe.wait_ge(u_low, U0["mlp"] + DT)
            for half in range(2):
                with pe.Fori(0, 4) as i:
                    c, j = phase(f"up{half}", 4, 4, i)
                    for m in range(4):
                        job(c + m, j + m, DT, uh, ul)
                pe.wait_ge(f_low, 16 * half + 16)
                with pe.Fori(0, 4) as i:
                    c, j = phase(f"down{half}", 4, 2, i)
                    for m in range(2):
                        o = open_job(j + m)[:]
                        for b in range(2):
                            cc = c + (2 * m + b)
                            wait(pe, lo_made, (cc + 1).v())
                            for k in range(DT):
                                ins = products(o, cc.slot(4), k, 0, fh[:, DT * b + k, :], fl[:, DT * b + k, :],
                                               b == 0 and k == 0, b == 1 and k == DT - 1, P, k == 0)
                        ins.then_inc(lin_ready, 1)
            sums("final")
            broadcast("final")
            sums("second")
            broadcast("second")

            pe.wait_ge(u_low, U0["second"] + DT)
            with pe.Fori(0, 2) as i:
                c, j = phase("av", 4, 4, i)
                for m in range(4):
                    job(c + m, j + m, DT, uh, ul)
            sums("gate_v")
            broadcast("gate_v")
            pe.wait_ge(rbc_made, 1)

            with pe.Fori(0, PAIRS) as i:
                c, j = phase("pairs", 8, 8, i)
                g, n0, n1 = Idx(0, 1, i), Idx(HEADS, 2, i), Idx(HEADS + 1, 2, i)
                for m in range(4):
                    job(c + m, j + m, DT, uh, ul)
                evacuated(pe, j + 2)
                turn_tile(tr[0], lambda q: td[:, q * P:(q + 1) * P]).then_inc(vtr_ready, 1)
                evacuated(pe, j)
                evacuated(pe, j + 1)
                scores(n0, slice(0, 64))
                job(c + 4, j + 4, DT, uh, ul)
                pe.wait_ge(vtok_placed, g.times(1, HEADS + 1))
                finish(n0, lambda kb: vtok[:, kb, 0:64])
                scores(n1, slice(64, P))
                pe.wait_ge(gv_made, g.times(1, 1))
                turn_tile(tr[1], lambda q: tc[:, q * P:(q + 1) * P]).then_inc(gvt_ready, 1)
                job(c + 5, j + 5, DT, uh, ul)
                pe.wait_ge(atok_placed, g.times(1, 1))
                finish(n1, lambda kb: vtok[:, kb, 64:P])
                pe.wait_ge(ws_masked, g.times(1, 1))
                job(c + 6, j + 6, DT, uh, ul)
                pe.wait_ge(out_copied, n1.times(1, 1))
                pe.transpose(ob[:, 0:P], ws, ident[:]).then_inc(wst_ready, 1)
                turn_tile(tr[0], lambda q: otp[:, q, :]).then_inc(ob_ready, 1)
                pe.wait_ge(wst_placed, g.times(1, 1))
                for q in range(QT):
                    ins = pe.matmul(tr[1][:, q * P:(q + 1) * P], atok[:, q, :], wst[:], start=True, stop=True)
                ins.then_inc(mix_ready, 1)
                job(c + 7, j + 7, DT, uh, ul)
                pe.wait_ge(mix_read, g.times(1, 1))
                pe.wait_ge(yb_made, g.times(1, 1))

            for name, hi, lo, ready, base in (("proj_a", uh, ul, ya_low, 0), ("proj_b", ybh, ybl, yb_low, 0),
                                              ("w_out2", uh, ul, m_low, DT)):
                c, j = phase(name)
                for m in range(DT):
                    job(c + m, j + m, DT, hi, lo, before=tiles_of(ready, base) if m == 0 else None)
                    if name == "w_out2" and m:
                        sum_squares("out", m - 1)
            sum_squares("out", DT - 1)
            broadcast("out")
            for f in range(DT):
                pe.wait_ge(fin_made, f + 1)
                if f >= 3:
                    pe.wait_ge(fin_copied, f - 2)
                turn_tile(sc[f % 3], lambda q: (tc, td)[f % 2][:, q * P:(q + 1) * P]).then_inc(fin_ready, 1)

        @block.scalar
        def _(act):
            act.dma_start(xtok[:], a["x"][0].rearrange("(q p) n -> p q n", p=P)).then_inc(x_landed, 16)
            for name, n in VECS:
                v = a[name] if len(a[name].shape) == 1 else a[name][0]
                act.dma_start(vrows[COL[name]:COL[name] + n, :], v.rearrange("(n p) -> n p", p=P))\
                    .then_inc(vecs_landed, 16)
            act.dma_start(crows[:], a["conv_w"][0]).then_inc(taps_landed, 16)
            act.dma_start(consts[:], a["shape_consts"]).then_inc(consts_landed, 16)
            act.dma_start(qt[64:128, :].bitcast(I32), a["positions"][0].partition_broadcast(64)).then_inc(pos_landed, 16)

            def split(c):
                if c.i is None and c.static >= NCHUNKS:
                    return
                size = chunk_size(c.static)
                v = 16 * (c.static // 2 + 1)
                act.wait_ge(raw_landed[c.slot(2)], v if c.i is None else v + (8 * c.per) * c.i)
                if size == 3 * P or c.static == CHUNK0["latent"] + 5:
                    v = 32 if size != 3 * P else 64 + 8 * (c.static - CHUNK0["heads"])
                    act.wait_ge(swapped_landed, v if c.i is None else v + (8 * c.per) * c.i)
                wait(act, chunk_entered, (c + -2).v())
                act.activation(wh[:, c.slot(4), 0:size], raw[:, c.slot(2), 0:size], ACT.Copy).then_inc(hi_made, 1)

            def read(j):
                act.wait_ge(lin_ready, (j + 1).v())
                return lin[j.slot(2)]

            def to(j, dst, func, rows=slice(0, P), n=S, **kw):
                act.activation(dst, read(j)[rows, 0:n], func, **kw).then_inc(lin_freed[j.slot(2)], 1)

            def square(name, f, src):
                s, n = SQ0[name] + f, NTOK.get(name, S)
                wait(act, sq_summed, s - 1)
                act.activation((ta, tb)[s % 2][:, 0:n], src[:, 0:n], ACT.Square).then_inc(sq_made, 1)

            def norm_std(name, eps_=eps):
                act.wait_ge(sq_summed, SQ0[name] + NTILES[name])
                wait(act, rstd_made, NORM_NO[name])
                n = NTOK.get(name, S) // P
                act.activation(std[:, 0:n], tr[1][:, 0:n], ACT.Sqrt, bias=eps_, scale=1.0 / WIDTH.get(name, D))\
                    .then_inc(std_made, 1)

            def norm_high(name, dst):
                for f in range(NTILES[name]):
                    u, n = U0[name] + f, NTOK.get(name, S)
                    act.wait_ge(u_made, u + 1)
                    act.activation(dst[:, f, :], (tc, td)[u % 2][:, 0:n], ACT.Copy).then_inc(u_high, 1)

            def exps(n):
                for q in range(QT):
                    wait(act, logits_made, n.times(4, q + 1))
                    p = logit[:, LOFF[q]:LOFF[q] + KEYS[q]]
                    act.activation(p, p, ACT.Exp, bias=nmax[:, q:q + 1], scale=-1.0, accum_out=den[:, q:q + 1])\
                        .then_inc(probs_made, 1)

            def copy_turned(n, k):
                w = (384, 512)[k]
                wait(act, pt_ready, n.times(3, 1 + 2 * k))
                act.activation(pt[:, 0:w], tr[0][:, 0:w], ACT.Copy).then_inc(pt_act, 1)

            split(Idx(0))
            split(Idx(1))
            act.wait_ge(start_made, 2)
            for f in range(DT):
                act.wait_ge(xt_copied, f + 1)
                square("mix", f, h[:, f, :])
            norm_std("mix")
            norm_high("mix", uh)
            act.wait_ge(trig_arg, 1)
            act.activation(trig[64:128, :], kt[64:128, :], ACT.Sin).then_inc(trig_made, 1)

            c, j = phase("latent")
            for m in range(6):
                split(c + (m + 2))
                if m < 5:
                    name, f = ("q", m) if m < 3 else ("kv", m - 3)
                    square(name, f, read(j + m))
                    to(j + m, cq[:, m, :], ACT.Copy)
                if m == 3:
                    norm_std("q")
            norm_high("q", cqh)
            norm_std("kv")

            c, j = phase("conv")
            for m in range(8):
                split(c + (m + 2))
                if m % 2 == 0:
                    to(j + m, z[:, m // 2, PAD:PAD + S], ACT.Copy, scale=0.5)
                else:
                    wait(act, z_made, m // 2 - 1)
                    to(j + m, (logit[:, 512:1024], pt[:, 0:512])[(m // 2) % 2], ACT.Tanh, scale=0.5)
                if m == 2:
                    norm_high("kv", ckh)

            def head(c, j, n, g):
                split(c + 2)
                act.activation(kt[0:64, :], read(j + 1)[0:64, :], ACT.Copy)
                to(j + 1, td[64:128, :], ACT.Copy, rows=slice(64, 128))
                split(c + 3)
                to(j + 2, gates[:, g, :], ACT.Tanh, scale=0.5)
                exps(n)
                split(c + 4)
                split(c + 5)
                to(j + 3, gates[:, g + 1, :], ACT.Tanh, scale=0.5)
                copy_turned(n, 0)
                copy_turned(n, 1)

            act.wait_ge(z_made, CT)
            with act.Fori(0, HEADS - 1) as i:
                head(*phase("heads", 4, 4, i), Idx(0, 1, i), 2 * i)
            c, j = phase("heads")
            head(c + 4 * (HEADS - 1), j + 4 * (HEADS - 1), Idx(HEADS - 1), 2 * (HEADS - 1))

            for t in range(CT):
                act.wait_ge(ot_ready, t + 1)
                act.activation(oh[:, t, :], sc[1 + t % 2][:], ACT.Copy).then_inc(o_high, 1)
            c, _ = phase("mla_out")
            split(c + 2)
            for t in range(CT):
                act.wait_ge(centred, t + 1)
                square("conv", t, acc[:, t, :])
            split(c + 3)
            norm_std("conv")
            split(c + 4)
            for t in range(CT + 1):
                if t < CT:
                    act.wait_ge(y_norm, t + 1)
                    act.activation((qt, kt)[t % 2][:], (tc, td)[t % 2][:], ACT.Identity, bias=hb[:, t:t + 1], scale=0.5)\
                        .then_inc(y_half, 1)
                    act.wait_ge(y_half, t + 1)
                    act.activation((ta, tb)[t % 2][:], (qt, kt)[t % 2][:], ACT.Tanh).then_inc(y_tanh, 1)
                if t:
                    act.wait_ge(y_made, t)
                    act.activation(yh[:, t - 1, :], (tc, td)[(t - 1) % 2][:], ACT.Copy).then_inc(y_high, 1)
            split(c + 5)
            c, _ = phase("conv_out")
            for m in range(4):
                split(c + (m + 2))
                for f in (2 * m, 2 * m + 1):
                    act.wait_ge(m_made, f + 1)
                    act.activation(uh[:, f, :], (tc, td)[f % 2][:], ACT.Copy).then_inc(m_high, 1)

            c, j = phase("w_out")
            for m in range(DT):
                split(c + (m + 2))
                act.wait_ge(mt_copied, m + 1)
                square("mem", m, memt[:, m, :])
            norm_std("mem")
            norm_high("mem", memh)
            for m in range(DT):
                evacuated(act, j + m)
                square("xattn", m, h[:, m, :])
            c, j = phase("xkv")
            for m in range(8):
                split(c + (m + 2))
                if m == 4:
                    norm_high("xattn", uh)
                if m < 4:
                    to(j + m, xk[:, m, :], ACT.Copy, n=MEM)
                else:
                    wait(act, xvt_ready, m - 5)
                    to(j + m, (qt, kt)[m % 2][:, 0:MEM], ACT.Copy, n=MEM)
                if m == 1:
                    norm_std("xattn")
            c, j = phase("xq")
            for m in range(XH):
                split(c + (m + 2))
                to(j + m, xq[:, m, :], ACT.Copy, scale=CROSS_Q_SCALE)

            def x_exps(hd):
                for q in range(QT):
                    act.wait_ge(xmax_made, 2 * hd + q // 2 + 1)
                    b = ((sc[0], sc[1]), (sc[2], ob))[hd % 2][q // 2]
                    k = 4 * (hd % 2) + q
                    act.activation(xp[:, hd % 2, q, :], b[:, (q % 2) * MEM:(q % 2 + 1) * MEM], ACT.Exp,
                                   bias=xnmax[:, k:k + 1], scale=-1.0, accum_out=xden[:, k:k + 1]).then_inc(xp_made, 1)

            x_exps(0)
            for hd in range(XH):
                if hd + 1 < XH:
                    x_exps(hd + 1)
                act.wait_ge(xpt_ready, 2 * hd + 1)
                act.activation(xpt[:, hd % 2, :, 0:256], tr[0][:].rearrange("p (k q) -> p k q", k=2), ACT.Copy)\
                    .then_inc(xpt_act, 1)
                act.wait_ge(xo_ready, hd + 1)
                act.activation(xoh[:, hd, :], sc[2 * (hd % 2)][:], ACT.Copy).then_inc(xo_high, 1)
            c, j = phase("xo")
            for m in range(4):
                split(c + (m + 2))
                for f in (2 * m, 2 * m + 1):
                    evacuated(act, j + f)
                    square("mlp", f, h[:, f, :])
            norm_std("mlp")
            norm_high("mlp", uh)

            for half in range(2):
                with act.Fori(0, 4) as i:
                    c, j = phase(f"up{half}", 4, 4, i)
                    f = Idx(16 * half, 4, i)
                    for m in range(4):
                        split(c + (m + 2))
                        to(j + m, (ta, tb)[m % 2][:], ACT.Relu)
                        act.wait_ge(f_sq, f.times(1, m + 1))
                        act.activation(fh[:, 4 * i + m, :], (tc, td)[m % 2][:], ACT.Copy).then_inc(f_high, 1)
                with act.Fori(0, 4) as i:
                    c, _ = phase(f"down{half}", 4, 2, i)
                    for m in range(4):
                        split(c + (m + 2))
            j = Idx(JOB0["down1"])
            for m in range(DT):
                evacuated(act, j + m)
                square("final", m, h[:, m, :])
            norm_std("final")
            for m in range(DT):
                act.wait_ge(x1_made, m + 1)
                square("second", m, h[:, m, :])
            norm_std("second")
            norm_high("second", uh)

            def gelu(j, k):
                act.activation(ta[:], read(j)[:], ACT.Square).then_inc(g_square, 1)
                act.wait_ge(g_poly, k)
                act.activation(ta[:], tb[:], ACT.Tanh, scale=GELU_C * GELU_A).then_inc(g_tanh, 1)

            with act.Fori(0, 2) as i:
                c, j = phase("av", 4, 4, i)
                for m in range(4):
                    split(c + (m + 2))
                    evacuated(act, j + (m - 1))
                    gelu(j + m, 4 * i + m + 1)
            evacuated(act, Idx(JOB0["av"] + 7))
            for g in range(PAIRS):
                square("gate_v", g, av[:, g, :])
            norm_std("gate_v", eps4)

            with act.Fori(0, PAIRS) as i:
                c, j = phase("pairs", 8, 8, i)
                g, n0, n1 = Idx(0, 1, i), Idx(HEADS, 2, i), Idx(HEADS + 1, 2, i)
                split(c + 2)
                to(j, qt[:], ACT.Copy, scale=DILATED_Q_SCALE)
                split(c + 3)
                split(c + 4)
                to(j + 2, td[:], ACT.Copy)
                split(c + 5)
                act.wait_ge(ya_made, g.v())
                gelu(j + 3, g.times(1, PAIRS + 1))
                exps(n0)
                split(c + 6)
                evacuated(act, j + 3)
                act.activation(ta[:], read(j + 4)[:], ACT.Tanh, scale=0.5).then_inc(silu_tanh, 1)
                copy_turned(n0, 0)
                copy_turned(n0, 1)
                exps(n1)
                split(c + 7)
                evacuated(act, j + 4)
                act.activation(ta[:], read(j + 5)[:], ACT.Tanh, scale=0.5).then_inc(silu_tanh, 1)
                copy_turned(n1, 0)
                copy_turned(n1, 1)
                split(c + 8)
                act.wait_ge(gv_made, g.times(1, 1))
                to(j + 6, av[:, g.v(), :], ACT.Tanh, scale=0.5)
                act.wait_ge(wst_ready, g.times(1, 1))
                act.activation(wst[:], ob[:, 0:P], ACT.Copy).then_inc(wst_placed, 1)
                act.wait_ge(yb_made, g.times(1, 1))
                act.activation(ybh[:, g.v(), :], tc[:], ACT.Copy).then_inc(yb_high, 1)
                split(c + 9)
                to(j + 7, gb[:, g.v(), :], ACT.Tanh, scale=0.5)

            act.wait_ge(ya_made, PAIRS)
            act.wait_ge(lin_ready, JOB0["proj_a"])
            for f in range(DT):
                act.activation(uh[:, f, :], ya[:, f, :], ACT.Copy).then_inc(ya_high, 1)
            c, _ = phase("proj_a")
            for m in range(DT):
                split(c + (m + 2))
            c, _ = phase("proj_b")
            for m in range(DT):
                split(c + (m + 2))
                act.wait_ge(m_made, DT + m + 1)
                act.activation(uh[:, m, :], (tc, td)[m % 2][:], ACT.Copy).then_inc(m_high, 1)
            c, j = phase("w_out2")
            for m in range(DT):
                split(c + (m + 2))
                evacuated(act, j + m)
                square("out", m, h[:, m, :])
            norm_std("out")
            for f in range(DT):
                act.wait_ge(fin_ready, f + 1)
                act.activation(ya[:, f, :], sc[f % 3][:], ACT.Copy).then_inc(fin_copied, 1)

        @block.vector
        def _(dve):
            step = chain(dve, vector_steps)

            def lower(c):
                if c.i is None and c.static >= NCHUNKS:
                    return
                size = chunk_size(c.static)
                dve.wait_ge(hi_made, (c + 1).v())
                dve.tensor_tensor(wl[:, c.slot(4), 0:size], raw[:, c.slot(2), 0:size],
                                  wh[:, c.slot(4), 0:size].bitcast(F32), ALU.subtract).then_inc(lo_made, 1)

            def read(j):
                dve.wait_ge(lin_ready, (j + 1).v())
                return lin[j.slot(2)]

            def freed(ins, j):
                ins.then_inc(lin_freed[j.slot(2)], 1)

            def low(dst, whole, high, high_sem, k, low_sem):
                dve.wait_ge(high_sem, k)
                dve.tensor_tensor(dst, whole, high.bitcast(F32), ALU.subtract).then_inc(low_sem, 1)

            def norm_diag(name):
                k, n = NORM_NO[name], NTOK.get(name, S) // P
                dve.wait_ge(std_made, k + 1)
                dve.reciprocal(rstd[:, 0:n], std[:, 0:n]).then_inc(rstd_made, 1)
                dve.wait_ge(rstd_made, k + 1)
                for q in range(n):
                    ins = dve.tensor_scalar(te[:, q * P:(q + 1) * P], ident[:], rstd[:, q:q + 1], None, ALU.mult)
                ins.then_inc(diag_made, 1)

            def norm_apply(name, gain, src, hi, lo):
                n, w = NTILES[name], NTOK.get(name, S)
                dve.wait_ge(bc_ready, NORM_NO[name] + 1)
                for f in range(n + 1):
                    u = U0[name] + f
                    if f < n:
                        wait(dve, u_low, u - 1)
                        dve.scalar_tensor_tensor((tc, td)[u % 2][:, 0:w], src(f), col(gain, f), tr[0][:, 0:w],
                                                 ALU.mult, ALU.mult).then_inc(u_made, 1)
                    if f:
                        dve.wait_ge(u_made, u)
                        low(lo[:, f - 1, :], (tc, td)[(u - 1) % 2][:, 0:w], hi[:, f - 1, :], u_high, u, u_low)

            def maxima(n):
                for q in range(QT):
                    at = now(dve, n.times(3, SCORES_AT[q]))
                    dve.wait_ge(pool_made, 2)
                    wait(dve, scores_ready, at)
                    b, o = SBANK[q]
                    dve.tensor_tensor_reduce(logit[:, LOFF[q]:LOFF[q] + KEYS[q]], sc[b][:, o:o + KEYS[q]],
                                             bias[:, S - KEYS[q]:S], 1.0, 3e38, ALU.add, ALU.min,
                                             nmax[:, q:q + 1]).then_inc(logits_made, 1)

            def middle(n):
                wait(dve, probs_made, n.times(4, 4))
                wait(dve, out_copied, n.v())
                dve.reciprocal(rden, den).then_inc(rden_made, 1)
                wait(dve, pt_ready, n.times(3, 2))
                dve.tensor_copy(pt[:, 512:896], tr[1][:, 0:384]).then_inc(pt_dve, 1)

            def outputs(n, dst):
                wait(dve, rden_made, n.times(1, 1))
                wait(dve, out_ready, n.times(1, 1))
                dve.tensor_tensor(dst, ob[:, 0:QT * VD].rearrange("p (q d) -> p q d", q=QT),
                                  rden.unsqueeze(2).broadcast_to([P, QT, VD]), ALU.mult).then_inc(out_copied, 1)

            dve.memset(ones[:], 1.0).then_inc(start_made, 1)
            dve.memset(small[:, 0:1], EPS)
            dve.memset(small[:, 1:2], 4 * EPS).then_inc(start_made, 1)
            dve.memset(z[:, :, 0:PAD], 0.0).then_inc(start_made, 1)
            dve.memset(trig[0:64, :], 1.0).then_inc(start_made, 1)
            dve.memset(sel[:], 0.0).then_inc(start_made, 1)
            dve.wait_ge(start_made, 5)
            dve.wait_ge(pool_made, 1)
            for o in (64, 96):
                dve.tensor_tensor(sel[64:128, o:o + 32], ident[64:128, 64:96], ident[64:128, 96:128], ALU.add)\
                    .then_inc(start_made, 1)
            dve.wait_ge(vec_ready, 1)
            dve.tensor_copy(cols[:], tr[0][:, 0:NVEC]).then_inc(vec_copied, 1)
            dve.wait_ge(vec_ready, 2)
            dve.tensor_copy(taps[:].rearrange("p (t w) -> p t w", t=CT),
                            tr[1][:, 0:CT * 32].rearrange("p (t w) -> p t w", t=CT)[:, :, 0:TAPS])\
                .then_inc(vec_copied, 1)
            dve.wait_ge(vec_copied, 2)
            step(dve.tensor_scalar(hb, cols[:, COL["conv_ln_b"]:COL["conv_ln_b"] + CT], 0.5, None, ALU.mult))
            for f in range(DT):
                dve.wait_ge(xt_ready, f + 1)
                dve.tensor_copy(h[:, f, :], sc[f % 3][:]).then_inc(xt_copied, 1)
            lower(Idx(0))
            lower(Idx(1))
            norm_diag("mix")
            dve.wait_ge(xt_copied, DT)
            norm_apply("mix", "norm_mix_g", lambda f: h[:, f, :], uh, ul)

            r = slice(64, 128)
            dve.wait_ge(consts_landed, 16)
            dve.wait_ge(pos_landed, 16)
            ang, tmp = kt[r, :], logit[r, 0:S]
            freq, c_a, c_b, c_c = (consts[r, k:k + 1] for k in range(4))
            step(dve.tensor_copy(tmp, qt[r, :].bitcast(I32)))
            step(dve.tensor_scalar(ang, tmp, freq, None, ALU.mult))
            step(dve.tensor_scalar(tmp, ang, float(np.float32(1 / (2 * np.pi))), ROUND, ALU.mult, ALU.add))
            step(dve.tensor_scalar(tmp, tmp, -ROUND, None, ALU.add))
            for part in TWO_PI:
                step(dve.scalar_tensor_tensor(ang, tmp, -part, ang, ALU.mult, ALU.add))
            step(dve.tensor_scalar(ang, ang, 3.141592, -3.141592, ALU.min, ALU.max))
            step(dve.scalar_tensor_tensor(tmp, ang, -1.0, ang, ALU.mult, ALU.max))
            step(dve.tensor_scalar(tmp, tmp, c_b, c_c, ALU.mult, ALU.add))
            dve.scalar_tensor_tensor(ang, ang, c_a, tmp, ALU.mult, ALU.add).then_inc(trig_arg, 1)

            c, j = phase("latent")
            for m in range(6):
                lower(c + (m + 2))
                if m == 3:
                    norm_diag("q")
            for m in range(3):
                evacuated(dve, j + m)
            norm_apply("q", "q_norm_g", lambda f: cq[:, f, :], cqh, cql)
            dve.wait_ge(trig_made, 1)
            freed(dve.tensor_tensor(logit[:, 0:S], read(j + 5)[:], trig[:], ALU.mult), j + 5)
            c, j = phase("conv")
            lower(c + 2)
            dve.wait_ge(kr_ready, 1)
            dve.tensor_copy(kt[64:128, :], sc[0][64:128, :]).then_inc(kr_placed, 1)
            norm_diag("kv")
            for m in range(1, 8):
                if m == 2:
                    for k in (3, 4):
                        evacuated(dve, Idx(JOB0["latent"] + k))
                    norm_apply("kv", "kv_norm_g", lambda f: cq[:, 3 + f, :], ckh, ckl)
                lower(c + (m + 2))
                if m % 2:
                    t = m // 2
                    evacuated(dve, j + (m - 1))
                    evacuated(dve, j + m)
                    th = (logit[:, 512:1024], pt[:, 0:512])[t % 2]
                    zt = z[:, t, PAD:PAD + S]
                    dve.scalar_tensor_tensor(zt, th, 1.0, zt, ALU.add, ALU.mult).then_inc(z_made, 1)

            dve.wait_ge(z_made, CT)
            dve.wait_ge(pool_made, 2)

            def head(c, j, n, run):
                lower(c + 2)
                freed(dve.scalar_tensor_tensor(qt[:], read(j)[:], LINEAR_Q_SCALE, trig[:], ALU.mult, ALU.mult), j)
                lower(c + 3)
                run(0)
                wait(dve, vtr_ready, n.times(1, 1))
                dve.tensor_copy(vtok[:, :, 0:VD], ob[:, 256:512].rearrange("p (q d) -> p q d", q=QT))\
                    .then_inc(vtok_placed, 1)
                maxima(n)
                lower(c + 4)
                lower(c + 5)
                run(1)
                middle(n)
                run(2)
                at = n.times(VD)
                outputs(n, otok[:, :, at:at + VD] if n.i is None else otok[:, :, bass.ds(at, VD)])

            def two_heads(c, j, t, n):
                def tap(w):
                    zt, at = z[:, t, w:w + S], acc[:, t, :]
                    k = TAPS * t + w
                    if w == 0:
                        dve.tensor_scalar(at, zt, taps[:, bass.ds(k, 1)],
                                          cols[:, bass.ds(COL["conv_b"] + t, 1)], ALU.mult, ALU.add)\
                            .then_inc(tap_done, 1)
                    else:
                        dve.wait_ge(tap_done, k)
                        dve.scalar_tensor_tensor(at, zt, taps[:, bass.ds(k, 1)], at, ALU.mult, ALU.add)\
                            .then_inc(tap_done, 1)

                for p, cuts in ((0, (0, 6, 10, 16)), (1, (16, 22, 26, TAPS))):
                    head(c + 4 * p, j + 4 * p, n + p, lambda k: [tap(w) for w in range(cuts[k], cuts[k + 1])])

            with dve.Fori(0, CT - 1) as i:
                two_heads(*phase("heads", 8, 8, i), i, Idx(0, 2, i))
            c, j = phase("heads")
            two_heads(c + 8 * (CT - 1), j + 8 * (CT - 1), CT - 1, Idx(2 * (CT - 1)))

            dve.wait_ge(mean_ready, 1)
            dve.wait_ge(tap_done, CT * TAPS)
            for t in range(CT):
                dve.scalar_tensor_tensor(acc[:, t, :], sc[0][:], -1.0 / CONV, acc[:, t, :], ALU.mult, ALU.add)\
                    .then_inc(centred, 1)
                low(ol[:, t, :], sc[1 + t % 2][:], oh[:, t, :], o_high, t + 1, o_low)
            c, j = phase("mla_out")

            def mla_out(f):
                g = gates[:, DT + f, :]
                freed(dve.scalar_tensor_tensor(g, g, 1.0, read(j + f)[:], ALU.add, ALU.mult), j + f)

            lower(c + 2)
            mla_out(0)
            lower(c + 3)
            lower(c + 4)
            mla_out(1)
            norm_diag("conv")
            dve.wait_ge(centred, CT)
            dve.wait_ge(bc_ready, NORM_NO["conv"] + 1)
            for t in range(CT + 2):
                if t >= 2:
                    low(yl[:, t - 2, :], (tc, td)[t % 2][:], yh[:, t - 2, :], y_high, t - 1, y_low)
                if t < CT:
                    wait(dve, y_low, t - 1)
                    dve.scalar_tensor_tensor((tc, td)[t % 2][:], acc[:, t, :], col("conv_ln_g", t), tr[0][:],
                                             ALU.mult, ALU.mult).then_inc(y_norm, 1)
                    if t % 2 == 0:
                        mla_out(2 + t // 2)
                if 1 <= t <= CT:
                    dve.wait_ge(y_tanh, t)
                    dve.scalar_tensor_tensor((tc, td)[(t - 1) % 2][:], (ta, tb)[(t - 1) % 2][:], 1.0,
                                             (qt, kt)[(t - 1) % 2][:], ALU.add, ALU.mult).then_inc(y_made, 1)
            mla_out(4)
            mla_out(5)
            lower(c + 5)
            mla_out(6)
            mla_out(7)

            def merge(f, j, mine, other, base):
                freed(dve.scalar_tensor_tensor(mine[:, f, :], mine[:, f, :], 1.0, read(j)[:], ALU.add, ALU.mult), j)
                evacuated(dve, j)
                wait(dve, m_low, base + f - 1)
                dve.tensor_tensor((tc, td)[f % 2][:], mine[:, f, :], other[:, f, :], ALU.add).then_inc(m_made, 1)
                if f:
                    merge_low(f - 1, base)

            def merge_low(f, base):
                low(ul[:, f, :], (tc, td)[f % 2][:], uh[:, f, :], m_high, base + f + 1, m_low)

            def add_to_h(f, j, scale=None):
                at = h[:, f, :]
                if scale is None:
                    freed(dve.tensor_tensor(at, read(j)[:], at, ALU.add), j)
                else:
                    freed(dve.scalar_tensor_tensor(at, read(j)[:], scale, at, ALU.mult, ALU.add), j)

            c, j = phase("conv_out")
            for m in range(4):
                lower(c + (m + 2))
                for f in (2 * m, 2 * m + 1):
                    merge(f, j + f, gates, gates[:, DT:2 * DT, :], 0)
            merge_low(DT - 1, 0)

            c, j = phase("w_out")
            for m in range(DT):
                lower(c + (m + 2))
                add_to_h(m, j + m, 0.5)
                dve.wait_ge(mt_ready, m + 1)
                dve.tensor_copy(memt[:, m, :], sc[m % 3][:, 0:MEM]).then_inc(mt_copied, 1)
            norm_diag("mem")
            dve.wait_ge(mt_copied, DT)
            norm_apply("mem", "norm_mem_g", lambda f: memt[:, f, :], memh, meml)
            c, j = phase("xkv")

            def place_values(hd):
                dve.wait_ge(xvt_ready, hd + 1)
                dve.tensor_copy(xv[:, :, hd * XD:(hd + 1) * XD], ob[:, 0:256].rearrange("p (q d) -> p q d", q=2))\
                    .then_inc(xv_placed, 1)

            for m in range(8):
                lower(c + (m + 2))
                if m == 2:
                    norm_diag("xattn")
                if m == 4:
                    norm_apply("xattn", "norm_xattn_g", lambda f: h[:, f, :], uh, ul)
                if m >= 6:
                    place_values(m - 6)
            place_values(2)
            place_values(3)
            c, _ = phase("xq")
            for m in range(XH):
                lower(c + (m + 2))

            def x_maxima(hd):
                for b in range(2):
                    dve.wait_ge(xs_ready, 2 * hd + b + 1)
                    s_, k = ((sc[0], sc[1]), (sc[2], ob))[hd % 2][b], 4 * (hd % 2) + 2 * b
                    dve.tensor_reduce(xnmax[:, k:k + 2], s_[:].rearrange("p (q k) -> p q k", q=2), AX_X, ALU.min)\
                        .then_inc(xmax_made, 1)

            x_maxima(0)
            for hd in range(XH):
                if hd + 1 < XH:
                    x_maxima(hd + 1)
                for b in range(2):
                    k = 4 * (hd % 2) + 2 * b
                    dve.wait_ge(xp_made, 4 * hd + 2 * b + 2)
                    dve.reciprocal(xrden[:, k:k + 2], xden[:, k:k + 2]).then_inc(xrden_made, 1)
                    dve.wait_ge(xrden_made, 2 * hd + b + 1)
                    p_ = xp[:, hd % 2, 2 * b:2 * b + 2, :]
                    dve.tensor_tensor(p_, p_, xrden[:, k:k + 2].unsqueeze(2).broadcast_to([P, 2, MEM]), ALU.mult)\
                        .then_inc(xp_scaled, 1)
                dve.wait_ge(xpt_ready, 2 * hd + 2)
                dve.tensor_copy(xpt[:, hd % 2, :, 256:512], tr[1][:].rearrange("p (k q) -> p k q", k=2))\
                    .then_inc(xpt_dve, 1)
                dve.wait_ge(xo_ready, hd + 1)
                low(xol[:, hd, :], sc[2 * (hd % 2)][:], xoh[:, hd, :], xo_high, hd + 1, xo_low)
            c, j = phase("xo")
            for m in range(4):
                lower(c + (m + 2))
                for f in (2 * m, 2 * m + 1):
                    add_to_h(f, j + f)
            norm_diag("mlp")
            norm_apply("mlp", "norm_mlp_g", lambda f: h[:, f, :], uh, ul)

            for half in range(2):
                with dve.Fori(0, 4) as i:
                    c, j = phase(f"up{half}", 4, 4, i)
                    f = Idx(16 * half, 4, i)
                    for m in range(4):
                        lower(c + (m + 2))
                        evacuated(dve, j + m)
                        r_ = (ta, tb)[m % 2][:]
                        dve.wait_ge(f_low, f.times(1, m))
                        dve.tensor_tensor((tc, td)[m % 2][:], r_, r_, ALU.mult).then_inc(f_sq, 1)
                        low(fl[:, 4 * i + m, :], (tc, td)[m % 2][:], fh[:, 4 * i + m, :], f_high, f.times(1, m + 1),
                            f_low)
                with dve.Fori(0, 4) as i:
                    c, j = phase(f"down{half}", 4, 2, i)
                    for m in range(2):
                        lower(c + (2 * m + 2))
                        lower(c + (2 * m + 3))
                        add_to_h(2 * i + m, j + m)
                if half == 0:
                    dve.wait_ge(pool_made, 3)
                    dint = atok[:].rearrange("p a b -> p (a b)").bitcast(I32)
                    tint = rbc[:].bitcast(I32)
                    step(dve.tensor_scalar(tint, dint, 3, None, ALU.bitwise_and))
                    step(dve.tensor_scalar(nlog[:], tint, 0.0, None, ALU.is_equal))
                    step(dve.tensor_scalar(tint, dint, 15, None, ALU.bitwise_and))
                    step(dve.tensor_scalar(bias[:], tint, 0.0, None, ALU.is_equal))
                    step(dve.tensor_tensor(nlog[:], nlog[:], bias[:], ALU.add))
                    step(dve.tensor_scalar(bias[:], dist[:], 128.0, None, ALU.is_le))
                    step(dve.tensor_tensor(nlog[:], nlog[:], bias[:], ALU.add))
                    step(dve.tensor_scalar(rbc[:], nlog[:], 2.0, -float(np.log(2.0)), ALU.is_equal, ALU.mult))
                    step(dve.tensor_scalar(bias[:], nlog[:], 3.0, -float(np.log(3.0)), ALU.is_equal, ALU.mult))
                    step(dve.tensor_tensor(rbc[:], rbc[:], bias[:], ALU.add))
                    step(dve.tensor_scalar(bias[:], nlog[:], 0.0, BIG, ALU.is_equal, ALU.mult))
                    dve.tensor_tensor(nlog[:], rbc[:], bias[:], ALU.add).then_inc(table_made, 1)
            norm_diag("final")
            dve.wait_ge(bc_ready, NORM_NO["final"] + 1)
            for f in range(DT):
                dve.scalar_tensor_tensor(h[:, f, :], h[:, f, :], col("final_norm_g", f), tr[0][:], ALU.mult,
                                         ALU.mult).then_inc(x1_made, 1)
            norm_diag("second")
            norm_apply("second", "g_norm_2", lambda f: h[:, f, :], uh, ul)

            def gelu(j, k, dst):
                dve.wait_ge(g_square, k)
                dve.scalar_tensor_tensor(tb[:], ta[:], 1.0 / GELU_A, read(j)[:], ALU.add, ALU.mult).then_inc(g_poly, 1)
                dve.wait_ge(g_tanh, k)
                freed(dve.scalar_tensor_tensor(dst, ta[:], 1.0, read(j)[:], ALU.add, ALU.mult), j)

            with dve.Fori(0, 2) as i:
                c, j = phase("av", 4, 4, i)
                for m in range(4):
                    lower(c + (m + 2))
                    gelu(j + m, 4 * i + m + 1, av[:, 4 * i + m, :])
            norm_diag("gate_v")
            dve.wait_ge(bc_ready, NORM_NO["gate_v"] + 1)
            dve.tensor_copy(rbc[:], tr[0][:]).then_inc(rbc_made, 1)
            dve.wait_ge(rbc_made, 1)
            dve.wait_ge(pool_made, 4)

            def mask(n, k):
                dve.wait_ge(logits_made, n.times(4))
                dve.scalar_tensor_tensor(bias[:], dist[:], consts[:, bass.ds(4 + k, 1)], nlog[:], ALU.mult, ALU.add)\
                    .then_inc(bias_made, 1)
                dve.wait_ge(bias_made, (n + (1 - HEADS)).v())

            with dve.Fori(0, PAIRS) as i:
                c, j = phase("pairs", 8, 8, i)
                g, n0, n1 = Idx(0, 1, i), Idx(HEADS, 2, i), Idx(HEADS + 1, 2, i)
                lower(c + 2)
                lower(c + 3)
                freed(dve.tensor_copy(kt[:], read(j + 1)[:]), j + 1)
                lower(c + 4)
                lower(c + 5)
                dve.wait_ge(yb_low, g.v())
                dve.scalar_tensor_tensor(tc[:], av[:, i, :], cols[:, bass.ds(COL["g_v_2"] + i, 1)], rbc[:],
                                         ALU.mult, ALU.mult).then_inc(gv_made, 1)
                mask(n0, 2 * i)
                gelu(j + 3, g.times(1, PAIRS + 1), tb[:])
                dve.wait_ge(vtr_ready, g.times(1, HEADS + 1))
                dve.tensor_copy(vtok[:].rearrange("p q d -> p (q d)"), tr[0][:]).then_inc(vtok_placed, 1)
                maxima(n0)
                lower(c + 6)
                dve.wait_ge(silu_tanh, g.times(2, 1))
                freed(dve.scalar_tensor_tensor(te[:], ta[:], 1.0, read(j + 4)[:], ALU.add, ALU.mult), j + 4)
                evacuated(dve, j + 4)
                evacuated(dve, j + 3)
                dve.scalar_tensor_tensor(tb[:], tb[:], 0.25, te[:], ALU.mult, ALU.mult).then_inc(gate_prod, 1)
                middle(n0)
                mask(n1, 2 * i + 1)
                outputs(n0, otp[:, :, 0:VD])
                maxima(n1)
                dve.wait_ge(gvt_ready, g.times(1, 1))
                dve.tensor_copy(atok[:].rearrange("p q d -> p (q d)"), tr[1][:]).then_inc(atok_placed, 1)
                lower(c + 7)
                dve.wait_ge(gate_prod, g.times(1, 1))
                dve.wait_ge(silu_tanh, g.times(2, 2))
                freed(dve.scalar_tensor_tensor(te[:], ta[:], 1.0, read(j + 5)[:], ALU.add, ALU.mult), j + 5)
                middle(n1)
                outputs(n1, otp[:, :, VD:P])
                lower(c + 8)
                dve.wait_ge(ob_ready, g.times(1, 1))
                evacuated(dve, j + 5)
                dve.scalar_tensor_tensor(tc[:], tr[0][:], 0.5, te[:], ALU.mult, ALU.mult).then_inc(yb_made, 1)
                dve.wait_ge(mix_ready, g.times(1, 1))
                dve.tensor_tensor(ta[:].rearrange("p (q t) -> p q t", q=QT), tr[1][:].rearrange("p (q t) -> p q t", q=QT),
                                  bsb.unsqueeze(1).broadcast_to([P, QT, P]), ALU.add).then_inc(mix_read, 1)
                dve.wait_ge(mix_read, g.times(1, 1))
                dve.wait_ge(gate_prod, g.times(1, 1))
                dve.tensor_tensor(ya[:, i, :], ta[:], tb[:], ALU.mult).then_inc(ya_made, 1)
                low(ybl[:, i, :], tc[:], ybh[:, i, :], yb_high, g.times(1, 1), yb_low)
                lower(c + 9)

            c, j = phase("proj_a")
            for f in range(DT):
                low(ul[:, f, :], ya[:, f, :], uh[:, f, :], ya_high, f + 1, ya_low)
            for m in range(DT):
                lower(c + (m + 2))
                at = av[:, m, :]
                freed(dve.scalar_tensor_tensor(at, at, 1.0, read(j + m)[:], ALU.add, ALU.mult), j + m)
            evacuated(dve, j + (DT - 1))
            c, j = phase("proj_b")
            for m in range(DT):
                lower(c + (m + 2))
                merge(m, j + m, gb, av, DT)
            merge_low(DT - 1, DT)
            c, j = phase("w_out2")
            for m in range(DT):
                lower(c + (m + 2))
                add_to_h(m, j + m, 0.5)
            norm_diag("out")
            dve.wait_ge(bc_ready, NORM_NO["out"] + 1)
            for f in range(DT):
                wait(dve, fin_ready, f - 1)
                dve.scalar_tensor_tensor((tc, td)[f % 2][:], h[:, f, :], col("g_final_2", f), tr[0][:], ALU.mult,
                                         ALU.mult).then_inc(fin_made, 1)


USED = ["x", "mem", "positions", "norm_mix_g", "w_in", "conv_w", "conv_b", "conv_ln_g", "conv_ln_b", "w_conv_out",
        "q_norm_g", "w_uq", "kv_norm_g", "w_ukv", "w_mla_out", "w_out", "norm_xattn_g", "norm_mem_g", "w_xq", "w_xkv",
        "w_xo", "norm_mlp_g", "w_mlp1", "w_mlp2", "final_norm_g", "g_norm_2", "w_in_2", "w_s_2", "b_s_2", "g_v_2",
        "w_proj_a_2", "w_proj_b_2", "w_out_2", "g_final_2"]


def shape_consts():
    c = np.zeros((P, NCONST), np.float32)
    half = ROPE // 2
    freq = np.float32(10000.0) ** (-np.arange(half, dtype=np.float32) / np.float32(half))
    c[64:, 0] = np.tile(freq, 4)
    c[64:96, 2], c[64:96, 3] = -1.0, np.float32(np.pi / 2)
    c[96:112, 1], c[112:, 1] = -1.0, 1.0
    c[:, 4:] = np.float32(2.0) ** (np.float32(-0.5) * np.arange(1, 17, dtype=np.float32))
    return c


def kernel(**inputs):
    import concourse.bacc as bacc
    from concourse.bass_utils import run_bass_kernel_spmd

    nc = bacc.Bacc("TRN2", target_bir_lowering=False, num_devices=1)
    arrays = {f"in_{n}_dram": np.ascontiguousarray(inputs[n]) for n in USED}
    arrays["in_shape_consts_dram"] = shape_consts()
    aps = {}
    for name, v in arrays.items():
        aps[name[3:-5]] = nc.dram_tensor(name, v.shape, mybir.dt.from_np(v.dtype), kind="ExternalInput").ap()
    out = nc.dram_tensor("out_0_dram", (1, S, D), F32, kind="ExternalOutput").ap()
    build(nc, aps, out)
    r = run_bass_kernel_spmd(nc, [arrays], core_ids=[0])
    return r.results[0]["out_0_dram"]
```

```python
from contextlib import ExitStack

import numpy as np

import concourse.bass as bass
from concourse import mybir

F32 = mybir.dt.float32
F32R = mybir.dt.float32r
I32 = mybir.dt.int32
ALU = mybir.AluOpType
ACT = mybir.ActivationFunctionType
AX_X = mybir.AxisListType.X

P = 128
S = 512
D = 1024
DT = D // P
QT = S // P
MEM = 256
CONV = 512
CT = CONV // P
TAPS = 31
PAD = TAPS - 1
HEADS = 8
NOPE, ROPE, VD = 64, 32, 64
QLORA, KVLORA = 384, 256
XH, XD = 4, 128
FF = 4096
EPS = 1e-6
BIG = 1e30
PAIRS = 8
GELU_A = 0.044715
GELU_C = 0.7978845608028654
LINEAR_Q_SCALE = -float((NOPE + ROPE) ** -0.5)
CROSS_Q_SCALE = -float(XD ** -0.5)
DILATED_Q_SCALE = -0.125

VECS = [("norm_mix_g", 8), ("conv_b", 4), ("conv_ln_g", 4), ("conv_ln_b", 4), ("q_norm_g", 3), ("kv_norm_g", 2),
        ("norm_xattn_g", 8), ("norm_mem_g", 8), ("norm_mlp_g", 8), ("final_norm_g", 8), ("g_norm_2", 8),
        ("g_v_2", 8), ("g_final_2", 8)]
COL, NVEC = {}, 0
for _name, _n in VECS:
    COL[_name] = NVEC
    NVEC += _n

PHASES = [("latent", 6, 6), ("conv", 8, 8), ("heads", 32, 32), ("mla_out", 4, 8), ("conv_out", 4, 8),
          ("w_out", 8, 8), ("xkv", 8, 8), ("xq", 4, 4), ("xo", 4, 8), ("up0", 16, 16), ("down0", 16, 8), ("up1", 16, 16),
          ("down1", 16, 8), ("av", 8, 8), ("pairs", 64, 64), ("proj_a", 8, 8), ("proj_b", 8, 8), ("w_out2", 8, 8)]
CHUNK0, JOB0, NCHUNKS, NJOBS = {}, {}, 0, 0
for _name, _c, _j in PHASES:
    CHUNK0[_name], JOB0[_name] = NCHUNKS, NJOBS
    NCHUNKS += _c
    NJOBS += _j

NORMS = [("mix", 8), ("q", 3), ("kv", 2), ("conv", 4), ("mem", 8), ("xattn", 8), ("mlp", 8), ("second", 0),
         ("final", 0), ("gate_v", 0), ("out", 8)]
NORM_NO = {n: k for k, (n, _) in enumerate(NORMS)}
BROADCAST = ["mix", "q", "kv", "conv", "mem", "mlp", "second", "final", "out"]
BC_NO = {n: k for k, n in enumerate(BROADCAST)}
SQ0, _t = {}, 0
for _name, _n in NORMS:
    SQ0[_name] = _t
    _t += _n
SPLITS = [("mix", 8, 1), ("q", 3, 1), ("kv", 2, 1), ("xattn", 8, 0), ("mlp", 8, 0), ("raw", 8, 0),
          ("second", 8, 1)]
U0, NORMED0, _t, _m = {}, {}, 0, 0
for _name, _n, _normed in SPLITS:
    U0[_name], NORMED0[_name] = _t, _m
    _t, _m = _t + _n, _m + _n * _normed


COUNTS = {n: (c, j) for n, c, j in PHASES}
NCONST = 4 + 16
SEL_MADE = 7
ROUND = 1.5 * 2.0 ** 23
TWO_PI = (6.28125, 0.00193500518798828125, 2 * np.pi - 6.28125 - 0.00193500518798828125)
TWO_PI = tuple(float(v) for v in TWO_PI)


def chunk_size(c):
    k = c - CHUNK0["heads"]
    return 1024 if not 0 <= k < COUNTS["heads"][0] else (3 * P, 2 * P, 1024, 1024)[k % 4]


class Idx:

    def __init__(self, static, per=0, i=None):
        self.static, self.per, self.i = static, per, i

    def __add__(self, k):
        return Idx(self.static + k, self.per, self.i)

    def times(self, m, k=0):
        v = self.static * m + k
        return v if self.i is None else v + (self.per * m) * self.i

    def v(self):
        return self.times(1)

    def half(self):
        assert self.per % 2 == 0
        return self.static // 2 if self.i is None else self.static // 2 + (self.per // 2) * self.i

    def slot(self, m):
        assert self.per % m == 0
        return self.static % m


def build(nc, a, out):
    ctx = ExitStack()
    with ctx:
        def sem(name):
            return ctx.enter_context(nc.semaphore(name))

        def sb(name, shape, dt=F32, stack=ctx):
            return stack.enter_context(nc.sbuf_tensor(name, shape, dt))

        def bank(name):
            return ctx.enter_context(nc.psum_tensor(name, [P, 512], F32))

        lin = [bank("lin0"), bank("lin1")]
        sc = [bank("sc0"), bank("sc1"), bank("sc2")]
        tr = [bank("tr0"), bank("tr1")]
        ob = bank("ob")

        h = sb("h", [P, DT, S])
        uh = sb("uh", [P, DT, S], F32R)
        ul = sb("ul", [P, DT, S], F32R)
        raw = sb("raw", [P, 2, 1024])
        wh = sb("wh", [P, 4, 1024], F32R)
        wl = sb("wl", [P, 4, 1024], F32R)
        ident = sb("ident", [P, P])
        ones = sb("ones", [P, P])
        cols = sb("cols", [P, NVEC])
        both = sb("both", [P, DT])
        taps = sb("taps", [P, CT * TAPS])
        consts = sb("consts", [P, NCONST])
        small = sb("small", [P, 64])
        logit = sb("logit", [P, 1280])
        pt = sb("pt", [P, 896])
        qt = sb("qt", [P, S])
        kt = sb("kt", [P, S])
        vtok = sb("vtok", [P, QT, P])
        ta, tb, tc, td, te = (sb(n, [P, S]) for n in ("ta", "tb", "tc", "td", "te"))
        bias = sb("bias", [P, S])
        wst = sb("wst", [P, P])
        sel = wst
        trig = sb("trig", [P, S])
        dist = trig

        eps, eps4 = small[:, 0:1], small[:, 1:2]
        std, rstd = small[:, 4:8], small[:, 8:12]
        nmax = small[:, 12:16]
        den, rden = small[:, 16:20], small[:, 20:24]
        hb = small[:, 24:28]
        xnmax, xden, xrden = small[:, 32:40], small[:, 40:48], small[:, 48:56]
        mem_rstd = small[:, 56:58]
        minus_rstd = small[:, 60:64]
        final_rstd, final_sq = small[:, 28:32], small[:, 60:64]

        st = ExitStack()
        gates = sb("gates", [P, 16, S], stack=st)
        acc = sb("acc", [P, CT, S], stack=st)
        otok = sb("otok", [P, QT, S], stack=st)
        s2 = ExitStack()
        cqh = sb("cqh", [P, 3, S], F32R, s2)
        cql = sb("cql", [P, 3, S], F32R, s2)
        ckh = sb("ckh", [P, 2, S], F32R, s2)
        ckl = sb("ckl", [P, 2, S], F32R, s2)
        z = sb("z", [P, CT, S + PAD], stack=s2)
        s2.close()
        yh = sb("yh", [P, CT, S], F32R, st)
        yl = sb("yl", [P, CT, S], F32R, st)
        oh = sb("oh", [P, 4, S], F32R, st)
        ol = sb("ol", [P, 4, S], F32R, st)
        st.close()
        st = ExitStack()
        xtok = sb("xtok", [P, QT, D], stack=st)
        vrows = sb("vrows", [P, P], stack=st)
        crows = sb("crows", [TAPS, CONV], stack=st)
        st.close()
        st = ExitStack()
        xq = sb("xq", [P, XH, S], stack=st)
        s2 = ExitStack()
        xuh = sb("xuh", [P, DT, S], F32R, s2)
        xul = sb("xul", [P, DT, S], F32R, s2)
        s2.close()
        xp = sb("xp", [P, 2, QT, MEM], stack=st)
        xpt = sb("xpt", [P, 2, 2, S], stack=st)
        xoh = sb("xoh", [P, XH, S], F32R, st)
        xol = sb("xol", [P, XH, S], F32R, st)
        memtok = sb("memtok", [P, 2, D], stack=st)
        memh = sb("memh", [P, DT, MEM], F32R, st)
        meml = sb("meml", [P, DT, MEM], F32R, st)
        xk = sb("xk", [P, XH, MEM], stack=st)
        xv = sb("xv", [P, 2, XH * XD], stack=st)
        st.close()
        st = ExitStack()
        fh = sb("fh", [P, 16, S], F32R, st)
        fl = sb("fl", [P, 16, S], F32R, st)
        st.close()
        st = ExitStack()
        av = sb("av", [P, PAIRS, S], stack=st)
        gb = sb("gb", [P, PAIRS, S], stack=st)
        ya = sb("ya", [P, PAIRS, S], stack=st)
        vh = sb("vh", [P, DT, S], F32R, st)
        vl = sb("vl", [P, DT, S], F32R, st)
        ybh, ybl = uh, ul
        otp = sb("otp", [P, QT, P], stack=st)
        rbc = sb("rbc", [P, S], stack=st)
        nlog = sb("nlog", [P, S], stack=st)
        atok = sb("atok", [P, QT, P], stack=st)
        st.close()
        cq = gates[:, 11:16, :]
        ws, bsb = ya[:, PAIRS - 1, 0:P], ya[:, PAIRS - 1, P:2 * P]

        mlp_scale = logit[:, 0:S]
        mem_scale = td[:, 0:MEM]
        scaled = pt[:, 0:S]
        sum_h, sum_x1, sum_gate, gate_sq = qt, kt, logit[:, S:2 * S], logit[:, 0:S]

        x_landed, mem_landed, vecs_landed, taps_landed, consts_landed, pos_landed = (
            sem(n + "_landed") for n in ("x", "mem", "vecs", "taps", "consts", "pos"))
        raw_landed = [sem("raw0_landed"), sem("raw1_landed")]
        swapped_landed, gating_landed = sem("swapped_landed"), sem("gating_landed")
        hi_made, lo_made = sem("hi_made"), sem("lo_made")
        chunk_entered = sem("chunk_entered")
        lin_ready = sem("lin_ready")
        lin_freed = [sem("lin0_freed"), sem("lin1_freed")]
        pool_made, table_made = sem("pool_made"), sem("table_made")
        start_made = sem("start_made")
        xt_ready, xt_copied = sem("xt_ready"), sem("xt_copied")
        vec_ready, vec_copied = sem("vec_ready"), sem("vec_copied")
        trig_arg, trig_made = sem("trig_arg"), sem("trig_made")
        sq_made, sq_summed = sem("sq_made"), sem("sq_summed")
        std_made, rstd_made, diag_made, bc_ready = (sem(n) for n in ("std_made", "rstd_made", "diag_made", "bc_ready"))
        u_made, u_high, u_low = sem("u_made"), sem("u_high"), sem("u_low")
        kr_ready, kr_placed = sem("kr_ready"), sem("kr_placed")
        z_made, tap_done = sem("z_made"), sem("tap_done")
        vtr_ready, vtok_placed = sem("vtr_ready"), sem("vtok_placed")
        bias_made = sem("bias_made")
        scores_ready, logits_made, probs_made = sem("scores_ready"), sem("logits_made"), sem("probs_made")
        pt_ready, pt_act, pt_dve = sem("pt_ready"), sem("pt_copied_scalar"), sem("pt_copied_vector")
        rden_made, out_ready, out_copied = sem("rden_made"), sem("out_ready"), sem("out_copied")
        ot_ready, o_high, o_low = sem("ot_ready"), sem("o_high"), sem("o_low")
        mean_ready, centred = sem("mean_ready"), sem("centred")
        y_norm, y_half, y_tanh, y_made, y_high, y_low = (
            sem(n) for n in ("y_norm", "y_half", "y_tanh", "y_made", "y_high", "y_low"))
        m_made, m_high, m_low = sem("merged_made"), sem("merged_high"), sem("merged_low")
        mt_ready = sem("mt_ready")
        xvt_ready, xv_placed = sem("xvt_ready"), sem("xv_placed")
        xs_ready, xmax_made, xp_made, xrden_made, xp_scaled = (
            sem(n) for n in ("xs_ready", "xmax_made", "xp_made", "xrden_made", "xp_scaled"))
        xpt_ready, xpt_act, xpt_dve = sem("xpt_ready"), sem("xpt_copied_scalar"), sem("xpt_copied_vector")
        xo_ready, xo_high, xo_low = sem("xo_ready"), sem("xo_high"), sem("xo_low")
        f_sq, f_high, f_low = sem("f_sq"), sem("f_high"), sem("f_low")
        x1_made = sem("x1_made")
        g_square, g_poly, g_tanh = sem("gelu_square"), sem("gelu_poly"), sem("gelu_tanh")
        rbc_made = sem("rbc_made")
        mlp_scaled, mem_scaled, h_added = sem("mlp_scale_made"), sem("mem_scale_made"), sem("h_added")
        sums_cleared, minus_made = sem("sums_cleared"), sem("minus_made")
        hsq_made, hsq_added, gsq_made, gsq_added = (sem(n) for n in ("hsq_made", "hsq_added", "gsq_made", "gsq_added"))
        xmin_made, mem_high, mem_low = sem("xmin_made"), sem("mem_high"), sem("mem_low")
        added_summed, gating_made = sem("added_summed"), sem("gating_made")
        gv_made, gvt_ready, atok_placed = sem("gv_made"), sem("gvt_ready"), sem("atok_placed")
        ws_masked, wst_ready, wst_placed = sem("ws_masked"), sem("wst_ready"), sem("wst_placed")
        mix_ready, mix_read, ya_made = sem("mix_ready"), sem("mix_read"), sem("ya_made")
        silu_tanh, gate_prod = sem("silu_tanh"), sem("gate_prod")
        ob_ready, yb_made, yb_high, yb_low = (sem(n) for n in ("ob_ready", "yb_made", "yb_high", "yb_low"))
        ya_high, ya_low = sem("ya_high"), sem("ya_low")
        fin_made, fin_ready, fin_copied, stored = (sem(n) for n in ("fin_made", "fin_ready", "fin_copied", "stored"))
        vector_steps, pool_steps = sem("vector_steps"), sem("pool_steps")

        def wait(eng, s, v):
            if not isinstance(v, int) or v > 0:
                eng.wait_ge(s, v)

        def now(eng, v):
            return v if isinstance(v, int) else eng.snap(eng.to_reg(v))

        def phase(name, per_c=0, per_j=0, i=None):
            return Idx(CHUNK0[name], per_c, i), Idx(JOB0[name], per_j, i)

        def col(name, k=0):
            return cols[:, COL[name] + k:COL[name] + k + 1]

        def evacuated(eng, j):
            eng.wait_ge(lin_freed[j.slot(2)], (j + 2).half())

        def chain(eng, s):
            done = [0]

            def step(ins):
                done[0] += 1
                ins.then_inc(s, 1)
                eng.wait_ge(s, done[0])
            return step

        BC_READ = {n: (u_made, NORMED0[n] + k) for n, k in (("mix", 8), ("q", 3), ("kv", 2))}
        BC_READ.update(conv=(y_norm, CT), mem=(mem_scaled, 1), mlp=(mlp_scaled, 1), second=(rbc_made, 1),
                       final=(x1_made, DT), out=(fin_made, DT))
        NTOK = {"mem": MEM}
        WIDTH = {"q": QLORA, "kv": KVLORA, "conv": CONV}
        NTILES = dict(NORMS)
        SPLIT_TILES = {n: k for n, k, _ in SPLITS}
        SLOTS = {"mlp": (qt, kt)}

        KEYS = [P * (q + 1) for q in range(QT)]
        LOFF = [0, 128, 384, 768]
        SBANK = [(0, 0), (0, 128), (1, 0), (2, 0)]
        PTBANK = [(0, 0), (0, 128), (1, 0), (0, 0)]
        PTOFF = [0, 128, 512, 0]
        SCORES_AT = [1, 1, 2, 3]

        block = ctx.enter_context(nc.Block())

        @block.sync
        def _(sp):
            def view(w):
                return w.rearrange("(k p) m -> p k m", p=P)

            def place(c, k, m):
                at = now(sp, (c + -1).v())
                if not isinstance(at, int):
                    sp.wait_ge(lo_made, 1)
                wait(sp, lo_made, at)
                return raw[:, c.slot(2), 0:k * m].rearrange("p (k m) -> p k m", k=k)

            def load(c, w, first, k, m):
                src = view(w)[:, :, bass.ds(now(sp, first), m)]
                sp.dma_start(place(c, k, m), src).then_inc(raw_landed[c.slot(2)], 16)

            def load_rope(c, w, first, rope, k):
                half = ROPE // 2
                src, second, front = (view(w)[:, :, bass.ds(now(sp, at), n)] for at, n in
                                      ((first, 96), (rope + half, half), (rope, half)))
                dst = place(c, k, P)
                sp.dma_start(dst[:, :, 0:96], src).then_inc(raw_landed[c.slot(2)], 16)
                sp.dma_start(dst[:, :, 96:96 + half], second).then_inc(swapped_landed, 16)
                sp.dma_start(dst[:, :, 96 + half:P], front).then_inc(swapped_landed, 16)

            def stream(name, w, first, k, m):
                with sp.Fori(0, COUNTS[name][0] // 4) as i:
                    c, _ = phase(name, 4, 0, i)
                    for n in range(4):
                        load(c + n, w, first + m * n + (m * 4) * i, k, m)

            w_in, w_in2 = a["w_in"][0], a["w_in_2"][0]
            c, _ = phase("latent")
            for m in range(5):
                load(c + m, w_in, 2 * CONV + P * m, DT, P)
            rope0 = 2 * CONV + QLORA + KVLORA
            load_rope(c + 5, w_in, rope0 - NOPE, rope0, DT)
            with sp.Fori(0, 2) as i:
                c, _ = phase("conv", 4, 0, i)
                for m in range(4):
                    load(c + m, w_in, (m % 2) * CONV + (m // 2) * P + (2 * P) * i, DT, P)
            with sp.Fori(0, HEADS) as i:
                c, _ = phase("heads", 4, 0, i)
                load_rope(c, a["w_uq"][0], 96 * i, 96 * i + NOPE, 3)
                load(c + 1, a["w_ukv"][0], P * i, 2, P)
                for m in range(2):
                    load(c + 2 + m, w_in, rope0 + ROPE + P * m + (2 * P) * i, DT, P)
            stream("mla_out", a["w_mla_out"][0], 0, 4, 256)
            stream("conv_out", a["w_conv_out"][0], 0, 4, 256)
            c, _ = phase("w_out")
            for m in range(DT):
                if m == 2:
                    sp.wait_ge(m_made, DT)
                    sp.dma_start(memtok[:], a["mem"][0].rearrange("(q p) n -> p q n", p=P)).then_inc(mem_landed, 16)
                load(c + m, a["w_out"][0], P * m, DT, P)
            stream("xkv", a["w_xkv"][0], 0, DT, P)
            stream("xq", a["w_xq"][0], 0, DT, P)
            stream("xo", a["w_xo"][0], 0, 4, 256)
            for half in range(2):
                stream(f"up{half}", a["w_mlp1"][0], half * FF // 2, DT, P)
                with sp.Fori(0, 4) as i:
                    c, _ = phase(f"down{half}", 4, 0, i)
                    for m in range(4):
                        first = half * FF // 2 + (m % 2) * D
                        load(c + m, a["w_mlp2"][0][first:first + D, :], (m // 2) * P + (2 * P) * i, DT, P)
            stream("av", w_in2, D, DT, P)
            with sp.Fori(0, PAIRS) as i:
                c, _ = phase("pairs", 8, 0, i)
                for m, first in enumerate((3, 4, 5, 0, 2, 6, 7, 8)):
                    load(c + m, w_in2, first * D + P * i, DT, P)
                    if m == 3:
                        weights, biases = a["w_s_2"][0][i], a["b_s_2"][0][i].partition_broadcast(P)
                        sp.wait_ge(mix_read, i)
                        sp.dma_start(ws, weights).then_inc(gating_landed, 16)
                        sp.dma_start(bsb, biases).then_inc(gating_landed, 16)
            stream("proj_a", a["w_proj_a_2"][0], 0, DT, P)
            stream("proj_b", a["w_proj_b_2"][0], 0, DT, P)
            stream("w_out2", a["w_out_2"][0], 0, DT, P)
            for f in range(DT):
                sp.wait_ge(fin_copied, f + 1)
                sp.dma_start(out[0].rearrange("(q p) n -> p q n", p=P)[:, :, f * P:(f + 1) * P],
                             ya[:, f, :].rearrange("p (q n) -> p q n", q=QT)).then_inc(stored, 16)
            sp.wait_ge(stored, 16 * DT)

        @block.gpsimd
        def _(pool):
            step = chain(pool, pool_steps)
            step(pool.memset(ident[:], 0.0))
            pool.affine_select(out=ident[:], in_=ident[:], compare_op=ALU.not_equal, fill=1.0, base=0,
                               pattern=[[-1, P]], channel_multiplier=1).then_inc(pool_made, 1)
            step(pool.memset(bias[:], 0.0))
            pool.affine_select(out=bias[:], in_=bias[:], compare_op=ALU.is_ge, fill=BIG, base=S - P,
                               pattern=[[-1, S]], channel_multiplier=1).then_inc(pool_made, 1)
            pool.wait_ge(xo_low, XH)
            dint = atok[:].rearrange("p a b -> p (a b)").bitcast(I32)
            step(pool.iota(dint, [[-1, S]], base=S - P, channel_multiplier=1))
            pool.tensor_copy(dist[:], dint).then_inc(pool_made, 1)
            pool.wait_ge(table_made, 1)
            pool.affine_select(out=nlog[:], in_=nlog[:], compare_op=ALU.is_ge, fill=BIG, base=S - P,
                               pattern=[[-1, S]], channel_multiplier=1).then_inc(pool_made, 1)
            pool.wait_ge(std_made, NORM_NO["mlp"] + 1)
            pool.memset(sum_h[:], 0.0).then_inc(sums_cleared, 1)
            pool.memset(sum_x1[:], 0.0).then_inc(sums_cleared, 1)
            pool.wait_ge(sums_cleared, 2)
            with pool.Fori(0, DT) as f:
                for n, (total, part) in enumerate(((sum_h, ta), (sum_x1, tb))):
                    pool.wait_ge(hsq_made, 2 * f + (n + 1))
                    pool.wait_ge(hsq_added, 2 * f + n)
                    pool.tensor_tensor(total[:], total[:], part[:], ALU.add).then_inc(hsq_added, 1)
            pool.memset(sum_gate, 0.0).then_inc(sums_cleared, 1)
            pool.wait_ge(sums_cleared, 3)
            with pool.Fori(0, PAIRS) as f:
                pool.wait_ge(gsq_made, f + 1)
                pool.wait_ge(gsq_added, f)
                pool.tensor_tensor(sum_gate, sum_gate, gate_sq, ALU.add).then_inc(gsq_added, 1)
            with pool.Fori(0, PAIRS) as i:
                at = now(pool, 32 * i + 32)
                pool.wait_ge(table_made, 1)
                pool.wait_ge(gating_landed, at)
                pool.affine_select(out=ws, in_=ws, compare_op=ALU.is_ge, fill=0.0, base=0, pattern=[[-1, P]],
                                   channel_multiplier=1).then_inc(ws_masked, 1)

        @block.tensor
        def _(pe):
            def products(o, slot, k, m, xh_, xl_, start, stop, w, enter):
                at = slice(k * w + m * P, k * w + (m + 1) * P)
                ins = pe.matmul(o, wh[:, slot, at], xh_, start=start, stop=False)
                if enter:
                    ins.then_inc(chunk_entered, 1)
                pe.matmul(o, wh[:, slot, at], xl_, start=False, stop=False)
                return pe.matmul(o, wl[:, slot, at], xh_, start=False, stop=stop)

            def open_job(j):
                wait(pe, lin_freed[j.slot(2)], j.half())
                return lin[j.slot(2)]

            def job(c, j, rows, xh_, xl_, n=S, before=None, between={}):
                o = open_job(j)[:, 0:n]
                wait(pe, lo_made, (c + 1).v())
                for k in range(rows):
                    if before is not None:
                        before(k)
                    if k in between:
                        between[k]()
                    ins = products(o, c.slot(4), k, 0, xh_[:, k, :], xl_[:, k, :], k == 0, k == rows - 1, P, k == 0)
                ins.then_inc(lin_ready, 1)

            def two_jobs(c, j, xh_, xl_, before=None):
                wait(pe, lo_made, (c + 1).v())
                for m in range(2):
                    o = open_job(j + m)[:]
                    for k in range(4):
                        if before is not None and m == 0:
                            before(k)
                        ins = products(o, c.slot(4), k, m, xh_[:, k, :], xl_[:, k, :], k == 0, k == 3, 256,
                                       m == 0 and k == 0)
                    ins.then_inc(lin_ready, 1)

            def tiles_of(sem_, base):
                return lambda k: pe.wait_ge(sem_, base + k + 1)

            def turn_tile(dst, src, n=QT, idt=ident):
                for q in range(n):
                    ins = pe.transpose(dst[:, q * P:(q + 1) * P], src(q), idt[:])
                return ins

            def sum_squares(name, f):
                s, n = SQ0[name] + f, NTILES[name]
                if f == 0:
                    wait(pe, std_made, NORM_NO[name])
                pe.wait_ge(sq_made, s + 1)
                for q in range(NTOK.get(name, S) // P):
                    ins = pe.matmul(tr[1][:, q:q + 1], SLOTS.get(name, (ta, tb))[s % 2][:, q * P:(q + 1) * P], ones[:, 0:1],
                                    start=(f == 0 and q == 0), stop=(f == n - 1), skip_group_check=True)
                ins.then_inc(sq_summed, 1)

            def sums(name):
                for f in range(NTILES[name]):
                    sum_squares(name, f)

            def broadcast(name):
                k = BC_NO[name]
                if k:
                    pe.wait_ge(*BC_READ[BROADCAST[k - 1]])
                pe.wait_ge(diag_made, k + 1)
                n = NTOK.get(name, S)
                pe.matmul(tr[0][:, 0:n], ones[:], te[:, 0:n], start=True, stop=True).then_inc(bc_ready, 1)

            def sum_added(*totals):
                for k, total in enumerate(totals):
                    for q in range(QT):
                        ins = pe.matmul(tr[1][:, 4 * k + q:4 * k + q + 1], total[:, q * P:(q + 1) * P], ones[:, 0:1],
                                        start=(k == 0 and q == 0), stop=True, skip_group_check=True)
                ins.then_inc(added_summed, 1)

            def scores(n, rows):
                wait(pe, logits_made, n.times(4))
                for q in range(QT):
                    b, o = SBANK[q]
                    ins = pe.matmul(sc[b][:, o:o + KEYS[q]], qt[rows, q * P:(q + 1) * P], kt[rows, 0:KEYS[q]],
                                    start=True, stop=True)
                    if q:
                        ins.then_inc(scores_ready, 1)

            def turn(q):
                b, o = PTBANK[q]
                for kb in range(q + 1):
                    ins = pe.transpose(tr[b][:, o + kb * P:o + (kb + 1) * P],
                                       logit[:, LOFF[q] + kb * P:LOFF[q] + (kb + 1) * P], ident[:])
                return ins

            def weigh(q, v):
                for kb in range(q + 1):
                    ins = pe.matmul(ob[:, q * VD:(q + 1) * VD], pt[:, PTOFF[q] + kb * P:PTOFF[q] + (kb + 1) * P],
                                    v(kb), start=kb == 0, stop=kb == q)
                return ins

            def finish(n, v):
                def turn_0_1():
                    wait(pe, probs_made, n.times(4, 2))
                    wait(pe, pt_act, n.times(2))
                    turn(0)
                    turn(1).then_inc(pt_ready, 1)

                def turn_2():
                    wait(pe, probs_made, n.times(4, 3))
                    wait(pe, pt_dve, n.v())
                    turn(2).then_inc(pt_ready, 1)

                def weigh_0_1_turn_3():
                    wait(pe, pt_act, n.times(2, 1))
                    wait(pe, out_copied, n.v())
                    weigh(0, v)
                    weigh(1, v)
                    wait(pe, probs_made, n.times(4, 4))
                    turn(3).then_inc(pt_ready, 1)

                def weigh_2():
                    wait(pe, pt_dve, n.times(1, 1))
                    weigh(2, v)

                def weigh_3():
                    wait(pe, pt_act, n.times(2, 2))
                    weigh(3, v).then_inc(out_ready, 1)

                return turn_0_1, turn_2, weigh_0_1_turn_3, weigh_2, weigh_3

            pe.wait_ge(pool_made, 1)
            pe.wait_ge(vecs_landed, 16 * len(VECS))
            pe.transpose(tr[0][:, 0:NVEC], vrows[0:NVEC, :], ident[0:NVEC, 0:NVEC]).then_inc(vec_ready, 1)
            pe.wait_ge(taps_landed, 16)
            for t in range(CT):
                ins = pe.transpose(tr[1][:, t * 32:t * 32 + TAPS], crows[:, t * P:(t + 1) * P],
                                   ident[0:TAPS, 0:TAPS])
            ins.then_inc(vec_ready, 1)
            pe.wait_ge(start_made, 1)
            pe.wait_ge(vec_copied, 2)
            pe.wait_ge(x_landed, 16)
            for f in range(DT + 1):
                if f < DT:
                    if f >= 3:
                        pe.wait_ge(xt_copied, f - 2)
                    turn_tile(sc[f % 3], lambda q: xtok[:, q, f * P:(f + 1) * P]).then_inc(xt_ready, 1)
                if f:
                    sum_squares("mix", f - 1)
            broadcast("mix")

            c, j = phase("latent")
            for m in range(6):
                job(c + m, j + m, DT, uh, ul, before=tiles_of(u_low, U0["mix"]) if m == 0 else None)
                if m == 3:
                    sums("q")
                if m == 4:
                    broadcast("q")
            sums("kv")

            c, j = phase("conv")
            for m in range(8):
                job(c + m, j + m, DT, uh, ul)
                if m == 0:
                    evacuated(pe, Idx(JOB0["latent"] + 5))
                    pe.wait_ge(start_made, SEL_MADE)
                    pe.matmul(sc[0][:], sel[64:128, :], logit[64:128, 0:S], start=True, stop=True).then_inc(kr_ready, 1)
                if m == 1:
                    broadcast("kv")

            pe.wait_ge(u_low, U0["kv"] + 2)
            pe.wait_ge(kr_placed, 1)
            with pe.Fori(0, HEADS) as i:
                c, j = phase("heads", 4, 4, i)
                n = Idx(0, 1, i)
                job(c, j, 3, cqh, cql)
                job(c + 1, j + 1, 2, ckh, ckl)

                def turn_values_and_score():
                    pe.wait_ge(pool_made, 1)
                    wait(pe, out_copied, n.v())
                    evacuated(pe, j + 1)
                    for kb in range(QT):
                        ins = pe.transpose(ob[:, 256 + kb * VD:256 + (kb + 1) * VD], td[64:128, kb * P:(kb + 1) * P],
                                           ident[64:128, 64:128])
                    ins.then_inc(vtr_ready, 1)
                    evacuated(pe, j)
                    scores(n, slice(0, P))

                parts = finish(n, lambda kb: vtok[:, kb, 0:VD])

                def first_part():
                    pe.wait_ge(vtok_placed, n.times(1, 1))
                    parts[0]()

                job(c + 2, j + 2, DT, uh, ul, between={3: turn_values_and_score})
                job(c + 3, j + 3, DT, uh, ul,
                    between={3: first_part, 4: parts[1], 5: parts[2], 7: parts[3]})
                parts[4]()

            pe.wait_ge(tap_done, CT * (TAPS + 1))
            for t in range(CT):
                ins = pe.matmul(sc[0][:], ones[:], acc[:, t, :], start=t == 0, stop=t == CT - 1)
            ins.then_inc(mean_ready, 1)
            pe.wait_ge(out_copied, HEADS)
            for f in range(4):
                if f >= 2:
                    pe.wait_ge(o_low, f - 1)
                turn_tile(sc[1 + f % 2], lambda q: otok[:, q, f * P:(f + 1) * P]).then_inc(ot_ready, 1)
            c, j = phase("mla_out")
            for m in range(4):
                two_jobs(c + m, j + 2 * m, oh, ol, tiles_of(o_low, 0) if m == 0 else None)
                if m == 0:
                    sums("conv")
                if m == 1:
                    broadcast("conv")
            c, j = phase("conv_out")
            for m in range(4):
                two_jobs(c + m, j + 2 * m, yh, yl, tiles_of(y_low, 0) if m == 0 else None)

            c, j = phase("w_out")
            for m in range(DT):
                job(c + m, j + m, DT, uh, ul, before=tiles_of(m_low, 0) if m == 0 else None)
                if m == 0:
                    pe.wait_ge(mem_landed, 16)
                if m >= 3:
                    pe.wait_ge(mem_low, m - 2)
                turn_tile(sc[m % 3], lambda q: memtok[:, q, m * P:(m + 1) * P], 2).then_inc(mt_ready, 1)
                if m:
                    sum_squares("mem", m - 1)
            sum_squares("mem", DT - 1)

            def turn_values(hd):
                evacuated(pe, Idx(JOB0["xkv"] + XH + hd))
                wait(pe, xv_placed, hd)
                turn_tile(ob, lambda q: (qt, kt)[hd % 2][:, q * P:(q + 1) * P], 2).then_inc(xvt_ready, 1)

            c, j = phase("xkv")
            for m in range(8):
                job(c + m, j + m, DT, memh, meml, MEM, tiles_of(mem_low, 0) if m == 0 else None)
                if m == 0:
                    broadcast("mem")
                if 1 <= m <= 4:
                    sum_squares("xattn", 2 * m - 2)
                    sum_squares("xattn", 2 * m - 1)
                if m >= 5:
                    turn_values(m - 5)
            c, j = phase("xq")
            for m in range(XH):
                job(c + m, j + m, DT, xuh, xul, before=tiles_of(u_low, U0["xattn"]) if m == 0 else None)
                if m == 0:
                    turn_values(3)

            def x_scores(hd):
                evacuated(pe, Idx(JOB0["xq"] + hd))
                if hd >= 2:
                    pe.wait_ge(xo_low, hd - 1)
                for q in range(QT):
                    b = ((sc[0], sc[1]), (sc[2], ob))[hd % 2][q // 2]
                    ins = pe.matmul(b[:, (q % 2) * MEM:(q % 2 + 1) * MEM], xq[:, hd, q * P:(q + 1) * P], xk[:, hd, :],
                                    start=True, stop=True)
                    if q % 2:
                        ins.then_inc(xs_ready, 1)

            def x_finish(hd):
                for b in range(2):
                    pe.wait_ge(xp_scaled, 2 * hd + b + 1)
                    wait(pe, (xpt_act, xpt_dve)[b], hd)
                    for q in range(2):
                        for kb in range(2):
                            ins = pe.transpose(tr[b][:, kb * 256 + q * P:kb * 256 + (q + 1) * P],
                                               xp[:, hd % 2, 2 * b + q, kb * P:(kb + 1) * P], ident[:])
                    ins.then_inc(xpt_ready, 1)
                pe.wait_ge(xpt_act, hd + 1)
                pe.wait_ge(xpt_dve, hd + 1)
                for kb in range(2):
                    ins = pe.matmul(sc[2 * (hd % 2)][:], xv[:, kb, hd * XD:(hd + 1) * XD], xpt[:, hd % 2, kb, :],
                                    start=kb == 0, stop=kb == 1)
                ins.then_inc(xo_ready, 1)

            pe.wait_ge(xv_placed, XH)
            x_scores(0)
            for hd in range(XH):
                if hd + 1 < XH:
                    x_scores(hd + 1)
                x_finish(hd)
            c, j = phase("xo")
            for m in range(4):
                two_jobs(c + m, j + 2 * m, xoh, xol, tiles_of(xo_low, 0) if m == 0 else None)
                if m:
                    sum_squares("mlp", 2 * m - 2)
                    sum_squares("mlp", 2 * m - 1)

            c, j = phase("up0")
            for m in range(4):
                job(c + m, j + m, DT, uh, ul, before=tiles_of(u_low, U0["mlp"]) if m == 0 else None)
            sum_squares("mlp", 6)
            sum_squares("mlp", 7)
            for half in range(2):
                with pe.Fori(1 - half, 4) as i:
                    c, j = phase(f"up{half}", 4, 4, i)
                    for m in range(4):
                        job(c + m, j + m, DT, uh, ul)
                if half == 0:
                    broadcast("mlp")
                pe.wait_ge(f_low, 16 * half + 16)
                with pe.Fori(0, 4) as i:
                    c, j = phase(f"down{half}", 4, 2, i)
                    for m in range(2):
                        o = open_job(j + m)[:]
                        for b in range(2):
                            cc = c + (2 * m + b)
                            wait(pe, lo_made, (cc + 1).v())
                            for k in range(DT):
                                ins = products(o, cc.slot(4), k, 0, fh[:, DT * b + k, :], fl[:, DT * b + k, :],
                                               b == 0 and k == 0, b == 1 and k == DT - 1, P, k == 0)
                        ins.then_inc(lin_ready, 1)

            c, j = phase("av")
            job(c, j, DT, uh, ul, before=tiles_of(u_low, U0["raw"]))
            pe.wait_ge(hsq_added, 2 * DT)
            sum_added(sum_h, sum_x1)
            job(c + 1, j + 1, DT, uh, ul)
            broadcast("second")
            job(c + 2, j + 2, DT, uh, ul, between={3: lambda: broadcast("final")})
            job(c + 3, j + 3, DT, uh, ul)
            with pe.Fori(1, 2) as i:
                c, j = phase("av", 4, 4, i)
                for m in range(4):
                    job(c + m, j + m, DT, uh, ul)

            def pair(c, j, g, n0, n1):
                for m in range(1, 3):
                    job(c + m, j + m, DT, vh, vl)

                def first_scores():
                    evacuated(pe, j)
                    evacuated(pe, j + 1)
                    scores(n0, slice(0, 64))

                def turn_values():
                    pe.wait_ge(x1_made, DT)
                    evacuated(pe, j + 2)
                    turn_tile(tr[0], lambda q: td[:, q * P:(q + 1) * P]).then_inc(vtr_ready, 1)

                job(c + 3, j + 3, DT, vh, vl, between={2: first_scores, 5: turn_values})
                pe.wait_ge(vtok_placed, g.times(1, HEADS + 1))
                parts = finish(n0, lambda kb: vtok[:, kb, 0:64])
                job(c + 4, j + 4, DT, vh, vl, between={
                    1: parts[0], 2: parts[1], 4: parts[2], 5: parts[3], 6: parts[4],
                    7: lambda: scores(n1, slice(64, P))})
                pe.wait_ge(gv_made, g.times(1, 1))
                turn_tile(tr[1], lambda q: tc[:, q * P:(q + 1) * P]).then_inc(gvt_ready, 1)
                job(c + 5, j + 5, DT, vh, vl)
                pe.wait_ge(atok_placed, g.times(1, 1))
                parts = finish(n1, lambda kb: vtok[:, kb, 64:P])
                job(c + 6, j + 6, DT, vh, vl, between={
                    1: parts[0], 2: parts[1], 4: parts[2], 5: parts[3], 6: parts[4]})

                def turn_out_and_mixing():
                    pe.wait_ge(ws_masked, g.times(1, 1))
                    pe.wait_ge(out_copied, n1.times(1, 1))
                    pe.transpose(ob[:, 0:P], ws, ident[:]).then_inc(wst_ready, 1)
                    turn_tile(tr[0], lambda q: otp[:, q, :]).then_inc(ob_ready, 1)

                def mix():
                    pe.wait_ge(wst_placed, g.times(1, 1))
                    for q in range(QT):
                        ins = pe.matmul(tr[1][:, q * P:(q + 1) * P], atok[:, q, :], wst[:], start=True, stop=True)
                    ins.then_inc(mix_ready, 1)

                job(c + 7, j + 7, DT, vh, vl, between={2: turn_out_and_mixing, 5: mix})
                pe.wait_ge(mix_read, g.times(1, 1))
                pe.wait_ge(yb_made, g.times(1, 1))

            c, j = phase("pairs")
            job(c, j, DT, vh, vl, before=tiles_of(u_low, U0["second"]))
            pe.wait_ge(gsq_added, PAIRS)
            sum_added(sum_gate)
            with pe.Fori(0, PAIRS - 1) as i:
                c, j = phase("pairs", 8, 8, i)
                pair(c, j, Idx(0, 1, i), Idx(HEADS, 2, i), Idx(HEADS + 1, 2, i))
                job(c + 8, j + 8, DT, vh, vl)
            c, j = phase("pairs")
            g = PAIRS - 1
            pair(c + 8 * g, j + 8 * g, Idx(g), Idx(HEADS + 2 * g), Idx(HEADS + 1 + 2 * g))

            for name, hi, lo, ready, base in (("proj_a", vh, vl, ya_low, 0), ("proj_b", ybh, ybl, yb_low, 0),
                                              ("w_out2", vh, vl, m_low, DT)):
                c, j = phase(name)
                for m in range(DT):
                    job(c + m, j + m, DT, hi, lo, before=tiles_of(ready, base) if m == 0 else None)
                    if name == "w_out2" and m:
                        sum_squares("out", m - 1)
            sum_squares("out", DT - 1)
            broadcast("out")
            for f in range(DT):
                pe.wait_ge(fin_made, f + 1)
                if f >= 3:
                    pe.wait_ge(fin_copied, f - 2)
                turn_tile(sc[f % 3], lambda q: (tc, td)[f % 2][:, q * P:(q + 1) * P]).then_inc(fin_ready, 1)

        @block.scalar
        def _(act):
            act.dma_start(xtok[:], a["x"][0].rearrange("(q p) n -> p q n", p=P)).then_inc(x_landed, 16)
            for name, n in VECS:
                v = a[name] if len(a[name].shape) == 1 else a[name][0]
                act.dma_start(vrows[COL[name]:COL[name] + n, :], v.rearrange("(n p) -> n p", p=P))\
                    .then_inc(vecs_landed, 16)
            act.dma_start(crows[:], a["conv_w"][0]).then_inc(taps_landed, 16)
            act.dma_start(consts[:], a["shape_consts"]).then_inc(consts_landed, 16)
            act.dma_start(qt[64:128, :].bitcast(I32), a["positions"][0].partition_broadcast(64)).then_inc(pos_landed, 16)

            def split(c):
                if c.i is None and c.static >= NCHUNKS:
                    return
                size = chunk_size(c.static)
                v = 16 * (c.static // 2 + 1)
                act.wait_ge(raw_landed[c.slot(2)], v if c.i is None else v + (8 * c.per) * c.i)
                if size == 3 * P or c.static == CHUNK0["latent"] + 5:
                    v = 32 if size != 3 * P else 64 + 8 * (c.static - CHUNK0["heads"])
                    act.wait_ge(swapped_landed, v if c.i is None else v + (8 * c.per) * c.i)
                wait(act, chunk_entered, (c + -2).v())
                act.activation(wh[:, c.slot(4), 0:size], raw[:, c.slot(2), 0:size], ACT.Copy).then_inc(hi_made, 1)

            def read(j):
                act.wait_ge(lin_ready, (j + 1).v())
                return lin[j.slot(2)]

            def to(j, dst, func, rows=slice(0, P), n=S, **kw):
                act.activation(dst, read(j)[rows, 0:n], func, **kw).then_inc(lin_freed[j.slot(2)], 1)

            def square(name, f, src):
                s, n = SQ0[name] + f, NTOK.get(name, S)
                wait(act, sq_summed, s - 1)
                act.activation(SLOTS.get(name, (ta, tb))[s % 2][:, 0:n], src[:, 0:n], ACT.Square).then_inc(sq_made, 1)

            def norm_std(name):
                if NTILES[name]:
                    act.wait_ge(sq_summed, SQ0[name] + NTILES[name])
                wait(act, rstd_made, NORM_NO[name])
                n = NTOK.get(name, S) // P
                act.activation(std[:, 0:n], tr[1][:, 0:n], ACT.Sqrt, bias=eps4 if name == "gate_v" else eps,
                               scale=1.0 / WIDTH.get(name, D)).then_inc(std_made, 1)

            def norm_high(name, dst):
                for f in range(SPLIT_TILES[name]):
                    u = U0[name] + f
                    act.wait_ge(u_made, NORMED0[name] + f + 1)
                    act.activation(dst[:, f, :], (tc, td)[u % 2][:], ACT.Copy).then_inc(u_high, 1)

            def gain_high(dst, src, gain):
                act.activation(dst, src, ACT.Identity, scale=gain).then_inc(u_high, 1)

            def exps(n):
                for q in range(QT):
                    wait(act, logits_made, n.times(4, q + 1))
                    p = logit[:, LOFF[q]:LOFF[q] + KEYS[q]]
                    act.activation(p, p, ACT.Exp, bias=nmax[:, q:q + 1], scale=-1.0, accum_out=den[:, q:q + 1])\
                        .then_inc(probs_made, 1)

            def copy_turned(n, k):
                w = (384, 512)[k]
                wait(act, pt_ready, n.times(3, 1 + 2 * k))
                act.activation(pt[:, 0:w], tr[0][:, 0:w], ACT.Copy).then_inc(pt_act, 1)

            split(Idx(0))
            split(Idx(1))
            act.wait_ge(start_made, 2)
            for f in range(DT):
                act.wait_ge(xt_copied, f + 1)
                square("mix", f, h[:, f, :])
            norm_std("mix")
            norm_high("mix", uh)
            act.wait_ge(trig_arg, 1)
            act.activation(trig[64:128, :], kt[64:128, :], ACT.Sin).then_inc(trig_made, 1)

            c, j = phase("latent")
            for m in range(6):
                split(c + (m + 2))
                if m < 5:
                    name, f = ("q", m) if m < 3 else ("kv", m - 3)
                    square(name, f, read(j + m))
                    to(j + m, cq[:, m, :], ACT.Copy)
                if m == 3:
                    norm_std("q")
            norm_high("q", cqh)
            norm_std("kv")

            c, j = phase("conv")
            for m in range(8):
                split(c + (m + 2))
                if m % 2 == 0:
                    to(j + m, z[:, m // 2, PAD:PAD + S], ACT.Copy, scale=0.5)
                else:
                    wait(act, z_made, m // 2 - 1)
                    to(j + m, (logit[:, 512:1024], pt[:, 0:512])[(m // 2) % 2], ACT.Tanh, scale=0.5)
                if m == 2:
                    norm_high("kv", ckh)

            def head(c, j, n, g):
                split(c + 3)
                act.activation(kt[0:64, :], read(j + 1)[0:64, :], ACT.Copy)
                to(j + 1, td[64:128, :], ACT.Copy, rows=slice(64, 128))
                exps(n)
                to(j + 2, gates[:, g, :], ACT.Tanh, scale=0.5)
                split(c + 4)
                split(c + 5)
                copy_turned(n, 0)
                copy_turned(n, 1)
                split(c + 6)
                to(j + 3, gates[:, g + 1, :], ACT.Tanh, scale=0.5)

            split(phase("heads")[0] + 2)
            act.wait_ge(z_made, CT)
            with act.Fori(0, HEADS - 1) as i:
                head(*phase("heads", 4, 4, i), Idx(0, 1, i), 2 * i)
            c, j = phase("heads")
            head(c + 4 * (HEADS - 1), j + 4 * (HEADS - 1), Idx(HEADS - 1), 2 * (HEADS - 1))

            for t in range(CT):
                act.wait_ge(ot_ready, t + 1)
                act.activation(oh[:, t, :], sc[1 + t % 2][:], ACT.Copy).then_inc(o_high, 1)
            c, _ = phase("mla_out")
            for t in range(CT):
                act.wait_ge(centred, t + 1)
                square("conv", t, acc[:, t, :])
            split(c + 3)
            norm_std("conv")
            split(c + 4)
            for t in range(CT + 1):
                if t < CT:
                    act.wait_ge(y_norm, t + 1)
                    act.activation((qt, kt)[t % 2][:], (tc, td)[t % 2][:], ACT.Identity, bias=hb[:, t:t + 1], scale=0.5)\
                        .then_inc(y_half, 1)
                    act.wait_ge(y_half, t + 1)
                    act.activation((ta, tb)[t % 2][:], (qt, kt)[t % 2][:], ACT.Tanh).then_inc(y_tanh, 1)
                if t:
                    act.wait_ge(y_made, t)
                    act.activation(yh[:, t - 1, :], (tc, td)[(t - 1) % 2][:], ACT.Copy).then_inc(y_high, 1)
            split(c + 5)
            c, _ = phase("conv_out")
            for m in range(4):
                split(c + (m + 2))
                for f in (2 * m, 2 * m + 1):
                    act.wait_ge(m_made, f + 1)
                    act.activation(uh[:, f, :], (tc, td)[f % 2][:], ACT.Copy).then_inc(m_high, 1)

            c, j = phase("w_out")
            for m in range(DT):
                split(c + (m + 2))
                act.wait_ge(mt_ready, m + 1)
                square("mem", m, sc[m % 3])
                act.activation(memh[:, m, :], sc[m % 3][:, 0:MEM], ACT.Identity, scale=col("norm_mem_g", m))\
                    .then_inc(mem_high, 1)
                if m:
                    evacuated(act, j + (m - 1))
                    gain_high(xuh[:, m - 1, :], h[:, m - 1, :], col("norm_xattn_g", m - 1))
            evacuated(act, j + (DT - 1))
            gain_high(xuh[:, DT - 1, :], h[:, DT - 1, :], col("norm_xattn_g", DT - 1))
            norm_std("mem")
            c, j = phase("xkv")
            for m in range(8):
                split(c + (m + 2))
                if m < 4:
                    square("xattn", 2 * m, h[:, 2 * m, :])
                    square("xattn", 2 * m + 1, h[:, 2 * m + 1, :])
                else:
                    wait(act, xvt_ready, m - 5)
                    to(j + m, (qt, kt)[m % 2][:, 0:MEM], ACT.Copy, n=MEM)
            norm_std("xattn")
            c, j = phase("xq")
            for m in range(XH):
                split(c + (m + 2))
                to(j + m, xq[:, m, :], ACT.Copy, scale=CROSS_Q_SCALE)
            act.wait_ge(minus_made, 1)

            def x_exps(hd):
                for q in range(QT):
                    act.wait_ge(xmax_made, 2 * hd + q // 2 + 1)
                    b = ((sc[0], sc[1]), (sc[2], ob))[hd % 2][q // 2]
                    k = 4 * (hd % 2) + q
                    act.activation(xp[:, hd % 2, q, :], b[:, (q % 2) * MEM:(q % 2 + 1) * MEM], ACT.Exp,
                                   bias=xnmax[:, k:k + 1], scale=minus_rstd[:, q:q + 1], accum_out=xden[:, k:k + 1]).then_inc(xp_made, 1)

            x_exps(0)
            for hd in range(XH):
                if hd + 1 < XH:
                    x_exps(hd + 1)
                act.wait_ge(xpt_ready, 2 * hd + 1)
                act.activation(xpt[:, hd % 2, :, 0:256], tr[0][:].rearrange("p (k q) -> p k q", k=2), ACT.Copy)\
                    .then_inc(xpt_act, 1)
                act.wait_ge(xo_ready, hd + 1)
                act.activation(xoh[:, hd, :], sc[2 * (hd % 2)][:], ACT.Copy).then_inc(xo_high, 1)
            c, j = phase("xo")
            for m in range(4):
                split(c + (m + 2))
                for f in (2 * m, 2 * m + 1):
                    evacuated(act, j + f)
                    gain_high(uh[:, f, :], h[:, f, :], col("norm_mlp_g", f))
                    square("mlp", f, h[:, f, :])

            def up(half, trip):
                c, j = phase(f"up{half}", 4, 4, trip)
                f = Idx(16 * half, 4, trip)
                for m in range(4):
                    split(c + (m + 2))
                    to(j + m, (ta, tb)[m % 2][:], ACT.Relu)
                    act.wait_ge(f_sq, f.times(1, m + 1))
                    act.activation(fh[:, 4 * trip + m, :], (tc, td)[m % 2][:], ACT.Copy).then_inc(f_high, 1)

            with act.Fori(0, 1) as i:
                up(0, i)
            norm_std("mlp")
            for half in range(2):
                with act.Fori(1 - half, 4) as i:
                    up(half, i)
                with act.Fori(0, 4) as i:
                    c, _ = phase(f"down{half}", 4, 2, i)
                    for m in range(2):
                        split(c + (2 * m + 2))
                        split(c + (2 * m + 3))
                        if half == 1:
                            f = Idx(m, 2, i)
                            grown, added = now(act, f.times(1, DT + 1)), now(act, f.times(2))
                            act.wait_ge(start_made, 2)
                            act.wait_ge(h_added, grown)
                            act.wait_ge(hsq_added, added)
                            src = h[:, f.v(), :]
                            act.activation(uh[:, f.v(), :], src, ACT.Identity, scale=both[:, bass.ds(f.v(), 1)])\
                                .then_inc(u_high, 1)
                            act.activation(ta[:], src, ACT.Square).then_inc(hsq_made, 1)
                            act.activation(tb[:], src, ACT.Square, scale=cols[:, bass.ds(COL["final_norm_g"] + f.v(), 1)])\
                                .then_inc(hsq_made, 1)

            def gelu(j, k):
                act.activation(ta[:], read(j)[:], ACT.Square).then_inc(g_square, 1)
                act.wait_ge(g_poly, k)
                act.activation(ta[:], tb[:], ACT.Tanh, scale=GELU_C * GELU_A).then_inc(g_tanh, 1)

            c, j = phase("av")
            split(c + 2)
            act.wait_ge(added_summed, 1)
            norm_std("second")
            act.wait_ge(rstd_made, NORM_NO["second"] + 1)
            act.activation(std[:], final_sq[:], ACT.Sqrt, bias=eps).then_inc(std_made, 1)
            for m in range(PAIRS):
                if m:
                    split(c + (m + 2))
                evacuated(act, j + m)
                wait(act, gating_made, m)
                act.activation(ta[:], scaled, ACT.Square).then_inc(g_square, 1)
                act.wait_ge(g_poly, m + 1)
                act.activation(ta[:], tb[:], ACT.Tanh, scale=GELU_C * GELU_A).then_inc(g_tanh, 1)
                act.wait_ge(u_made, NORMED0["second"] + m + 1)
                act.activation(vh[:, m, :], (tc, td)[(U0["second"] + m) % 2][:], ACT.Copy).then_inc(u_high, 1)
                act.wait_ge(gating_made, m + 1)
                wait(act, gsq_added, m)
                act.activation(gate_sq, av[:, m, :], ACT.Square).then_inc(gsq_made, 1)
            act.wait_ge(added_summed, 2)
            norm_std("gate_v")

            with act.Fori(0, PAIRS) as i:
                c, j = phase("pairs", 8, 8, i)
                g, n0, n1 = Idx(0, 1, i), Idx(HEADS, 2, i), Idx(HEADS + 1, 2, i)
                split(c + 2)
                to(j, qt[:], ACT.Copy, scale=DILATED_Q_SCALE)
                split(c + 3)
                split(c + 4)
                to(j + 2, td[:], ACT.Copy)
                split(c + 5)
                exps(n0)
                act.wait_ge(ya_made, g.v())
                gelu(j + 3, g.times(1, PAIRS + 1))
                split(c + 6)
                copy_turned(n0, 0)
                copy_turned(n0, 1)
                evacuated(act, j + 3)
                act.activation(ta[:], read(j + 4)[:], ACT.Tanh, scale=0.5).then_inc(silu_tanh, 1)
                exps(n1)
                split(c + 7)
                evacuated(act, j + 4)
                act.activation(ta[:], read(j + 5)[:], ACT.Tanh, scale=0.5).then_inc(silu_tanh, 1)
                copy_turned(n1, 0)
                copy_turned(n1, 1)
                split(c + 8)
                act.wait_ge(gv_made, g.times(1, 1))
                to(j + 6, av[:, g.v(), :], ACT.Tanh, scale=0.5)
                act.wait_ge(wst_ready, g.times(1, 1))
                act.activation(wst[:], ob[:, 0:P], ACT.Copy).then_inc(wst_placed, 1)
                act.wait_ge(yb_made, g.times(1, 1))
                act.activation(ybh[:, g.v(), :], tc[:], ACT.Copy).then_inc(yb_high, 1)
                split(c + 9)
                to(j + 7, gb[:, g.v(), :], ACT.Tanh, scale=0.5)

            act.wait_ge(ya_made, PAIRS)
            act.wait_ge(lin_ready, JOB0["proj_a"])
            for f in range(DT):
                act.activation(vh[:, f, :], ya[:, f, :], ACT.Copy).then_inc(ya_high, 1)
            c, _ = phase("proj_a")
            for m in range(DT):
                split(c + (m + 2))
            c, _ = phase("proj_b")
            for m in range(DT):
                split(c + (m + 2))
                act.wait_ge(m_made, DT + m + 1)
                act.activation(vh[:, m, :], (tc, td)[m % 2][:], ACT.Copy).then_inc(m_high, 1)
            c, j = phase("w_out2")
            for m in range(DT):
                split(c + (m + 2))
                evacuated(act, j + m)
                square("out", m, h[:, m, :])
            norm_std("out")
            for f in range(DT):
                act.wait_ge(fin_ready, f + 1)
                act.activation(ya[:, f, :], sc[f % 3][:], ACT.Copy).then_inc(fin_copied, 1)

        @block.vector
        def _(dve):
            step = chain(dve, vector_steps)

            def lower(c):
                if c.i is None and c.static >= NCHUNKS:
                    return
                size = chunk_size(c.static)
                dve.wait_ge(hi_made, (c + 1).v())
                dve.tensor_tensor(wl[:, c.slot(4), 0:size], raw[:, c.slot(2), 0:size],
                                  wh[:, c.slot(4), 0:size].bitcast(F32), ALU.subtract).then_inc(lo_made, 1)

            def read(j):
                dve.wait_ge(lin_ready, (j + 1).v())
                return lin[j.slot(2)]

            def freed(ins, j):
                ins.then_inc(lin_freed[j.slot(2)], 1)

            def low(dst, whole, high, high_sem, k, low_sem):
                dve.wait_ge(high_sem, k)
                dve.tensor_tensor(dst, whole, high.bitcast(F32), ALU.subtract).then_inc(low_sem, 1)

            def norm_rstd(name, dst=rstd):
                k, n = NORM_NO[name], NTOK.get(name, S) // P
                dve.wait_ge(std_made, k + 1)
                dve.reciprocal(dst[:, 0:n], std[:, 0:n]).then_inc(rstd_made, 1)
                dve.wait_ge(rstd_made, k + 1)

            def diagonal(name, r_, squared=False):
                for q in range(NTOK.get(name, S) // P):
                    at = r_[:, q:q + 1]
                    ins = dve.tensor_scalar(te[:, q * P:(q + 1) * P], ident[:], at, at if squared else None, ALU.mult,
                                            *((ALU.mult,) if squared else ()))
                ins.then_inc(diag_made, 1)

            def norm_diag(name):
                norm_rstd(name)
                diagonal(name, rstd)

            def norm_apply(name, gain, src, hi, lo):
                n = SPLIT_TILES[name]
                dve.wait_ge(bc_ready, BC_NO[name] + 1)
                for f in range(n + 1):
                    u = U0[name] + f
                    if f < n:
                        wait(dve, u_low, u - 1)
                        dve.scalar_tensor_tensor((tc, td)[u % 2][:], src(f), col(gain, f), tr[0][:], ALU.mult, ALU.mult)\
                            .then_inc(u_made, 1)
                    if f:
                        dve.wait_ge(u_made, NORMED0[name] + f)
                        low(lo[:, f - 1, :], (tc, td)[(u - 1) % 2][:], hi[:, f - 1, :], u_high, u, u_low)

            def gain_low(dst, src, gain, high, k):
                dve.wait_ge(u_high, k)
                dve.scalar_tensor_tensor(dst, src, gain, high.bitcast(F32), ALU.mult, ALU.subtract).then_inc(u_low, 1)

            def maxima(n):
                for q in range(QT):
                    at = now(dve, n.times(3, SCORES_AT[q]))
                    dve.wait_ge(pool_made, 2)
                    wait(dve, scores_ready, at)
                    b, o = SBANK[q]
                    dve.tensor_tensor_reduce(logit[:, LOFF[q]:LOFF[q] + KEYS[q]], sc[b][:, o:o + KEYS[q]],
                                             bias[:, S - KEYS[q]:S], 1.0, 3e38, ALU.add, ALU.min,
                                             nmax[:, q:q + 1]).then_inc(logits_made, 1)

            def middle(n):
                wait(dve, probs_made, n.times(4, 4))
                wait(dve, out_copied, n.v())
                dve.reciprocal(rden, den).then_inc(rden_made, 1)
                wait(dve, pt_ready, n.times(3, 2))
                dve.tensor_copy(pt[:, 512:896], tr[1][:, 0:384]).then_inc(pt_dve, 1)

            def outputs(n, dst):
                wait(dve, rden_made, n.times(1, 1))
                wait(dve, out_ready, n.times(1, 1))
                dve.tensor_tensor(dst, ob[:, 0:QT * VD].rearrange("p (q d) -> p q d", q=QT),
                                  rden.unsqueeze(2).broadcast_to([P, QT, VD]), ALU.mult).then_inc(out_copied, 1)

            dve.memset(ones[:], 1.0).then_inc(start_made, 1)
            dve.memset(small[:, 0:1], EPS)
            dve.memset(small[:, 1:2], 4 * EPS).then_inc(start_made, 1)
            dve.memset(z[:, :, 0:PAD], 0.0).then_inc(start_made, 1)
            dve.memset(trig[0:64, :], 1.0).then_inc(start_made, 1)
            dve.memset(sel[:], 0.0).then_inc(start_made, 1)
            dve.wait_ge(start_made, 5)
            dve.wait_ge(pool_made, 1)
            for o in (64, 96):
                dve.tensor_tensor(sel[64:128, o:o + 32], ident[64:128, 64:96], ident[64:128, 96:128], ALU.add)\
                    .then_inc(start_made, 1)
            dve.wait_ge(vec_ready, 1)
            dve.tensor_copy(cols[:], tr[0][:, 0:NVEC]).then_inc(vec_copied, 1)
            dve.wait_ge(vec_ready, 2)
            dve.tensor_copy(taps[:].rearrange("p (t w) -> p t w", t=CT),
                            tr[1][:, 0:CT * 32].rearrange("p (t w) -> p t w", t=CT)[:, :, 0:TAPS])\
                .then_inc(vec_copied, 1)
            dve.wait_ge(vec_copied, 2)
            step(dve.tensor_tensor(both[:], cols[:, COL["final_norm_g"]:COL["final_norm_g"] + DT],
                                   cols[:, COL["g_norm_2"]:COL["g_norm_2"] + DT], ALU.mult))
            step(dve.tensor_scalar(hb, cols[:, COL["conv_ln_b"]:COL["conv_ln_b"] + CT], 0.5, None, ALU.mult))
            for f in range(DT):
                dve.wait_ge(xt_ready, f + 1)
                dve.tensor_copy(h[:, f, :], sc[f % 3][:]).then_inc(xt_copied, 1)
            lower(Idx(0))
            lower(Idx(1))
            norm_diag("mix")
            dve.wait_ge(xt_copied, DT)
            norm_apply("mix", "norm_mix_g", lambda f: h[:, f, :], uh, ul)

            r = slice(64, 128)
            dve.wait_ge(consts_landed, 16)
            dve.wait_ge(pos_landed, 16)
            ang, tmp = kt[r, :], logit[r, 0:S]
            freq, c_a, c_b, c_c = (consts[r, k:k + 1] for k in range(4))
            step(dve.tensor_copy(tmp, qt[r, :].bitcast(I32)))
            step(dve.tensor_scalar(ang, tmp, freq, None, ALU.mult))
            step(dve.tensor_scalar(tmp, ang, float(np.float32(1 / (2 * np.pi))), ROUND, ALU.mult, ALU.add))
            step(dve.tensor_scalar(tmp, tmp, -ROUND, None, ALU.add))
            for part in TWO_PI:
                step(dve.scalar_tensor_tensor(ang, tmp, -part, ang, ALU.mult, ALU.add))
            step(dve.tensor_scalar(ang, ang, 3.141592, -3.141592, ALU.min, ALU.max))
            step(dve.scalar_tensor_tensor(tmp, ang, -1.0, ang, ALU.mult, ALU.max))
            step(dve.tensor_scalar(tmp, tmp, c_b, c_c, ALU.mult, ALU.add))
            dve.scalar_tensor_tensor(ang, ang, c_a, tmp, ALU.mult, ALU.add).then_inc(trig_arg, 1)

            c, j = phase("latent")
            for m in range(6):
                lower(c + (m + 2))
                if m == 3:
                    norm_diag("q")
            for m in range(3):
                evacuated(dve, j + m)
            norm_apply("q", "q_norm_g", lambda f: cq[:, f, :], cqh, cql)
            dve.wait_ge(trig_made, 1)
            freed(dve.tensor_tensor(logit[:, 0:S], read(j + 5)[:], trig[:], ALU.mult), j + 5)
            c, j = phase("conv")
            lower(c + 2)
            dve.wait_ge(kr_ready, 1)
            dve.tensor_copy(kt[64:128, :], sc[0][64:128, :]).then_inc(kr_placed, 1)
            norm_diag("kv")
            for m in range(1, 8):
                if m == 2:
                    for k in (3, 4):
                        evacuated(dve, Idx(JOB0["latent"] + k))
                    norm_apply("kv", "kv_norm_g", lambda f: cq[:, 3 + f, :], ckh, ckl)
                lower(c + (m + 2))
                if m % 2:
                    t = m // 2
                    evacuated(dve, j + (m - 1))
                    evacuated(dve, j + m)
                    th = (logit[:, 512:1024], pt[:, 0:512])[t % 2]
                    zt = z[:, t, PAD:PAD + S]
                    dve.scalar_tensor_tensor(zt, th, 1.0, zt, ALU.add, ALU.mult).then_inc(z_made, 1)

            dve.wait_ge(z_made, CT)
            dve.wait_ge(pool_made, 2)

            def head(c, j, n, run):
                freed(dve.scalar_tensor_tensor(qt[:], read(j)[:], LINEAR_Q_SCALE, trig[:], ALU.mult, ALU.mult), j)
                lower(c + 3)
                run(0)
                wait(dve, vtr_ready, n.times(1, 1))
                dve.tensor_copy(vtok[:, :, 0:VD], ob[:, 256:512].rearrange("p (q d) -> p q d", q=QT))\
                    .then_inc(vtok_placed, 1)
                maxima(n)
                lower(c + 4)
                lower(c + 5)
                run(1)
                middle(n)
                run(2)
                at = n.times(VD)
                outputs(n, otok[:, :, at:at + VD] if n.i is None else otok[:, :, bass.ds(at, VD)])
                lower(c + 6)

            def two_heads(c, j, t, n):
                def tap(w):
                    zt, at = z[:, t, w % TAPS:w % TAPS + S], (acc[:, t, :], te[:])[w % 2]
                    k = (TAPS + 1) * t + w
                    tap_ = taps[:, bass.ds(TAPS * t + w % TAPS, 1)]
                    if w:
                        dve.wait_ge(tap_done, k - (w < TAPS))
                    if w == 0:
                        ins = dve.tensor_scalar(at, zt, tap_, cols[:, bass.ds(COL["conv_b"] + t, 1)], ALU.mult, ALU.add)
                    elif w == 1:
                        ins = dve.tensor_scalar(at, zt, tap_, None, ALU.mult)
                    elif w < TAPS:
                        ins = dve.scalar_tensor_tensor(at, zt, tap_, at, ALU.mult, ALU.add)
                    else:
                        ins = dve.tensor_tensor(acc[:, t, :], acc[:, t, :], te[:], ALU.add)
                    ins.then_inc(tap_done, 1)

                for p, cuts in ((0, (0, 6, 11, 16)), (1, (16, 22, 27, TAPS + 1))):
                    head(c + 4 * p, j + 4 * p, n + p, lambda k: [tap(w) for w in range(cuts[k], cuts[k + 1])])

            lower(phase("heads")[0] + 2)
            with dve.Fori(0, CT - 1) as i:
                two_heads(*phase("heads", 8, 8, i), i, Idx(0, 2, i))
            c, j = phase("heads")
            two_heads(c + 8 * (CT - 1), j + 8 * (CT - 1), CT - 1, Idx(2 * (CT - 1)))

            dve.wait_ge(mean_ready, 1)
            dve.wait_ge(tap_done, CT * (TAPS + 1))
            for t in range(CT):
                dve.scalar_tensor_tensor(acc[:, t, :], sc[0][:], -1.0 / CONV, acc[:, t, :], ALU.mult, ALU.add)\
                    .then_inc(centred, 1)
                low(ol[:, t, :], sc[1 + t % 2][:], oh[:, t, :], o_high, t + 1, o_low)
            c, j = phase("mla_out")

            def mla_out(f):
                g = gates[:, DT + f, :]
                freed(dve.scalar_tensor_tensor(g, g, 1.0, read(j + f)[:], ALU.add, ALU.mult), j + f)

            mla_out(0)
            lower(c + 3)
            lower(c + 4)
            mla_out(1)
            norm_diag("conv")
            dve.wait_ge(centred, CT)
            dve.wait_ge(bc_ready, BC_NO["conv"] + 1)
            for t in range(CT + 2):
                if t >= 2:
                    low(yl[:, t - 2, :], (tc, td)[t % 2][:], yh[:, t - 2, :], y_high, t - 1, y_low)
                if t < CT:
                    wait(dve, y_low, t - 1)
                    dve.scalar_tensor_tensor((tc, td)[t % 2][:], acc[:, t, :], col("conv_ln_g", t), tr[0][:],
                                             ALU.mult, ALU.mult).then_inc(y_norm, 1)
                    if t % 2 == 0:
                        mla_out(2 + t // 2)
                if 1 <= t <= CT:
                    dve.wait_ge(y_tanh, t)
                    dve.scalar_tensor_tensor((tc, td)[(t - 1) % 2][:], (ta, tb)[(t - 1) % 2][:], 1.0,
                                             (qt, kt)[(t - 1) % 2][:], ALU.add, ALU.mult).then_inc(y_made, 1)
            mla_out(4)
            mla_out(5)
            lower(c + 5)
            mla_out(6)
            mla_out(7)

            def merge(f, j, mine, other, base, hi=uh, lo=ul):
                freed(dve.scalar_tensor_tensor(mine[:, f, :], mine[:, f, :], 1.0, read(j)[:], ALU.add, ALU.mult), j)
                evacuated(dve, j)
                wait(dve, m_low, base + f - 1)
                dve.tensor_tensor((tc, td)[f % 2][:], mine[:, f, :], other[:, f, :], ALU.add).then_inc(m_made, 1)
                if f:
                    merge_low(f - 1, base, hi, lo)

            def merge_low(f, base, hi=uh, lo=ul):
                low(lo[:, f, :], (tc, td)[f % 2][:], hi[:, f, :], m_high, base + f + 1, m_low)

            def add_to_h(f, j, scale=None):
                at = h[:, f, :]
                if scale is None:
                    freed(dve.tensor_tensor(at, read(j)[:], at, ALU.add), j)
                else:
                    freed(dve.scalar_tensor_tensor(at, read(j)[:], scale, at, ALU.mult, ALU.add), j)

            c, j = phase("conv_out")
            for m in range(4):
                lower(c + (m + 2))
                for f in (2 * m, 2 * m + 1):
                    merge(f, j + f, gates, gates[:, DT:2 * DT, :], 0)
            merge_low(DT - 1, 0)

            c, j = phase("w_out")
            for m in range(DT):
                lower(c + (m + 2))
                dve.wait_ge(mem_high, m + 1)
                dve.scalar_tensor_tensor(meml[:, m, :], sc[m % 3][:, 0:MEM], col("norm_mem_g", m),
                                         memh[:, m, :].bitcast(F32), ALU.mult, ALU.subtract).then_inc(mem_low, 1)
                if m:
                    evacuated(dve, j + (m - 1))
                    gain_low(xul[:, m - 1, :], h[:, m - 1, :], col("norm_xattn_g", m - 1), xuh[:, m - 1, :],
                             U0["xattn"] + m)
                add_to_h(m, j + m, 0.5)
            evacuated(dve, j + (DT - 1))
            gain_low(xul[:, DT - 1, :], h[:, DT - 1, :], col("norm_xattn_g", DT - 1), xuh[:, DT - 1, :],
                     U0["xattn"] + DT)
            norm_rstd("mem", mem_rstd)
            diagonal("mem", mem_rstd)
            c, j = phase("xkv")

            def place_values(hd):
                dve.wait_ge(xvt_ready, hd + 1)
                dve.tensor_tensor(xv[:, :, hd * XD:(hd + 1) * XD], ob[:, 0:256].rearrange("p (q d) -> p q d", q=2),
                                  mem_rstd.unsqueeze(2).broadcast_to([P, 2, XD]), ALU.mult).then_inc(xv_placed, 1)

            for m in range(8):
                lower(c + (m + 2))
                if m == 0:
                    dve.wait_ge(bc_ready, BC_NO["mem"] + 1)
                    dve.tensor_copy(mem_scale, tr[0][:, 0:MEM]).then_inc(mem_scaled, 1)
                    dve.wait_ge(mem_scaled, 1)
                if m < XH:
                    freed(dve.tensor_tensor(xk[:, m, :], read(j + m)[:, 0:MEM], mem_scale, ALU.mult), j + m)
                if m >= 6:
                    place_values(m - 6)
            norm_rstd("xattn")
            dve.tensor_scalar(minus_rstd, rstd, -1.0, None, ALU.mult).then_inc(minus_made, 1)
            c, _ = phase("xq")
            for m in range(XH):
                lower(c + (m + 2))
                if m < 2:
                    place_values(m + 2)

            def x_maxima(hd):
                for b in range(2):
                    dve.wait_ge(xs_ready, 2 * hd + b + 1)
                    s_, k = ((sc[0], sc[1]), (sc[2], ob))[hd % 2][b], 4 * (hd % 2) + 2 * b
                    dve.tensor_reduce(xnmax[:, k:k + 2], s_[:].rearrange("p (q k) -> p q k", q=2), AX_X, ALU.min)\
                        .then_inc(xmin_made, 1)
                    dve.wait_ge(xmin_made, 2 * hd + b + 1)
                    dve.tensor_tensor(xnmax[:, k:k + 2], xnmax[:, k:k + 2], rstd[:, 2 * b:2 * b + 2], ALU.mult)\
                        .then_inc(xmax_made, 1)

            x_maxima(0)
            for hd in range(XH):
                if hd + 1 < XH:
                    x_maxima(hd + 1)
                for b in range(2):
                    k = 4 * (hd % 2) + 2 * b
                    dve.wait_ge(xp_made, 4 * hd + 2 * b + 2)
                    dve.reciprocal(xrden[:, k:k + 2], xden[:, k:k + 2]).then_inc(xrden_made, 1)
                    dve.wait_ge(xrden_made, 2 * hd + b + 1)
                    p_ = xp[:, hd % 2, 2 * b:2 * b + 2, :]
                    dve.tensor_tensor(p_, p_, xrden[:, k:k + 2].unsqueeze(2).broadcast_to([P, 2, MEM]), ALU.mult)\
                        .then_inc(xp_scaled, 1)
                dve.wait_ge(xpt_ready, 2 * hd + 2)
                dve.tensor_copy(xpt[:, hd % 2, :, 256:512], tr[1][:].rearrange("p (k q) -> p k q", k=2))\
                    .then_inc(xpt_dve, 1)
                dve.wait_ge(xo_ready, hd + 1)
                low(xol[:, hd, :], sc[2 * (hd % 2)][:], xoh[:, hd, :], xo_high, hd + 1, xo_low)
            c, j = phase("xo")
            for m in range(4):
                lower(c + (m + 2))
                for f in (2 * m, 2 * m + 1):
                    add_to_h(f, j + f)
                    evacuated(dve, j + f)
                    gain_low(ul[:, f, :], h[:, f, :], col("norm_mlp_g", f), uh[:, f, :], U0["mlp"] + f + 1)

            def up(half, trip):
                c, j = phase(f"up{half}", 4, 4, trip)
                f = Idx(16 * half, 4, trip)
                for m in range(4):
                    lower(c + (m + 2))
                    evacuated(dve, j + m)
                    r_ = (ta, tb)[m % 2][:]
                    dve.wait_ge(f_low, f.times(1, m))
                    dve.tensor_tensor((tc, td)[m % 2][:], r_, r_, ALU.mult).then_inc(f_sq, 1)
                    low(fl[:, 4 * trip + m, :], (tc, td)[m % 2][:], fh[:, 4 * trip + m, :], f_high,
                        f.times(1, m + 1), f_low)

            with dve.Fori(0, 1) as i:
                up(0, i)
            norm_rstd("mlp")
            diagonal("mlp", rstd, squared=True)
            for half in range(2):
                with dve.Fori(1 - half, 4) as i:
                    up(half, i)
                if half == 0:
                    dve.wait_ge(bc_ready, BC_NO["mlp"] + 1)
                    dve.tensor_copy(mlp_scale, tr[0][:]).then_inc(mlp_scaled, 1)
                    dve.wait_ge(mlp_scaled, 1)
                with dve.Fori(0, 4) as i:
                    c, j = phase(f"down{half}", 4, 2, i)
                    for m in range(2):
                        lower(c + (2 * m + 2))
                        lower(c + (2 * m + 3))
                        f, part = Idx(m, 2, i), (tc, td)[m]
                        freed(dve.tensor_tensor(part[:], read(j + m)[:], mlp_scale, ALU.mult), j + m)
                        evacuated(dve, j + m)
                        at = h[:, f.v(), :]
                        dve.tensor_tensor(at, part[:], at, ALU.add).then_inc(h_added, 1)
                        if half == 1:
                            dve.wait_ge(u_high, f.times(1, U0["raw"] + 1))
                            dve.scalar_tensor_tensor(ul[:, f.v(), :], at, both[:, bass.ds(f.v(), 1)],
                                                     uh[:, f.v(), :].bitcast(F32), ALU.mult, ALU.subtract)\
                                .then_inc(u_low, 1)
                if half == 0:
                    dve.wait_ge(pool_made, 3)
                    dint = atok[:].rearrange("p a b -> p (a b)").bitcast(I32)
                    tint = rbc[:].bitcast(I32)
                    step(dve.tensor_scalar(tint, dint, 3, None, ALU.bitwise_and))
                    step(dve.tensor_scalar(nlog[:], tint, 0.0, None, ALU.is_equal))
                    step(dve.tensor_scalar(tint, dint, 15, None, ALU.bitwise_and))
                    step(dve.tensor_scalar(bias[:], tint, 0.0, None, ALU.is_equal))
                    step(dve.tensor_tensor(nlog[:], nlog[:], bias[:], ALU.add))
                    step(dve.tensor_scalar(bias[:], dist[:], 128.0, None, ALU.is_le))
                    step(dve.tensor_tensor(nlog[:], nlog[:], bias[:], ALU.add))
                    step(dve.tensor_scalar(rbc[:], nlog[:], 2.0, -float(np.log(2.0)), ALU.is_equal, ALU.mult))
                    step(dve.tensor_scalar(bias[:], nlog[:], 3.0, -float(np.log(3.0)), ALU.is_equal, ALU.mult))
                    step(dve.tensor_tensor(rbc[:], rbc[:], bias[:], ALU.add))
                    step(dve.tensor_scalar(bias[:], nlog[:], 0.0, BIG, ALU.is_equal, ALU.mult))
                    dve.tensor_tensor(nlog[:], rbc[:], bias[:], ALU.add).then_inc(table_made, 1)

            c, j = phase("av")
            lower(c + 2)
            k = NORM_NO["second"]
            dve.wait_ge(std_made, k + 1)
            step(dve.reciprocal(final_rstd, std))
            step(dve.scalar_tensor_tensor(final_sq, tr[1][:, 4:8], 1.0 / D, final_rstd, ALU.mult, ALU.mult))
            dve.tensor_tensor(final_sq, final_sq, final_rstd, ALU.mult).then_inc(rstd_made, 1)
            norm_rstd("final")
            step(dve.tensor_tensor(rstd, rstd, final_rstd, ALU.mult))
            diagonal("second", rstd)
            dve.wait_ge(bc_ready, BC_NO["second"] + 1)
            dve.tensor_copy(rbc[:], tr[0][:]).then_inc(rbc_made, 1)
            dve.wait_ge(rbc_made, 1)
            diagonal("final", final_rstd)

            def gelu(j, k, dst):
                dve.wait_ge(g_square, k)
                dve.scalar_tensor_tensor(tb[:], ta[:], 1.0 / GELU_A, read(j)[:], ALU.add, ALU.mult).then_inc(g_poly, 1)
                dve.wait_ge(g_tanh, k)
                freed(dve.scalar_tensor_tensor(dst, ta[:], 1.0, read(j)[:], ALU.add, ALU.mult), j)

            def first_output(m):
                dve.wait_ge(bc_ready, BC_NO["final"] + 1)
                dve.scalar_tensor_tensor(h[:, m, :], h[:, m, :], col("final_norm_g", m), tr[0][:], ALU.mult,
                                         ALU.mult).then_inc(x1_made, 1)

            for m in range(PAIRS):
                if m:
                    lower(c + (m + 2))
                freed(dve.tensor_tensor(scaled, read(j + m)[:], rbc[:], ALU.mult), j + m)
                evacuated(dve, j + m)
                u = U0["second"] + m
                wait(dve, u_low, u - 1)
                dve.scalar_tensor_tensor((tc, td)[u % 2][:], h[:, m, :], both[:, m:m + 1], rbc[:], ALU.mult, ALU.mult)\
                    .then_inc(u_made, 1)
                dve.wait_ge(g_square, m + 1)
                dve.scalar_tensor_tensor(tb[:], ta[:], 1.0 / GELU_A, scaled, ALU.add, ALU.mult).then_inc(g_poly, 1)
                dve.wait_ge(u_made, NORMED0["second"] + m + 1)
                low(vl[:, m, :], (tc, td)[u % 2][:], vh[:, m, :], u_high, u + 1, u_low)
                dve.wait_ge(g_tanh, m + 1)
                dve.scalar_tensor_tensor(av[:, m, :], ta[:], 1.0, scaled, ALU.add, ALU.mult).then_inc(gating_made, 1)
                dve.wait_ge(gating_made, m + 1)
                if m:
                    first_output(m - 1)
            first_output(PAIRS - 1)
            dve.wait_ge(pool_made, 4)

            def mask(n, k):
                dve.wait_ge(logits_made, n.times(4))
                dve.scalar_tensor_tensor(bias[:], dist[:], consts[:, bass.ds(4 + k, 1)], nlog[:], ALU.mult, ALU.add)\
                    .then_inc(bias_made, 1)
                dve.wait_ge(bias_made, (n + (1 - HEADS)).v())

            norm_rstd("gate_v")
            with dve.Fori(0, PAIRS) as i:
                c, j = phase("pairs", 8, 8, i)
                g, n0, n1 = Idx(0, 1, i), Idx(HEADS, 2, i), Idx(HEADS + 1, 2, i)
                lower(c + 2)
                lower(c + 3)
                freed(dve.tensor_copy(kt[:], read(j + 1)[:]), j + 1)
                lower(c + 4)
                dve.wait_ge(yb_low, g.v())
                dve.tensor_scalar(tc[:], av[:, i, :], cols[:, bass.ds(COL["g_v_2"] + i, 1)], None, ALU.mult)\
                    .then_inc(gv_made, 1)
                mask(n0, 2 * i)
                lower(c + 5)
                maxima(n0)
                dve.wait_ge(vtr_ready, g.times(1, HEADS + 1))
                dve.tensor_copy(vtok[:].rearrange("p q d -> p (q d)"), tr[0][:]).then_inc(vtok_placed, 1)
                gelu(j + 3, g.times(1, PAIRS + 1), tb[:])
                mask(n1, 2 * i + 1)
                middle(n0)
                outputs(n0, otp[:, :, 0:VD])
                lower(c + 6)
                maxima(n1)
                dve.wait_ge(silu_tanh, g.times(2, 1))
                freed(dve.scalar_tensor_tensor(te[:], ta[:], 1.0, read(j + 4)[:], ALU.add, ALU.mult), j + 4)
                evacuated(dve, j + 4)
                evacuated(dve, j + 3)
                dve.scalar_tensor_tensor(tb[:], tb[:], 0.25, te[:], ALU.mult, ALU.mult).then_inc(gate_prod, 1)
                dve.wait_ge(gvt_ready, g.times(1, 1))
                dve.tensor_tensor(atok[:], tr[1][:].rearrange("p (q d) -> p q d", q=QT),
                                  rstd.unsqueeze(2).broadcast_to([P, QT, P]), ALU.mult).then_inc(atok_placed, 1)
                lower(c + 7)
                dve.wait_ge(gate_prod, g.times(1, 1))
                dve.wait_ge(silu_tanh, g.times(2, 2))
                freed(dve.scalar_tensor_tensor(te[:], ta[:], 1.0, read(j + 5)[:], ALU.add, ALU.mult), j + 5)
                middle(n1)
                outputs(n1, otp[:, :, VD:P])
                lower(c + 8)
                dve.wait_ge(ob_ready, g.times(1, 1))
                evacuated(dve, j + 5)
                dve.scalar_tensor_tensor(tc[:], tr[0][:], 0.5, te[:], ALU.mult, ALU.mult).then_inc(yb_made, 1)
                dve.wait_ge(mix_ready, g.times(1, 1))
                dve.tensor_tensor(ta[:].rearrange("p (q t) -> p q t", q=QT), tr[1][:].rearrange("p (q t) -> p q t", q=QT),
                                  bsb.unsqueeze(1).broadcast_to([P, QT, P]), ALU.add).then_inc(mix_read, 1)
                dve.wait_ge(mix_read, g.times(1, 1))
                dve.wait_ge(gate_prod, g.times(1, 1))
                dve.tensor_tensor(ya[:, i, :], ta[:], tb[:], ALU.mult).then_inc(ya_made, 1)
                low(ybl[:, i, :], tc[:], ybh[:, i, :], yb_high, g.times(1, 1), yb_low)
                lower(c + 9)

            c, j = phase("proj_a")
            for f in range(DT):
                low(vl[:, f, :], ya[:, f, :], vh[:, f, :], ya_high, f + 1, ya_low)
            for m in range(DT):
                lower(c + (m + 2))
                at = av[:, m, :]
                freed(dve.scalar_tensor_tensor(at, at, 1.0, read(j + m)[:], ALU.add, ALU.mult), j + m)
            evacuated(dve, j + (DT - 1))
            c, j = phase("proj_b")
            for m in range(DT):
                lower(c + (m + 2))
                merge(m, j + m, gb, av, DT, vh, vl)
            merge_low(DT - 1, DT, vh, vl)
            c, j = phase("w_out2")
            for m in range(DT):
                lower(c + (m + 2))
                add_to_h(m, j + m, 0.5)
            norm_diag("out")
            dve.wait_ge(bc_ready, BC_NO["out"] + 1)
            for f in range(DT):
                wait(dve, fin_ready, f - 1)
                dve.scalar_tensor_tensor((tc, td)[f % 2][:], h[:, f, :], col("g_final_2", f), tr[0][:], ALU.mult,
                                         ALU.mult).then_inc(fin_made, 1)


USED = ["x", "mem", "positions", "norm_mix_g", "w_in", "conv_w", "conv_b", "conv_ln_g", "conv_ln_b", "w_conv_out",
        "q_norm_g", "w_uq", "kv_norm_g", "w_ukv", "w_mla_out", "w_out", "norm_xattn_g", "norm_mem_g", "w_xq", "w_xkv",
        "w_xo", "norm_mlp_g", "w_mlp1", "w_mlp2", "final_norm_g", "g_norm_2", "w_in_2", "w_s_2", "b_s_2", "g_v_2",
        "w_proj_a_2", "w_proj_b_2", "w_out_2", "g_final_2"]


def shape_consts():
    c = np.zeros((P, NCONST), np.float32)
    half = ROPE // 2
    freq = np.float32(10000.0) ** (-np.arange(half, dtype=np.float32) / np.float32(half))
    c[64:, 0] = np.tile(freq, 4)
    c[64:96, 2], c[64:96, 3] = -1.0, np.float32(np.pi / 2)
    c[96:112, 1], c[112:, 1] = -1.0, 1.0
    c[:, 4:] = np.float32(2.0) ** (np.float32(-0.5) * np.arange(1, 17, dtype=np.float32))
    return c


def kernel(**inputs):
    import concourse.bacc as bacc
    from concourse.bass_utils import run_bass_kernel_spmd

    nc = bacc.Bacc("TRN2", target_bir_lowering=False, num_devices=1)
    arrays = {f"in_{n}_dram": np.ascontiguousarray(inputs[n]) for n in USED}
    arrays["in_shape_consts_dram"] = shape_consts()
    aps = {}
    for name, v in arrays.items():
        aps[name[3:-5]] = nc.dram_tensor(name, v.shape, mybir.dt.from_np(v.dtype), kind="ExternalInput").ap()
    out = nc.dram_tensor("out_0_dram", (1, S, D), F32, kind="ExternalOutput").ap()
    build(nc, aps, out)
    r = run_bass_kernel_spmd(nc, [arrays], core_ids=[0])
    return r.results[0]["out_0_dram"]
```

```python
from contextlib import ExitStack

import numpy as np

import concourse.bass as bass
from concourse import mybir

F32 = mybir.dt.float32
F32R = mybir.dt.float32r
I32 = mybir.dt.int32
ALU = mybir.AluOpType
ACT = mybir.ActivationFunctionType
AX_X = mybir.AxisListType.X

P = 128
S = 512
D = 1024
DT = D // P
QT = S // P
MEM = 256
CONV = 512
CT = CONV // P
TAPS = 31
PAD = TAPS - 1
HEADS = 8
NOPE, ROPE, VD = 64, 32, 64
QLORA, KVLORA = 384, 256
XH, XD = 4, 128
FF = 4096
EPS = 1e-6
BIG = 1e30
PAIRS = 8
GELU_A = 0.044715
GELU_C = 0.7978845608028654
LINEAR_Q_SCALE = -float((NOPE + ROPE) ** -0.5)
CROSS_Q_SCALE = -float(XD ** -0.5)
DILATED_Q_SCALE = -0.125

VECS = [("norm_mix_g", 8), ("conv_b", 4), ("conv_ln_g", 4), ("conv_ln_b", 4), ("q_norm_g", 3), ("kv_norm_g", 2),
        ("norm_xattn_g", 8), ("norm_mem_g", 8), ("norm_mlp_g", 8), ("final_norm_g", 8), ("g_norm_2", 8),
        ("g_v_2", 8), ("g_final_2", 8)]
COL, NVEC = {}, 0
for _name, _n in VECS:
    COL[_name] = NVEC
    NVEC += _n

PHASES = [("latent", 6, 6), ("conv", 8, 8), ("heads", 32, 32), ("mla_out", 4, 8), ("conv_out", 4, 8),
          ("w_out", 8, 8), ("xkv", 8, 8), ("xq", 4, 4), ("xo", 4, 8), ("up0", 16, 16), ("down0", 16, 8), ("up1", 16, 16),
          ("down1", 16, 8), ("av", 8, 8), ("pairs", 64, 64), ("proj_b", 8, 8), ("proj_a", 8, 8), ("w_out2", 8, 8)]
CHUNK0, JOB0, NCHUNKS, NJOBS = {}, {}, 0, 0
for _name, _c, _j in PHASES:
    CHUNK0[_name], JOB0[_name] = NCHUNKS, NJOBS
    NCHUNKS += _c
    NJOBS += _j

NORMS = [("mix", 0), ("q", 3), ("kv", 2), ("conv", 4), ("mem", 8), ("xattn", 8), ("mlp", 8), ("second", 0),
         ("final", 0), ("gate_v", 0), ("out", 8)]
ADDED = ["mem", "xattn", "mlp", "out"]
NORM_NO = {n: k for k, (n, _) in enumerate(NORMS)}
BROADCAST = ["q", "kv", "conv", "mem", "mlp", "second", "final"]
BC_NO = {n: k for k, n in enumerate(BROADCAST)}
SQ0, SUMMED, _t, _s = {}, {}, 0, 0
for _name, _n in NORMS:
    SQ0[_name] = _t
    _t, _s = _t + _n, _s + (1 if _name in ADDED else _n)
    SUMMED[_name] = _s
ADD0 = {n: 7 * k for k, n in enumerate(ADDED)}
SPLITS = [("mix", 8, 0), ("q", 3, 1), ("kv", 2, 1), ("xattn", 8, 0), ("mlp", 8, 0), ("raw", 8, 0),
          ("second", 8, 1)]
U0, NORMED0, _t, _m = {}, {}, 0, 0
for _name, _n, _normed in SPLITS:
    U0[_name], NORMED0[_name] = _t, _m
    _t, _m = _t + _n, _m + _n * _normed


NORMED_IN = ((0,), (1,), (2,), (3,), (4,), (5, 6), (7,), ())
COUNTS = {n: (c, j) for n, c, j in PHASES}
NCONST = 4 + 16
SEL_MADE = 7
ROUND = 1.5 * 2.0 ** 23
TWO_PI = (6.28125, 0.00193500518798828125, 2 * np.pi - 6.28125 - 0.00193500518798828125)
TWO_PI = tuple(float(v) for v in TWO_PI)


def chunk_size(c):
    k = c - CHUNK0["heads"]
    return 1024 if not 0 <= k < COUNTS["heads"][0] else (3 * P, 2 * P, 1024, 1024)[k % 4]


class Idx:

    def __init__(self, static, per=0, i=None):
        self.static, self.per, self.i = static, per, i

    def __add__(self, k):
        return Idx(self.static + k, self.per, self.i)

    def times(self, m, k=0):
        v = self.static * m + k
        return v if self.i is None else v + (self.per * m) * self.i

    def v(self):
        return self.times(1)

    def half(self):
        assert self.per % 2 == 0
        return self.static // 2 if self.i is None else self.static // 2 + (self.per // 2) * self.i

    def slot(self, m):
        assert self.per % m == 0
        return self.static % m


def build(nc, a, out):
    ctx = ExitStack()
    with ctx:
        def sem(name):
            return ctx.enter_context(nc.semaphore(name))

        def sb(name, shape, dt=F32, stack=ctx):
            return stack.enter_context(nc.sbuf_tensor(name, shape, dt))

        def bank(name):
            return ctx.enter_context(nc.psum_tensor(name, [P, 512], F32))

        lin = [bank("lin0"), bank("lin1")]
        sc = [bank("sc0"), bank("sc1"), bank("sc2")]
        tr = [bank("tr0"), bank("tr1")]
        ob = bank("ob")

        h = sb("h", [P, DT, S])
        uh = sb("uh", [P, DT, S], F32R)
        ul = sb("ul", [P, DT, S], F32R)
        raw = sb("raw", [P, 2, 1024])
        wh = sb("wh", [P, 4, 1024], F32R)
        wl = sb("wl", [P, 4, 1024], F32R)
        ident = sb("ident", [P, P])
        ones = sb("ones", [P, P])
        cols = sb("cols", [P, NVEC])
        both = sb("both", [P, DT])
        taps = sb("taps", [P, CT * TAPS])
        consts = sb("consts", [P, NCONST])
        small = sb("small", [P, 80])
        logit = sb("logit", [P, 1280])
        pt = sb("pt", [P, 896])
        qt = sb("qt", [P, S])
        kt = sb("kt", [P, S])
        vtok = sb("vtok", [P, QT, P])
        ta, tb, tc, td, te = (sb(n, [P, S]) for n in ("ta", "tb", "tc", "td", "te"))
        bias = sb("bias", [P, S])
        wst = sb("wst", [P, P])
        sel = wst
        trig = sb("trig", [P, S])
        dist = trig

        eps, eps4 = small[:, 0:1], small[:, 1:2]
        std, rstd = small[:, 4:8], small[:, 8:12]
        nmax = small[:, 12:16]
        den, rden = small[:, 16:20], small[:, 20:24]
        x_sq = small[:, 76:80]
        hb = small[:, 24:28]
        xnmax, xden, xrden = small[:, 32:40], small[:, 40:48], small[:, 48:56]
        mem_rstd = small[:, 56:58]
        minus_rstd = small[:, 60:64]
        final_rstd, final_sq = small[:, 28:32], small[:, 60:64]

        st = ExitStack()
        gates = sb("gates", [P, 16, S], stack=st)
        acc = sb("acc", [P, CT, S], stack=st)
        otok = sb("otok", [P, QT, S], stack=st)
        s2 = ExitStack()
        cqh = sb("cqh", [P, 3, S], F32R, s2)
        cql = sb("cql", [P, 3, S], F32R, s2)
        ckh = sb("ckh", [P, 2, S], F32R, s2)
        ckl = sb("ckl", [P, 2, S], F32R, s2)
        z = sb("z", [P, CT, S + PAD], stack=s2)
        s2.close()
        yh = sb("yh", [P, CT, S], F32R, st)
        yl = sb("yl", [P, CT, S], F32R, st)
        oh = sb("oh", [P, 4, S], F32R, st)
        ol = sb("ol", [P, 4, S], F32R, st)
        st.close()
        st = ExitStack()
        xtok = sb("xtok", [P, QT, D], stack=st)
        vrows = sb("vrows", [P, P], stack=st)
        crows = sb("crows", [TAPS, CONV], stack=st)
        st.close()
        st = ExitStack()
        xq = sb("xq", [P, XH, S], stack=st)
        xuh = sb("xuh", [P, DT, S], F32R, st)
        xul = sb("xul", [P, DT, S], F32R, st)
        s2 = ExitStack()
        memtok = sb("memtok", [P, 2, D], stack=s2)
        memh = sb("memh", [P, DT, MEM], F32R, s2)
        meml = sb("meml", [P, DT, MEM], F32R, s2)
        s2.close()
        xp = sb("xp", [P, 2, QT, MEM], stack=st)
        xpt = sb("xpt", [P, 2, 2, S], stack=st)
        xoh = sb("xoh", [P, XH, S], F32R, st)
        xol = sb("xol", [P, XH, S], F32R, st)
        xk = sb("xk", [P, XH, MEM], stack=st)
        xv = sb("xv", [P, 2, XH * XD], stack=st)
        st.close()
        st = ExitStack()
        fh = sb("fh", [P, 16, S], F32R, st)
        fl = sb("fl", [P, 16, S], F32R, st)
        st.close()
        st = ExitStack()
        av = sb("av", [P, PAIRS, S], stack=st)
        gb = sb("gb", [P, PAIRS, S], stack=st)
        ya = sb("ya", [P, PAIRS, S], stack=st)
        vh = sb("vh", [P, DT, S], F32R, st)
        vl = sb("vl", [P, DT, S], F32R, st)
        ybh, ybl = uh, ul
        otp = sb("otp", [P, QT, P], stack=st)
        rbc = sb("rbc", [P, S], stack=st)
        nlog = sb("nlog", [P, S], stack=st)
        atok = sb("atok", [P, QT, P], stack=st)
        st.close()
        cq = gates[:, 11:16, :]
        ws, bsb = ya[:, PAIRS - 1, 0:P], ya[:, PAIRS - 1, P:2 * P]

        mlp_scale = logit[:, 0:S]
        mem_scale = td[:, 0:MEM]
        fin = ya[:].rearrange("p f s -> p (f s)").rearrange("p (q n) -> p q n", q=QT)
        scaled = pt[:, 0:S]
        sq_total = logit[:, 0:S]
        sum_h, sum_x1, sum_gate, gate_sq = qt, kt, logit[:, S:2 * S], logit[:, 0:S]

        mem_landed, vecs_landed, taps_landed, consts_landed, pos_landed = (
            sem(n + "_landed") for n in ("mem", "vecs", "taps", "consts", "pos"))
        x_landed = [sem(f"x{q}_landed") for q in range(QT)]
        xsq_made, x_diag, x_turned = sem("xsq_made"), sem("x_diag_made"), sem("x_turned")
        raw_landed = [sem("raw0_landed"), sem("raw1_landed")]
        swapped_landed, gating_landed = sem("swapped_landed"), sem("gating_landed")
        hi_made, lo_made = sem("hi_made"), sem("lo_made")
        chunk_entered = sem("chunk_entered")
        lin_ready = sem("lin_ready")
        lin_freed = [sem("lin0_freed"), sem("lin1_freed")]
        pool_made, table_made = sem("pool_made"), sem("table_made")
        start_made = sem("start_made")
        xt_ready, xt_copied = sem("xt_ready"), sem("xt_copied")
        vec_ready, vec_copied = sem("vec_ready"), sem("vec_copied")
        trig_arg, trig_made = sem("trig_arg"), sem("trig_made")
        sq_made, sq_summed = sem("sq_made"), sem("sq_summed")
        std_made, rstd_made, diag_made, bc_ready = (sem(n) for n in ("std_made", "rstd_made", "diag_made", "bc_ready"))
        u_made, u_high, u_low = sem("u_made"), sem("u_high"), sem("u_low")
        kr_ready, kr_placed = sem("kr_ready"), sem("kr_placed")
        z_made, tap_done = sem("z_made"), sem("tap_done")
        vtr_ready, vtok_placed = sem("vtr_ready"), sem("vtok_placed")
        bias_made = sem("bias_made")
        scores_ready, logits_made, probs_made = sem("scores_ready"), sem("logits_made"), sem("probs_made")
        pt_ready, pt_act, pt_dve = sem("pt_ready"), sem("pt_copied_scalar"), sem("pt_copied_vector")
        rden_made, out_ready, out_copied = sem("rden_made"), sem("out_ready"), sem("out_copied")
        ot_ready, o_high, o_low = sem("ot_ready"), sem("o_high"), sem("o_low")
        mean_ready, centred = sem("mean_ready"), sem("centred")
        y_norm, y_tanh, y_made, y_high, y_low = (sem(n) for n in ("y_norm", "y_tanh", "y_made", "y_high", "y_low"))
        m_made, m_high, m_low = sem("merged_made"), sem("merged_high"), sem("merged_low")
        mt_ready = sem("mt_ready")
        xvt_ready, xv_placed = sem("xvt_ready"), sem("xv_placed")
        xs_ready, xmax_made, xp_made, xrden_made, xp_scaled = (
            sem(n) for n in ("xs_ready", "xmax_made", "xp_made", "xrden_made", "xp_scaled"))
        xpt_ready, xpt_act, xpt_dve = sem("xpt_ready"), sem("xpt_copied_scalar"), sem("xpt_copied_vector")
        xo_ready, xo_high, xo_low = sem("xo_ready"), sem("xo_high"), sem("xo_low")
        f_sq, f_high, f_low = sem("f_sq"), sem("f_high"), sem("f_low")
        x1_made = sem("x1_made")
        g_square, g_poly, g_tanh = sem("gelu_square"), sem("gelu_poly"), sem("gelu_tanh")
        rbc_made = sem("rbc_made")
        mlp_scaled, mem_scaled, h_added = sem("mlp_scale_made"), sem("mem_scale_made"), sem("h_added")
        sums_cleared, minus_made = sem("sums_cleared"), sem("minus_made")
        hsq_made, hsq_added, gsq_made, gsq_added = (sem(n) for n in ("hsq_made", "hsq_added", "gsq_made", "gsq_added"))
        xmin_made, mem_high, mem_low = sem("xmin_made"), sem("mem_high"), sem("mem_low")
        fin_scaled_vector, fin_scaled_scalar = sem("fin_scaled_vector"), sem("fin_scaled_scalar")
        sq_added = sem("sq_added")
        added_summed, gating_made = sem("added_summed"), sem("gating_made")
        gv_made, gvt_ready, atok_placed = sem("gv_made"), sem("gvt_ready"), sem("atok_placed")
        ws_masked, wst_ready, wst_placed = sem("ws_masked"), sem("wst_ready"), sem("wst_placed")
        mix_ready, mix_read, ya_made = sem("mix_ready"), sem("mix_read"), sem("ya_made")
        silu_tanh, gate_prod = sem("silu_tanh"), sem("gate_prod")
        ob_ready, yb_made, yb_high, yb_low = (sem(n) for n in ("ob_ready", "yb_made", "yb_high", "yb_low"))
        ya_high, ya_low = sem("ya_high"), sem("ya_low")
        fin_made, fin_ready, fin_copied, stored = (sem(n) for n in ("fin_made", "fin_ready", "fin_copied", "stored"))
        vector_steps, pool_steps = sem("vector_steps"), sem("pool_steps")

        def wait(eng, s, v):
            if not isinstance(v, int) or v > 0:
                eng.wait_ge(s, v)

        def now(eng, v):
            return v if isinstance(v, int) else eng.snap(eng.to_reg(v))

        def phase(name, per_c=0, per_j=0, i=None):
            return Idx(CHUNK0[name], per_c, i), Idx(JOB0[name], per_j, i)

        def col(name, k=0):
            return cols[:, COL[name] + k:COL[name] + k + 1]

        def evacuated(eng, j):
            eng.wait_ge(lin_freed[j.slot(2)], (j + 2).half())

        def chain(eng, s):
            done = [0]

            def step(ins):
                done[0] += 1
                ins.then_inc(s, 1)
                eng.wait_ge(s, done[0])
            return step

        BC_READ = {n: (u_made, NORMED0[n] + k) for n, k in (("q", 3), ("kv", 2))}
        BC_READ.update(conv=(y_norm, CT), mem=(mem_scaled, 1), mlp=(mlp_scaled, 1), second=(rbc_made, 1),
                       final=(x1_made, DT))
        NTOK = {"mem": MEM}
        WIDTH = {"q": QLORA, "kv": KVLORA, "conv": CONV}
        NTILES = dict(NORMS)
        SPLIT_TILES = {n: k for n, k, _ in SPLITS}
        SLOTS = {"mlp": (qt, kt)}

        KEYS = [P * (q + 1) for q in range(QT)]
        LOFF = [0, 128, 384, 768]
        SBANK = [(0, 0), (0, 128), (1, 0), (2, 0)]
        PTBANK = [(0, 0), (0, 128), (1, 0), (0, 0)]
        PTOFF = [0, 128, 512, 0]
        SCORES_AT = [1, 1, 2, 3]

        block = ctx.enter_context(nc.Block())

        @block.sync
        def _(sp):
            def view(w):
                return w.rearrange("(k p) m -> p k m", p=P)

            def place(c, k, m):
                at = now(sp, (c + -1).v())
                if not isinstance(at, int):
                    sp.wait_ge(lo_made, 1)
                wait(sp, lo_made, at)
                return raw[:, c.slot(2), 0:k * m].rearrange("p (k m) -> p k m", k=k)

            def load(c, w, first, k, m):
                src = view(w)[:, :, bass.ds(now(sp, first), m)]
                sp.dma_start(place(c, k, m), src).then_inc(raw_landed[c.slot(2)], 16)

            def load_rope(c, w, first, rope, k):
                half = ROPE // 2
                src, second, front = (view(w)[:, :, bass.ds(now(sp, at), n)] for at, n in
                                      ((first, 96), (rope + half, half), (rope, half)))
                dst = place(c, k, P)
                sp.dma_start(dst[:, :, 0:96], src).then_inc(raw_landed[c.slot(2)], 16)
                sp.dma_start(dst[:, :, 96:96 + half], second).then_inc(swapped_landed, 16)
                sp.dma_start(dst[:, :, 96 + half:P], front).then_inc(swapped_landed, 16)

            def stream(name, w, first, k, m):
                with sp.Fori(0, COUNTS[name][0] // 4) as i:
                    c, _ = phase(name, 4, 0, i)
                    for n in range(4):
                        load(c + n, w, first + m * n + (m * 4) * i, k, m)

            w_in, w_in2 = a["w_in"][0], a["w_in_2"][0]
            for name, n in VECS:
                v = a[name] if len(a[name].shape) == 1 else a[name][0]
                sp.dma_start(vrows[COL[name]:COL[name] + n, :], v.rearrange("(n p) -> n p", p=P))\
                    .then_inc(vecs_landed, 16)
            c, _ = phase("latent")
            for m in range(5):
                if m == 2:
                    sp.dma_start(crows[:], a["conv_w"][0]).then_inc(taps_landed, 16)
                    sp.dma_start(consts[:], a["shape_consts"]).then_inc(consts_landed, 16)
                    sp.dma_start(qt[64:128, :].bitcast(I32), a["positions"][0].partition_broadcast(64))\
                        .then_inc(pos_landed, 16)
                load(c + m, w_in, 2 * CONV + P * m, DT, P)
            rope0 = 2 * CONV + QLORA + KVLORA
            load_rope(c + 5, w_in, rope0 - NOPE, rope0, DT)
            with sp.Fori(0, 2) as i:
                c, _ = phase("conv", 4, 0, i)
                for m in range(4):
                    load(c + m, w_in, (m % 2) * CONV + (m // 2) * P + (2 * P) * i, DT, P)
            with sp.Fori(0, HEADS) as i:
                c, _ = phase("heads", 4, 0, i)
                load_rope(c, a["w_uq"][0], 96 * i, 96 * i + NOPE, 3)
                load(c + 1, a["w_ukv"][0], P * i, 2, P)
                for m in range(2):
                    load(c + 2 + m, w_in, rope0 + ROPE + P * m + (2 * P) * i, DT, P)
            stream("mla_out", a["w_mla_out"][0], 0, 4, 256)
            stream("conv_out", a["w_conv_out"][0], 0, 4, 256)
            c, _ = phase("w_out")
            for m in range(DT):
                if m == 2:
                    sp.wait_ge(m_made, DT)
                    sp.dma_start(memtok[:], a["mem"][0].rearrange("(q p) n -> p q n", p=P)).then_inc(mem_landed, 16)
                load(c + m, a["w_out"][0], P * m, DT, P)
            stream("xkv", a["w_xkv"][0], 0, DT, P)
            stream("xq", a["w_xq"][0], 0, DT, P)
            stream("xo", a["w_xo"][0], 0, 4, 256)
            for half in range(2):
                stream(f"up{half}", a["w_mlp1"][0], half * FF // 2, DT, P)
                with sp.Fori(0, 4) as i:
                    c, _ = phase(f"down{half}", 4, 0, i)
                    for m in range(4):
                        first = half * FF // 2 + (m % 2) * D
                        load(c + m, a["w_mlp2"][0][first:first + D, :], (m // 2) * P + (2 * P) * i, DT, P)
            stream("av", w_in2, D, DT, P)
            with sp.Fori(0, PAIRS) as i:
                c, _ = phase("pairs", 8, 0, i)
                for m, first in enumerate((3, 4, 5, 0, 2, 6, 7, 8)):
                    load(c + m, w_in2, first * D + P * i, DT, P)
                    if m == 3:
                        weights, biases = a["w_s_2"][0][i], a["b_s_2"][0][i].partition_broadcast(P)
                        sp.wait_ge(mix_read, i + 1)
                        sp.dma_start(ws, weights).then_inc(gating_landed, 16)
                        sp.dma_start(bsb, biases).then_inc(gating_landed, 16)
            stream("proj_b", a["w_proj_b_2"][0], 0, DT, P)
            stream("proj_a", a["w_proj_a_2"][0], 0, DT, P)
            stream("w_out2", a["w_out_2"][0], 0, DT, P)
            for q in (0, 2, 1, 3):
                sp.wait_ge((fin_scaled_vector, fin_scaled_scalar)[q // 2], q % 2 + 1)
                sp.dma_start(out[0][q * P:(q + 1) * P, :], fin[:, q, :]).then_inc(stored, 16)
            sp.wait_ge(stored, 16 * QT)

        @block.gpsimd
        def _(pool):
            step = chain(pool, pool_steps)
            step(pool.memset(ident[:], 0.0))
            pool.affine_select(out=ident[:], in_=ident[:], compare_op=ALU.not_equal, fill=1.0, base=0,
                               pattern=[[-1, P]], channel_multiplier=1).then_inc(pool_made, 1)
            step(pool.memset(bias[:], 0.0))
            pool.affine_select(out=bias[:], in_=bias[:], compare_op=ALU.is_ge, fill=BIG, base=S - P,
                               pattern=[[-1, S]], channel_multiplier=1).then_inc(pool_made, 1)
            def add_squares(name):
                n = NTOK.get(name, S)
                for f in range(1, NTILES[name]):
                    s_ = SQ0[name] + f
                    pool.wait_ge(sq_made, s_ + 1)
                    wait(pool, sq_added, ADD0[name] + f - 1)
                    pool.tensor_tensor(sq_total[:, 0:n], sq_total[:, 0:n], SLOTS.get(name, (ta, tb))[s_ % 2][:, 0:n],
                                       ALU.add).then_inc(sq_added, 1)

            add_squares("mem")
            add_squares("xattn")
            pool.wait_ge(xo_low, XH)
            dint = atok[:].rearrange("p a b -> p (a b)").bitcast(I32)
            step(pool.iota(dint, [[-1, S]], base=S - P, channel_multiplier=1))
            pool.tensor_copy(dist[:], dint).then_inc(pool_made, 1)
            add_squares("mlp")
            pool.wait_ge(table_made, 1)
            pool.affine_select(out=nlog[:], in_=nlog[:], compare_op=ALU.is_ge, fill=BIG, base=S - P,
                               pattern=[[-1, S]], channel_multiplier=1).then_inc(pool_made, 1)
            pool.wait_ge(std_made, NORM_NO["mlp"] + 1)
            pool.memset(sum_h[:], 0.0).then_inc(sums_cleared, 1)
            pool.memset(sum_x1[:], 0.0).then_inc(sums_cleared, 1)
            pool.wait_ge(sums_cleared, 2)
            with pool.Fori(0, DT) as f:
                for n, (total, part) in enumerate(((sum_h, ta), (sum_x1, tb))):
                    pool.wait_ge(hsq_made, 2 * f + (n + 1))
                    pool.wait_ge(hsq_added, 2 * f + n + 1)
                    pool.tensor_tensor(total[:], total[:], part[:], ALU.add).then_inc(hsq_added, 1)
            pool.memset(sum_gate, 0.0).then_inc(sums_cleared, 1)
            pool.wait_ge(sums_cleared, 3)
            with pool.Fori(0, PAIRS) as f:
                pool.wait_ge(gsq_made, f + 1)
                pool.wait_ge(gsq_added, f + 1)
                pool.tensor_tensor(sum_gate, sum_gate, gate_sq, ALU.add).then_inc(gsq_added, 1)
            with pool.Fori(0, PAIRS) as i:
                at = now(pool, 32 * i + 32)
                pool.wait_ge(table_made, 1)
                pool.wait_ge(gating_landed, at)
                pool.affine_select(out=ws, in_=ws, compare_op=ALU.is_ge, fill=0.0, base=0, pattern=[[-1, P]],
                                   channel_multiplier=1).then_inc(ws_masked, 1)
            add_squares("out")

        @block.tensor
        def _(pe):
            def products(o, slot, k, m, xh_, xl_, start, stop, w, enter):
                at = slice(k * w + m * P, k * w + (m + 1) * P)
                ins = pe.matmul(o, wh[:, slot, at], xh_, start=start, stop=False)
                if enter:
                    ins.then_inc(chunk_entered, 1)
                pe.matmul(o, wh[:, slot, at], xl_, start=False, stop=False)
                return pe.matmul(o, wl[:, slot, at], xh_, start=False, stop=stop)

            def open_job(j):
                wait(pe, lin_freed[j.slot(2)], j.half())
                return lin[j.slot(2)]

            def job(c, j, rows, xh_, xl_, n=S, before=None, between={}):
                o = open_job(j)[:, 0:n]
                wait(pe, lo_made, (c + 1).v())
                for k in range(rows):
                    if before is not None:
                        before(k)
                    if k in between:
                        between[k]()
                    ins = products(o, c.slot(4), k, 0, xh_[:, k, :], xl_[:, k, :], k == 0, k == rows - 1, P, k == 0)
                ins.then_inc(lin_ready, 1)

            def two_jobs(c, j, xh_, xl_, before=None):
                wait(pe, lo_made, (c + 1).v())
                for m in range(2):
                    o = open_job(j + m)[:]
                    for k in range(4):
                        if before is not None and m == 0:
                            before(k)
                        ins = products(o, c.slot(4), k, m, xh_[:, k, :], xl_[:, k, :], k == 0, k == 3, 256,
                                       m == 0 and k == 0)
                    ins.then_inc(lin_ready, 1)

            def tiles_of(sem_, base):
                return lambda k: pe.wait_ge(sem_, base + k + 1)

            def turn_tile(dst, src, n=QT, idt=ident):
                for q in range(n):
                    ins = pe.transpose(dst[:, q * P:(q + 1) * P], src(q), idt[:])
                return ins

            def sum_squares(name, f):
                s, n = SQ0[name] + f, NTILES[name]
                if f == 0:
                    wait(pe, std_made, NORM_NO[name])
                pe.wait_ge(sq_made, s + 1)
                for q in range(NTOK.get(name, S) // P):
                    ins = pe.matmul(tr[1][:, q:q + 1], SLOTS.get(name, (ta, tb))[s % 2][:, q * P:(q + 1) * P], ones[:, 0:1],
                                    start=(f == 0 and q == 0), stop=(f == n - 1), skip_group_check=True)
                ins.then_inc(sq_summed, 1)

            def sums(name):
                for f in range(NTILES[name]):
                    sum_squares(name, f)

            def sum_total(name):
                pe.wait_ge(std_made, NORM_NO[name])
                pe.wait_ge(sq_added, ADD0[name] + NTILES[name] - 1)
                for q in range(NTOK.get(name, S) // P):
                    ins = pe.matmul(tr[1][:, q:q + 1], sq_total[:, q * P:(q + 1) * P], ones[:, 0:1], start=q == 0,
                                    stop=True, skip_group_check=True)
                ins.then_inc(sq_summed, 1)

            def broadcast(name):
                k = BC_NO[name]
                if k:
                    pe.wait_ge(*BC_READ[BROADCAST[k - 1]])
                pe.wait_ge(diag_made, k + 1)
                n = NTOK.get(name, S)
                pe.matmul(tr[0][:, 0:n], ones[:], te[:, 0:n], start=True, stop=True).then_inc(bc_ready, 1)

            def sum_added(*totals):
                for k, total in enumerate(totals):
                    for q in range(QT):
                        ins = pe.matmul(tr[1][:, 4 * k + q:4 * k + q + 1], total[:, q * P:(q + 1) * P], ones[:, 0:1],
                                        start=(k == 0 and q == 0), stop=True, skip_group_check=True)
                ins.then_inc(added_summed, 1)

            def scores(n, rows):
                wait(pe, logits_made, n.times(4, 1))
                for q in range(QT):
                    b, o = SBANK[q]
                    ins = pe.matmul(sc[b][:, o:o + KEYS[q]], qt[rows, q * P:(q + 1) * P], kt[rows, 0:KEYS[q]],
                                    start=True, stop=True)
                    if q:
                        ins.then_inc(scores_ready, 1)

            def turn(q):
                b, o = PTBANK[q]
                for kb in range(q + 1):
                    ins = pe.transpose(tr[b][:, o + kb * P:o + (kb + 1) * P],
                                       logit[:, LOFF[q] + kb * P:LOFF[q] + (kb + 1) * P], ident[:])
                return ins

            def weigh(q, v):
                for kb in range(q + 1):
                    ins = pe.matmul(ob[:, q * VD:(q + 1) * VD], pt[:, PTOFF[q] + kb * P:PTOFF[q] + (kb + 1) * P],
                                    v(kb), start=kb == 0, stop=kb == q)
                return ins

            def finish(n, v):
                def turn_0_1():
                    wait(pe, probs_made, n.times(4, 2))
                    wait(pe, pt_act, n.times(2, 1))
                    turn(0)
                    turn(1).then_inc(pt_ready, 1)

                def turn_2():
                    wait(pe, probs_made, n.times(4, 3))
                    wait(pe, pt_dve, n.times(1, 1))
                    turn(2).then_inc(pt_ready, 1)

                def weigh_0_1_turn_3():
                    wait(pe, pt_act, n.times(2, 2))
                    wait(pe, out_copied, n.times(1, 1))
                    weigh(0, v)
                    weigh(1, v)
                    wait(pe, probs_made, n.times(4, 4))
                    turn(3).then_inc(pt_ready, 1)

                def weigh_2():
                    wait(pe, pt_dve, n.times(1, 2))
                    weigh(2, v)

                def weigh_3():
                    wait(pe, pt_act, n.times(2, 3))
                    weigh(3, v).then_inc(out_ready, 1)

                return turn_0_1, turn_2, weigh_0_1_turn_3, weigh_2, weigh_3

            pe.wait_ge(pool_made, 1)
            pe.wait_ge(vecs_landed, 16 * len(VECS))
            pe.transpose(tr[0][:, 0:NVEC], vrows[0:NVEC, :], ident[0:NVEC, 0:NVEC]).then_inc(vec_ready, 1)
            pe.wait_ge(start_made, 1)

            def turn_normed(f):
                if f >= 3:
                    pe.wait_ge(u_low, f - 2)
                for q in range(QT):
                    ins = pe.matmul(sc[f % 3][:, q * P:(q + 1) * P], xtok[:, q, f * P:(f + 1) * P],
                                    te[:, q * P:(q + 1) * P], start=True, stop=True)
                ins.then_inc(xt_ready, 1)

            def turn_bare(f):
                pe.wait_ge(*((u_low, DT) if f < 3 else (xt_copied, f - 2)))
                turn_tile(sc[f % 3], lambda q: xtok[:, q, f * P:(f + 1) * P]).then_inc(x_turned, 1)

            for q in range(QT):
                pe.wait_ge(x_landed[q], 16)
            pe.wait_ge(x_diag, 1)
            for f in range(3):
                turn_normed(f)

            c, j = phase("latent")
            for m in range(6):
                if m == 0:
                    job(c, j, DT, uh, ul, before=tiles_of(u_low, U0["mix"]),
                        between={k: lambda k=k: turn_normed(k + 2) for k in range(1, 6)})
                else:
                    job(c + m, j + m, DT, uh, ul)
                if m < 4:
                    turn_bare(2 * m)
                    turn_bare(2 * m + 1)
                if m == 0:
                    pe.wait_ge(taps_landed, 16)
                    for t in range(CT):
                        ins = pe.transpose(tr[1][:, t * 32:t * 32 + TAPS], crows[:, t * P:(t + 1) * P],
                                           ident[0:TAPS, 0:TAPS])
                    ins.then_inc(vec_ready, 1)
                if m == 1:
                    pe.wait_ge(vec_copied, 2)
                if 1 <= m <= 3:
                    sum_squares("q", m - 1)
                if m == 4:
                    broadcast("q")
                if m >= 4:
                    sum_squares("kv", m - 4)
            pe.wait_ge(xt_copied, DT)

            c, j = phase("conv")
            for m in range(8):
                job(c + m, j + m, DT, uh, ul)
                if m == 0:
                    evacuated(pe, Idx(JOB0["latent"] + 5))
                    pe.wait_ge(start_made, SEL_MADE)
                    pe.matmul(sc[0][:], sel[64:128, :], logit[64:128, 0:S], start=True, stop=True).then_inc(kr_ready, 1)
                if m == 1:
                    broadcast("kv")

            pe.wait_ge(u_low, U0["kv"] + 2)
            pe.wait_ge(kr_placed, 1)
            with pe.Fori(0, HEADS) as i:
                c, j = phase("heads", 4, 4, i)
                n = Idx(0, 1, i)
                job(c, j, 3, cqh, cql)
                job(c + 1, j + 1, 2, ckh, ckl)

                def turn_values_and_score():
                    copied = now(pe, n.times(1, 1))
                    freed_ = now(pe, (j + 3).half())
                    pe.wait_ge(pool_made, 1)
                    pe.wait_ge(out_copied, copied)
                    pe.wait_ge(lin_freed[(j + 1).slot(2)], freed_)
                    for kb in range(QT):
                        ins = pe.transpose(ob[:, 256 + kb * VD:256 + (kb + 1) * VD], td[64:128, kb * P:(kb + 1) * P],
                                           ident[64:128, 64:128])
                    ins.then_inc(vtr_ready, 1)
                    evacuated(pe, j)
                    scores(n, slice(0, P))

                parts = finish(n, lambda kb: vtok[:, kb, 0:VD])

                def first_part():
                    pe.wait_ge(vtok_placed, n.times(1, 1))
                    parts[0]()

                job(c + 2, j + 2, DT, uh, ul, between={3: turn_values_and_score})
                job(c + 3, j + 3, DT, uh, ul,
                    between={3: first_part, 4: parts[1], 5: parts[2], 7: parts[3]})
                parts[4]()

            pe.wait_ge(tap_done, CT * (TAPS + 1))
            for t in range(CT):
                ins = pe.matmul(sc[0][:], ones[:], acc[:, t, :], start=t == 0, stop=t == CT - 1)
            ins.then_inc(mean_ready, 1)
            pe.wait_ge(out_copied, HEADS + 1)
            for f in range(4):
                if f >= 2:
                    pe.wait_ge(o_low, f - 1)
                turn_tile(sc[1 + f % 2], lambda q: otok[:, q, f * P:(f + 1) * P]).then_inc(ot_ready, 1)
            c, j = phase("mla_out")
            for m in range(4):
                two_jobs(c + m, j + 2 * m, oh, ol, tiles_of(o_low, 0) if m == 0 else None)
                if m == 0:
                    sums("conv")
                if m == 1:
                    broadcast("conv")
            c, j = phase("conv_out")
            for m in range(4):
                two_jobs(c + m, j + 2 * m, yh, yl, tiles_of(y_low, 0) if m == 0 else None)

            c, j = phase("w_out")
            for m in range(DT):
                job(c + m, j + m, DT, uh, ul, before=tiles_of(m_low, 0) if m == 0 else None)
                if m == 1:
                    pe.wait_ge(mem_landed, 16)
                for f in ((), (0, 1))[m] if m < 2 else (m,):
                    if f >= 3:
                        pe.wait_ge(mem_low, f - 2)
                    turn_tile(sc[f % 3], lambda q: memtok[:, q, f * P:(f + 1) * P], 2).then_inc(mt_ready, 1)

            def turn_values(hd):
                evacuated(pe, Idx(JOB0["xkv"] + XH + hd))
                wait(pe, xv_placed, hd)
                turn_tile(ob, lambda q: (qt, kt)[hd % 2][:, q * P:(q + 1) * P], 2).then_inc(xvt_ready, 1)

            c, j = phase("xkv")
            for m in range(8):
                job(c + m, j + m, DT, memh, meml, MEM, tiles_of(mem_low, 0) if m == 0 else None)
                if m == 0:
                    sum_total("mem")
                if m == 1:
                    broadcast("mem")
                if m == 6:
                    sum_total("xattn")
                if m >= 5:
                    turn_values(m - 5)
            def x_scores(hd):
                evacuated(pe, Idx(JOB0["xq"] + hd))
                if hd >= 2:
                    pe.wait_ge(xo_low, hd - 1)
                for q in range(QT):
                    b = ((sc[0], sc[1]), (sc[2], ob))[hd % 2][q // 2]
                    ins = pe.matmul(b[:, (q % 2) * MEM:(q % 2 + 1) * MEM], xq[:, hd, q * P:(q + 1) * P], xk[:, hd, :],
                                    start=True, stop=True)
                    if q % 2:
                        ins.then_inc(xs_ready, 1)

            def x_turn(hd):
                for b in range(2):
                    pe.wait_ge(xp_scaled, 2 * hd + b + 1)
                    wait(pe, (xpt_act, xpt_dve)[b], hd)
                    for q in range(2):
                        for kb in range(2):
                            ins = pe.transpose(tr[b][:, kb * 256 + q * P:kb * 256 + (q + 1) * P],
                                               xp[:, hd % 2, 2 * b + q, kb * P:(kb + 1) * P], ident[:])
                    ins.then_inc(xpt_ready, 1)

            def x_weigh(hd):
                pe.wait_ge(xpt_act, hd + 1)
                pe.wait_ge(xpt_dve, hd + 1)
                for kb in range(2):
                    ins = pe.matmul(sc[2 * (hd % 2)][:], xv[:, kb, hd * XD:(hd + 1) * XD], xpt[:, hd % 2, kb, :],
                                    start=kb == 0, stop=kb == 1)
                ins.then_inc(xo_ready, 1)

            c, j = phase("xq")
            job(c, j, DT, xuh, xul, before=tiles_of(u_low, U0["xattn"]))
            turn_values(3)

            def first_scores():
                pe.wait_ge(xv_placed, XH)
                x_scores(0)

            job(c + 1, j + 1, DT, xuh, xul, between={3: first_scores})
            job(c + 2, j + 2, DT, xuh, xul, between={3: lambda: x_scores(1), 5: lambda: x_turn(0)})
            x_weigh(0)
            job(c + 3, j + 3, DT, xuh, xul, between={3: lambda: x_scores(2), 5: lambda: x_turn(1)})
            x_weigh(1)
            x_turn(2)
            x_scores(3)
            x_weigh(2)
            x_turn(3)
            x_weigh(3)
            c, j = phase("xo")
            for m in range(4):
                two_jobs(c + m, j + 2 * m, xoh, xol, tiles_of(xo_low, 0) if m == 0 else None)

            c, j = phase("up0")
            for m in range(4):
                job(c + m, j + m, DT, uh, ul, before=tiles_of(u_low, U0["mlp"]) if m == 0 else None)
            sum_total("mlp")
            for half in range(2):
                with pe.Fori(1 - half, 4) as i:
                    c, j = phase(f"up{half}", 4, 4, i)
                    for m in range(4):
                        job(c + m, j + m, DT, uh, ul)
                if half == 0:
                    broadcast("mlp")
                with pe.Fori(0, 4) as i:
                    c, j = phase(f"down{half}", 4, 2, i)
                    for m in range(2):
                        o = open_job(j + m)[:]
                        for b in range(2):
                            cc = c + (2 * m + b)
                            wait(pe, lo_made, (cc + 1).v())
                            pe.wait_ge(f_low, 16 * half + (8, 15)[b])
                            for k in range(DT):
                                if b and k == DT - 1:
                                    pe.wait_ge(f_low, 16 * half + 16)
                                ins = products(o, cc.slot(4), k, 0, fh[:, DT * b + k, :], fl[:, DT * b + k, :],
                                               b == 0 and k == 0, b == 1 and k == DT - 1, P, k == 0)
                        ins.then_inc(lin_ready, 1)

            c, j = phase("av")
            job(c, j, DT, uh, ul, before=tiles_of(u_low, U0["raw"]))
            pe.wait_ge(hsq_added, 2 * DT + 1)
            sum_added(sum_h, sum_x1)
            job(c + 1, j + 1, DT, uh, ul)
            broadcast("second")
            job(c + 2, j + 2, DT, uh, ul)
            job(c + 3, j + 3, DT, uh, ul)
            with pe.Fori(1, 2) as i:
                c, j = phase("av", 4, 4, i)
                for m in range(4):
                    job(c + m, j + m, DT, uh, ul)

            def pair(c, j, g, n0, n1):
                job(c + 2, j + 2, DT, vh, vl)

                def first_scores():
                    evacuated(pe, j)
                    evacuated(pe, j + 1)
                    scores(n0, slice(0, 64))

                def turn_values():
                    pe.wait_ge(rbc_made, 1)
                    evacuated(pe, j + 2)
                    turn_tile(tr[0], lambda q: td[:, q * P:(q + 1) * P]).then_inc(vtr_ready, 1)

                job(c + 3, j + 3, DT, vh, vl, between={2: first_scores, 5: turn_values})
                pe.wait_ge(vtok_placed, g.times(1, HEADS + 1))
                parts = finish(n0, lambda kb: vtok[:, kb, 0:64])
                job(c + 4, j + 4, DT, vh, vl, between={
                    1: parts[0], 2: parts[1], 4: parts[2], 5: parts[3], 6: parts[4],
                    7: lambda: scores(n1, slice(64, P))})
                pe.wait_ge(gv_made, g.times(1, 1))
                turn_tile(tr[1], lambda q: tc[:, q * P:(q + 1) * P]).then_inc(gvt_ready, 1)
                job(c + 5, j + 5, DT, vh, vl)
                pe.wait_ge(atok_placed, g.times(1, 1))
                parts = finish(n1, lambda kb: vtok[:, kb, 64:P])
                job(c + 6, j + 6, DT, vh, vl, between={
                    1: parts[0], 2: parts[1], 4: parts[2], 5: parts[3], 6: parts[4]})

                def turn_out_and_mixing():
                    pe.wait_ge(ws_masked, g.times(1, 1))
                    pe.wait_ge(out_copied, n1.times(1, 2))
                    pe.transpose(ob[:, 0:P], ws, ident[:]).then_inc(wst_ready, 1)
                    turn_tile(tr[0], lambda q: otp[:, q, :]).then_inc(ob_ready, 1)

                def mix():
                    pe.wait_ge(wst_placed, g.times(1, 1))
                    for q in range(QT):
                        ins = pe.matmul(tr[1][:, q * P:(q + 1) * P], atok[:, q, :], wst[:], start=True, stop=True)
                    ins.then_inc(mix_ready, 1)

                job(c + 7, j + 7, DT, vh, vl, between={2: turn_out_and_mixing, 5: mix})
                pe.wait_ge(mix_read, g.times(1, 2))
                pe.wait_ge(yb_made, g.times(1, 1))

            c, j = phase("pairs")
            job(c, j, DT, vh, vl, before=tiles_of(u_low, U0["second"]))

            def sum_gating():
                pe.wait_ge(gsq_added, PAIRS + 1)
                sum_added(sum_gate)

            job(c + 1, j + 1, DT, vh, vl, between={6: sum_gating})
            with pe.Fori(0, PAIRS - 1) as i:
                c, j = phase("pairs", 8, 8, i)
                pair(c, j, Idx(0, 1, i), Idx(HEADS, 2, i), Idx(HEADS + 1, 2, i))
                job(c + 8, j + 8, DT, vh, vl)
                job(c + 9, j + 9, DT, vh, vl)
            c, j = phase("pairs")
            g = PAIRS - 1
            pair(c + 8 * g, j + 8 * g, Idx(g), Idx(HEADS + 2 * g), Idx(HEADS + 1 + 2 * g))

            def turn_output(f):
                pe.wait_ge(fin_made, f + 1)
                if f >= 3:
                    pe.wait_ge(fin_copied, f - 2)
                turn_tile(sc[f % 3], lambda q: (tc, td)[f % 2][:, q * P:(q + 1) * P]).then_inc(fin_ready, 1)

            for name, hi, lo, ready, base in (("proj_b", ybh, ybl, yb_low, 1), ("proj_a", vh, vl, ya_low, 0),
                                              ("w_out2", uh, ul, m_low, DT)):
                c, j = phase(name)
                for m in range(DT):
                    job(c + m, j + m, DT, hi, lo, before=tiles_of(ready, base) if m == 0 else None)
                    if name == "proj_b" and m == 0:
                        broadcast("final")
                    if name == "w_out2" and m:
                        turn_output(m - 1)
            turn_output(DT - 1)
            sum_total("out")

        @block.scalar
        def _(act):
            for q in range(QT):
                act.dma_start(xtok[:, q, :], a["x"][0][q * P:(q + 1) * P, :]).then_inc(x_landed[q], 16)

            def split(c):
                if c.i is None and c.static >= NCHUNKS:
                    return
                size = chunk_size(c.static)
                v = 16 * (c.static // 2 + 1)
                act.wait_ge(raw_landed[c.slot(2)], v if c.i is None else v + (8 * c.per) * c.i)
                if size == 3 * P or c.static == CHUNK0["latent"] + 5:
                    v = 32 if size != 3 * P else 64 + 8 * (c.static - CHUNK0["heads"])
                    act.wait_ge(swapped_landed, v if c.i is None else v + (8 * c.per) * c.i)
                wait(act, chunk_entered, (c + -2).v())
                act.activation(wh[:, c.slot(4), 0:size], raw[:, c.slot(2), 0:size], ACT.Copy).then_inc(hi_made, 1)

            def read(j):
                act.wait_ge(lin_ready, (j + 1).v())
                return lin[j.slot(2)]

            def to(j, dst, func, rows=slice(0, P), n=S, **kw):
                act.activation(dst, read(j)[rows, 0:n], func, **kw).then_inc(lin_freed[j.slot(2)], 1)

            def square(name, f, src):
                s, n = SQ0[name] + f, NTOK.get(name, S)
                dst = SLOTS.get(name, (ta, tb))[s % 2][:, 0:n]
                if name not in ADDED:
                    wait(act, sq_summed, s - 1)
                elif f == 0:
                    dst = sq_total[:, 0:n]
                elif f >= 3:
                    act.wait_ge(sq_added, ADD0[name] + f - 2)
                act.activation(dst, src[:, 0:n], ACT.Square).then_inc(sq_made, 1)

            def norm_std(name):
                if NTILES[name]:
                    act.wait_ge(sq_summed, SUMMED[name])
                wait(act, rstd_made, NORM_NO[name])
                n = NTOK.get(name, S) // P
                act.activation(std[:, 0:n], tr[1][:, 0:n], ACT.Sqrt, bias=eps4 if name == "gate_v" else eps,
                               scale=1.0 / WIDTH.get(name, D)).then_inc(std_made, 1)

            def norm_high(name, dst):
                for f in range(SPLIT_TILES[name]):
                    u = U0[name] + f
                    act.wait_ge(u_made, NORMED0[name] + f + 1)
                    act.activation(dst[:, f, :], (tc, td)[u % 2][:], ACT.Copy).then_inc(u_high, 1)

            def gain_high(dst, src, gain):
                act.activation(dst, src, ACT.Identity, scale=gain).then_inc(u_high, 1)

            def exps(n):
                for q in range(QT):
                    wait(act, logits_made, n.times(4, q + 1 + 1))
                    p = logit[:, LOFF[q]:LOFF[q] + KEYS[q]]
                    act.activation(p, p, ACT.Exp, bias=nmax[:, q:q + 1], scale=-1.0, accum_out=den[:, q:q + 1])\
                        .then_inc(probs_made, 1)

            def copy_turned(n, k):
                w = (384, 512)[k]
                wait(act, pt_ready, n.times(3, 1 + 2 * k))
                act.activation(pt[:, 0:w], tr[0][:, 0:w], ACT.Copy).then_inc(pt_act, 1)

            act.wait_ge(start_made, 2)
            act.activation(small[:, 2:3], eps, ACT.Sqrt)
            for q in range(QT):
                act.wait_ge(x_landed[q], 16)
                act.activation(logit[:, 0:D], xtok[:, q, :], ACT.Square, accum_out=x_sq[:, q:q + 1]).then_inc(xsq_made, 1)
                act.wait_ge(xsq_made, q + 1)
            act.activation(std, x_sq, ACT.Sqrt, bias=eps, scale=1.0 / D).then_inc(std_made, 1)
            split(Idx(0))
            act.wait_ge(vec_copied, 1)
            for f in range(DT):
                act.wait_ge(xt_ready, f + 1)
                gain_high(uh[:, f, :], sc[f % 3][:], col("norm_mix_g", f))
            split(Idx(1))
            c, j = phase("latent")
            for m in range(6):
                split(c + (m + 2))
                if m < 5:
                    name, f = ("q", m) if m < 3 else ("kv", m - 3)
                    square(name, f, read(j + m))
                    to(j + m, cq[:, m, :], ACT.Copy)
                if m < 4:
                    for f in (2 * m, 2 * m + 1):
                        act.wait_ge(x_turned, f + 1)
                        act.activation(h[:, f, :], sc[f % 3][:], ACT.Copy).then_inc(xt_copied, 1)
                if m == 3:
                    norm_std("q")
                    act.wait_ge(trig_arg, 1)
                    act.activation(trig[64:128, :], kt[64:128, :], ACT.Sin).then_inc(trig_made, 1)
            norm_high("q", cqh)
            norm_std("kv")

            c, j = phase("conv")
            for m in range(8):
                split(c + (m + 2))
                if m % 2 == 0:
                    to(j + m, z[:, m // 2, PAD:PAD + S], ACT.Copy, scale=0.5)
                else:
                    wait(act, z_made, m // 2 - 1)
                    to(j + m, (logit[:, 512:1024], pt[:, 0:512])[(m // 2) % 2], ACT.Tanh, scale=0.5)
                if m == 2:
                    norm_high("kv", ckh)

            def head(c, j, n, g):
                split(c + 3)
                act.activation(kt[0:64, :], read(j + 1)[0:64, :], ACT.Copy)
                to(j + 1, td[64:128, :], ACT.Copy, rows=slice(64, 128))
                exps(n)
                to(j + 2, gates[:, g, :], ACT.Tanh, scale=0.5)
                split(c + 4)
                split(c + 5)
                copy_turned(n, 0)
                copy_turned(n, 1)
                split(c + 6)
                to(j + 3, gates[:, g + 1, :], ACT.Tanh, scale=0.5)

            split(phase("heads")[0] + 2)
            act.wait_ge(z_made, CT)
            with act.Fori(0, HEADS - 1) as i:
                head(*phase("heads", 4, 4, i), Idx(0, 1, i), 2 * i)
            c, j = phase("heads")
            head(c + 4 * (HEADS - 1), j + 4 * (HEADS - 1), Idx(HEADS - 1), 2 * (HEADS - 1))

            for t in range(CT):
                act.wait_ge(ot_ready, t + 1)
                act.activation(oh[:, t, :], sc[1 + t % 2][:], ACT.Copy).then_inc(o_high, 1)
            c, _ = phase("mla_out")
            for t in range(CT):
                act.wait_ge(centred, t + 1)
                square("conv", t, acc[:, t, :])
            split(c + 3)
            norm_std("conv")
            split(c + 4)
            for t in range(CT + 1):
                if t < CT:
                    act.wait_ge(y_norm, t + 1)
                    y = acc[:, t, :]
                    act.activation((qt, kt)[t % 2][:], y, ACT.Identity, bias=hb[:, t:t + 1], scale=0.5)
                    act.activation((ta, tb)[t % 2][:], y, ACT.Tanh, bias=hb[:, t:t + 1], scale=0.5).then_inc(y_tanh, 1)
                if t:
                    act.wait_ge(y_made, t)
                    act.activation(yh[:, t - 1, :], (tc, td)[(t - 1) % 2][:], ACT.Copy).then_inc(y_high, 1)
                if t == 3:
                    split(c + 5)
            c, _ = phase("conv_out")
            for m in range(4):
                split(c + (m + 2))
                for f in (2 * m, 2 * m + 1):
                    act.wait_ge(m_made, f + 1)
                    act.activation(uh[:, f, :], (tc, td)[f % 2][:], ACT.Copy).then_inc(m_high, 1)

            c, j = phase("w_out")
            for m in range(DT):
                split(c + (m + 2))
                act.wait_ge(mt_ready, m + 1)
                square("mem", m, sc[m % 3])
                act.activation(memh[:, m, :], sc[m % 3][:, 0:MEM], ACT.Identity, scale=col("norm_mem_g", m))\
                    .then_inc(mem_high, 1)
                if m:
                    evacuated(act, j + (m - 1))
                    gain_high(xuh[:, m - 1, :], h[:, m - 1, :], col("norm_xattn_g", m - 1))
            evacuated(act, j + (DT - 1))
            gain_high(xuh[:, DT - 1, :], h[:, DT - 1, :], col("norm_xattn_g", DT - 1))
            norm_std("mem")
            c, j = phase("xkv")
            for m in range(8):
                split(c + (m + 2))
                if m < 4:
                    square("xattn", 2 * m, h[:, 2 * m, :])
                    square("xattn", 2 * m + 1, h[:, 2 * m + 1, :])
                else:
                    wait(act, xvt_ready, m - 5)
                    to(j + m, (qt, kt)[m % 2][:, 0:MEM], ACT.Copy, n=MEM)
            norm_std("xattn")
            def x_exps(hd):
                for q in range(QT):
                    act.wait_ge(xmax_made, 2 * hd + q // 2 + 1)
                    b = ((sc[0], sc[1]), (sc[2], ob))[hd % 2][q // 2]
                    k = 4 * (hd % 2) + q
                    act.activation(xp[:, hd % 2, q, :], b[:, (q % 2) * MEM:(q % 2 + 1) * MEM], ACT.Exp,
                                   bias=xnmax[:, k:k + 1], scale=minus_rstd[:, q:q + 1], accum_out=xden[:, k:k + 1]).then_inc(xp_made, 1)

            def x_copied(hd):
                act.wait_ge(xpt_ready, 2 * hd + 1)
                act.activation(xpt[:, hd % 2, :, 0:256], tr[0][:].rearrange("p (k q) -> p k q", k=2), ACT.Copy)\
                    .then_inc(xpt_act, 1)

            def x_high(hd):
                act.wait_ge(xo_ready, hd + 1)
                act.activation(xoh[:, hd, :], sc[2 * (hd % 2)][:], ACT.Copy).then_inc(xo_high, 1)

            c, j = phase("xq")
            for m in range(XH):
                split(c + (m + 2))
                if m == 1:
                    act.wait_ge(minus_made, 1)
                if m:
                    x_exps(m - 1)
                if m >= 2:
                    x_copied(m - 2)
                to(j + m, xq[:, m, :], ACT.Copy, scale=CROSS_Q_SCALE)
                if m >= 2:
                    x_high(m - 2)
            x_copied(2)
            x_exps(3)
            x_high(2)
            x_copied(3)
            x_high(3)
            c, j = phase("xo")
            for m in range(4):
                split(c + (m + 2))
                for f in (2 * m, 2 * m + 1):
                    evacuated(act, j + f)
                    gain_high(uh[:, f, :], h[:, f, :], col("norm_mlp_g", f))
                    square("mlp", f, h[:, f, :])

            def up(half, trip):
                c, j = phase(f"up{half}", 4, 4, trip)
                f = Idx(16 * half, 4, trip)
                for m in range(4):
                    split(c + (m + 2))
                    to(j + m, (ta, tb)[m % 2][:], ACT.Relu)
                    act.wait_ge(f_sq, f.times(1, m + 1))
                    act.activation(fh[:, 4 * trip + m, :], (tc, td)[m % 2][:], ACT.Copy).then_inc(f_high, 1)

            up(0, 0)
            norm_std("mlp")
            for half in range(2):
                with act.Fori(1 - half, 4) as i:
                    up(half, i)
                with act.Fori(0, 4) as i:
                    c, _ = phase(f"down{half}", 4, 2, i)
                    for m in range(2):
                        split(c + (2 * m + 2))
                        split(c + (2 * m + 3))
                        if half == 1:
                            f = Idx(m, 2, i)
                            grown, added = now(act, f.times(1, DT + 1)), now(act, f.times(2, 1))
                            act.wait_ge(start_made, 2)
                            act.wait_ge(h_added, grown)
                            act.wait_ge(hsq_added, added)
                            src = h[:, f.v(), :]
                            act.activation(uh[:, f.v(), :], src, ACT.Identity, scale=both[:, bass.ds(f.v(), 1)])\
                                .then_inc(u_high, 1)
                            act.activation(ta[:], src, ACT.Square).then_inc(hsq_made, 1)
                            act.activation(tb[:], src, ACT.Square, scale=cols[:, bass.ds(COL["final_norm_g"] + f.v(), 1)])\
                                .then_inc(hsq_made, 1)

            def gelu(j, k):
                act.activation(ta[:], read(j)[:], ACT.Square).then_inc(g_square, 1)
                act.wait_ge(g_poly, k)
                act.activation(ta[:], tb[:], ACT.Tanh, scale=GELU_C * GELU_A).then_inc(g_tanh, 1)

            c, j = phase("av")
            split(c + 2)
            act.wait_ge(added_summed, 1)
            norm_std("second")
            act.wait_ge(rstd_made, NORM_NO["second"] + 1)
            act.activation(std[:], final_sq[:], ACT.Sqrt, bias=eps).then_inc(std_made, 1)
            def gating_square(m):
                act.wait_ge(gating_made, m + 1)
                wait(act, gsq_added, m + 1)
                act.activation(gate_sq, av[:, m, :], ACT.Square).then_inc(gsq_made, 1)

            for m in range(PAIRS):
                if m:
                    split(c + (m + 2))
                    gating_square(m - 1)
                evacuated(act, j + m)
                wait(act, gating_made, m)
                act.activation(ta[:], scaled, ACT.Square).then_inc(g_square, 1)
                for k, f in enumerate(NORMED_IN[m] or (None,)):
                    if f is not None:
                        act.wait_ge(u_made, NORMED0["second"] + f + 1)
                        act.activation(vh[:, f, :], (tc, td)[(U0["second"] + f) % 2][:], ACT.Copy).then_inc(u_high, 1)
                    if k == 0:
                        act.wait_ge(g_poly, m + 1)
                        act.activation(ta[:], tb[:], ACT.Tanh, scale=GELU_C * GELU_A).then_inc(g_tanh, 1)
            gating_square(PAIRS - 1)
            split(phase("pairs")[0] + 2)
            act.wait_ge(added_summed, 2)
            norm_std("gate_v")

            with act.Fori(0, PAIRS) as i:
                c, j = phase("pairs", 8, 8, i)
                g, n0, n1 = Idx(0, 1, i), Idx(HEADS, 2, i), Idx(HEADS + 1, 2, i)
                to(j, qt[:], ACT.Copy, scale=DILATED_Q_SCALE)
                split(c + 3)
                split(c + 4)
                to(j + 2, td[:], ACT.Copy)
                split(c + 5)
                exps(n0)
                act.wait_ge(ya_made, g.times(1, 1))
                gelu(j + 3, g.times(1, PAIRS + 1))
                split(c + 6)
                copy_turned(n0, 0)
                copy_turned(n0, 1)
                evacuated(act, j + 3)
                act.activation(ta[:], read(j + 4)[:], ACT.Tanh, scale=0.5).then_inc(silu_tanh, 1)
                exps(n1)
                split(c + 7)
                evacuated(act, j + 4)
                act.activation(ta[:], read(j + 5)[:], ACT.Tanh, scale=0.5).then_inc(silu_tanh, 1)
                copy_turned(n1, 0)
                copy_turned(n1, 1)
                split(c + 8)
                act.wait_ge(gv_made, g.times(1, 1))
                to(j + 6, av[:, g.v(), :], ACT.Tanh, scale=0.5)
                act.wait_ge(wst_ready, g.times(1, 1))
                act.activation(wst[:], ob[:, 0:P], ACT.Copy).then_inc(wst_placed, 1)
                act.wait_ge(yb_made, g.times(1, 1))
                act.activation(ybh[:, g.v(), :], tc[:], ACT.Copy).then_inc(yb_high, 1)
                split(c + 9)
                to(j + 7, gb[:, g.v(), :], ACT.Tanh, scale=0.5)
                split(c + 10)

            act.wait_ge(lin_ready, JOB0["proj_b"])
            c, _ = phase("proj_b")
            for m in range(DT):
                if m:
                    split(c + (m + 2))
                act.wait_ge(ya_made, m + 2)
                act.activation(vh[:, m, :], ya[:, m, :], ACT.Copy).then_inc(ya_high, 1)
            c, _ = phase("proj_a")
            for m in range(DT):
                split(c + (m + 2))
                act.wait_ge(m_made, DT + m + 1)
                act.activation(uh[:, m, :], (tc, td)[m % 2][:], ACT.Copy).then_inc(m_high, 1)

            def fin_copy(f):
                act.wait_ge(fin_ready, f + 1)
                act.activation(fin[:, :, f * P:(f + 1) * P], sc[f % 3][:].rearrange("p (q n) -> p q n", q=QT), ACT.Copy)\
                    .then_inc(fin_copied, 1)

            act.activation(small[:, 2:3], eps, ACT.Sqrt)
            c, j = phase("w_out2")
            for m in range(DT):
                split(c + (m + 2))
                evacuated(act, j + m)
                square("out", m, h[:, m, :])
                if m:
                    fin_copy(m - 1)
            norm_std("out")
            fin_copy(DT - 1)
            act.wait_ge(fin_copied, DT)
            act.wait_ge(rstd_made, NORM_NO["out"] + 1)
            for q in (2, 3):
                act.activation(fin[:, q, :], fin[:, q, :], ACT.Copy, scale=rstd[:, q:q + 1]).then_inc(fin_scaled_scalar, 1)

        @block.vector
        def _(dve):
            step = chain(dve, vector_steps)

            def lower(c):
                if c.i is None and c.static >= NCHUNKS:
                    return
                size = chunk_size(c.static)
                dve.wait_ge(hi_made, (c + 1).v())
                dve.tensor_tensor(wl[:, c.slot(4), 0:size], raw[:, c.slot(2), 0:size],
                                  wh[:, c.slot(4), 0:size].bitcast(F32), ALU.subtract).then_inc(lo_made, 1)

            def read(j):
                dve.wait_ge(lin_ready, (j + 1).v())
                return lin[j.slot(2)]

            def freed(ins, j):
                ins.then_inc(lin_freed[j.slot(2)], 1)

            def low(dst, whole, high, high_sem, k, low_sem):
                dve.wait_ge(high_sem, k)
                dve.tensor_tensor(dst, whole, high.bitcast(F32), ALU.subtract).then_inc(low_sem, 1)

            def norm_rstd(name, dst=rstd):
                k, n = NORM_NO[name], NTOK.get(name, S) // P
                dve.wait_ge(std_made, k + 1)
                dve.reciprocal(dst[:, 0:n], std[:, 0:n]).then_inc(rstd_made, 1)
                dve.wait_ge(rstd_made, k + 1)

            def diagonal(name, r_, squared=False):
                for q in range(NTOK.get(name, S) // P):
                    at = r_[:, q:q + 1]
                    ins = dve.tensor_scalar(te[:, q * P:(q + 1) * P], ident[:], at, at if squared else None, ALU.mult,
                                            *((ALU.mult,) if squared else ()))
                ins.then_inc(diag_made, 1)

            def norm_diag(name):
                norm_rstd(name)
                diagonal(name, rstd)

            def norm_apply(name, gain, src, hi, lo):
                n = SPLIT_TILES[name]
                dve.wait_ge(bc_ready, BC_NO[name] + 1)
                for f in range(n + 1):
                    u = U0[name] + f
                    if f < n:
                        wait(dve, u_low, u - 1)
                        dve.scalar_tensor_tensor((tc, td)[u % 2][:], src(f), col(gain, f), tr[0][:], ALU.mult, ALU.mult)\
                            .then_inc(u_made, 1)
                    if f:
                        dve.wait_ge(u_made, NORMED0[name] + f)
                        low(lo[:, f - 1, :], (tc, td)[(u - 1) % 2][:], hi[:, f - 1, :], u_high, u, u_low)

            def gain_low(dst, src, gain, high, k):
                dve.wait_ge(u_high, k)
                dve.scalar_tensor_tensor(dst, src, gain, high.bitcast(F32), ALU.mult, ALU.subtract).then_inc(u_low, 1)

            def maxima(n):
                for q in range(QT):
                    at = now(dve, n.times(3, SCORES_AT[q]))
                    dve.wait_ge(pool_made, 2)
                    wait(dve, scores_ready, at)
                    b, o = SBANK[q]
                    dve.tensor_tensor_reduce(logit[:, LOFF[q]:LOFF[q] + KEYS[q]], sc[b][:, o:o + KEYS[q]],
                                             bias[:, S - KEYS[q]:S], 1.0, 3e38, ALU.add, ALU.min,
                                             nmax[:, q:q + 1]).then_inc(logits_made, 1)

            def middle(n):
                wait(dve, probs_made, n.times(4, 4))
                wait(dve, out_copied, n.times(1, 1))
                dve.reciprocal(rden, den).then_inc(rden_made, 1)
                wait(dve, pt_ready, n.times(3, 2))
                dve.tensor_copy(pt[:, 512:896], tr[1][:, 0:384]).then_inc(pt_dve, 1)

            def outputs(n, dst):
                wait(dve, rden_made, n.times(1, 1))
                wait(dve, out_ready, n.times(1, 1))
                dve.tensor_tensor(dst, ob[:, 0:QT * VD].rearrange("p (q d) -> p q d", q=QT),
                                  rden.unsqueeze(2).broadcast_to([P, QT, VD]), ALU.mult).then_inc(out_copied, 1)

            for k, s_ in enumerate((logits_made, pt_act, pt_dve, out_copied, mix_read, yb_low, ya_made, gsq_added,
                                    hsq_added)):
                dve.memset(small[:, 64 + k:65 + k], 0.0).then_inc(s_, 1)
            dve.memset(ones[:], 1.0).then_inc(start_made, 1)
            dve.memset(small[:, 0:1], EPS)
            dve.memset(small[:, 1:2], 4 * EPS).then_inc(start_made, 1)
            dve.memset(z[:, :, 0:PAD], 0.0).then_inc(start_made, 1)
            dve.memset(trig[0:64, :], 1.0).then_inc(start_made, 1)
            dve.memset(sel[:], 0.0).then_inc(start_made, 1)
            dve.wait_ge(start_made, 5)
            dve.wait_ge(pool_made, 1)
            for o in (64, 96):
                dve.tensor_tensor(sel[64:128, o:o + 32], ident[64:128, 64:96], ident[64:128, 96:128], ALU.add)\
                    .then_inc(start_made, 1)
            dve.wait_ge(vec_ready, 1)
            dve.tensor_copy(cols[:], tr[0][:, 0:NVEC]).then_inc(vec_copied, 1)
            dve.wait_ge(vec_copied, 1)
            step(dve.tensor_tensor(both[:], cols[:, COL["final_norm_g"]:COL["final_norm_g"] + DT],
                                   cols[:, COL["g_norm_2"]:COL["g_norm_2"] + DT], ALU.mult))
            step(dve.tensor_scalar(hb, cols[:, COL["conv_ln_b"]:COL["conv_ln_b"] + CT], 0.5, None, ALU.mult))
            norm_rstd("mix")
            for q in range(QT):
                ins = dve.tensor_scalar(te[:, q * P:(q + 1) * P], ident[:], rstd[:, q:q + 1], None, ALU.mult)
            ins.then_inc(x_diag, 1)
            lower(Idx(0))
            for f in range(DT):
                dve.wait_ge(xt_ready, f + 1)
                gain_low(ul[:, f, :], sc[f % 3][:], col("norm_mix_g", f), uh[:, f, :], f + 1)
            lower(Idx(1))

            def rope_arguments():
                r = slice(64, 128)
                dve.wait_ge(consts_landed, 16)
                dve.wait_ge(pos_landed, 16)
                ang, tmp = kt[r, :], logit[r, 0:S]
                freq, c_a, c_b, c_c = (consts[r, k:k + 1] for k in range(4))
                step(dve.tensor_copy(tmp, qt[r, :].bitcast(I32)))
                step(dve.tensor_scalar(ang, tmp, freq, None, ALU.mult))
                step(dve.tensor_scalar(tmp, ang, float(np.float32(1 / (2 * np.pi))), ROUND, ALU.mult, ALU.add))
                step(dve.tensor_scalar(tmp, tmp, -ROUND, None, ALU.add))
                for part in TWO_PI:
                    step(dve.scalar_tensor_tensor(ang, tmp, -part, ang, ALU.mult, ALU.add))
                step(dve.tensor_scalar(ang, ang, 3.141592, -3.141592, ALU.min, ALU.max))
                step(dve.scalar_tensor_tensor(tmp, ang, -1.0, ang, ALU.mult, ALU.max))
                step(dve.tensor_scalar(tmp, tmp, c_b, c_c, ALU.mult, ALU.add))
                dve.scalar_tensor_tensor(ang, ang, c_a, tmp, ALU.mult, ALU.add).then_inc(trig_arg, 1)

            c, j = phase("latent")
            for m in range(6):
                lower(c + (m + 2))
                if m == 1:
                    rope_arguments()
                if m == 0:
                    dve.wait_ge(vec_ready, 2)
                    dve.tensor_copy(taps[:].rearrange("p (t w) -> p t w", t=CT),
                                    tr[1][:, 0:CT * 32].rearrange("p (t w) -> p t w", t=CT)[:, :, 0:TAPS])\
                        .then_inc(vec_copied, 1)
                if m == 3:
                    norm_diag("q")
            for m in range(3):
                evacuated(dve, j + m)
            norm_apply("q", "q_norm_g", lambda f: cq[:, f, :], cqh, cql)
            dve.wait_ge(trig_made, 1)
            freed(dve.tensor_tensor(logit[:, 0:S], read(j + 5)[:], trig[:], ALU.mult), j + 5)
            c, j = phase("conv")
            lower(c + 2)
            dve.wait_ge(kr_ready, 1)
            dve.tensor_copy(kt[64:128, :], sc[0][64:128, :]).then_inc(kr_placed, 1)
            norm_diag("kv")
            for m in range(1, 8):
                if m == 2:
                    for k in (3, 4):
                        evacuated(dve, Idx(JOB0["latent"] + k))
                    norm_apply("kv", "kv_norm_g", lambda f: cq[:, 3 + f, :], ckh, ckl)
                lower(c + (m + 2))
                if m % 2:
                    t = m // 2
                    evacuated(dve, j + (m - 1))
                    evacuated(dve, j + m)
                    th = (logit[:, 512:1024], pt[:, 0:512])[t % 2]
                    zt = z[:, t, PAD:PAD + S]
                    dve.scalar_tensor_tensor(zt, th, 1.0, zt, ALU.add, ALU.mult).then_inc(z_made, 1)

            dve.wait_ge(z_made, CT)
            dve.wait_ge(pool_made, 2)

            def head(c, j, n, run):
                freed(dve.scalar_tensor_tensor(qt[:], read(j)[:], LINEAR_Q_SCALE, trig[:], ALU.mult, ALU.mult), j)
                lower(c + 3)
                run(0)
                wait(dve, vtr_ready, n.times(1, 1))
                dve.tensor_copy(vtok[:, :, 0:VD], ob[:, 256:512].rearrange("p (q d) -> p q d", q=QT))\
                    .then_inc(vtok_placed, 1)
                maxima(n)
                lower(c + 4)
                lower(c + 5)
                run(1)
                middle(n)
                run(2)
                at = n.times(VD)
                outputs(n, otok[:, :, at:at + VD] if n.i is None else otok[:, :, bass.ds(at, VD)])
                lower(c + 6)

            def two_heads(c, j, t, n):
                def tap(w):
                    zt, at = z[:, t, w % TAPS:w % TAPS + S], (acc[:, t, :], te[:])[w % 2]
                    k = (TAPS + 1) * t + w
                    tap_ = taps[:, bass.ds(TAPS * t + w % TAPS, 1)]
                    if w:
                        dve.wait_ge(tap_done, k - (1 < w < TAPS))
                    if w == 0:
                        ins = dve.tensor_scalar(at, zt, tap_, cols[:, bass.ds(COL["conv_b"] + t, 1)], ALU.mult, ALU.add)
                    elif w == 1:
                        ins = dve.tensor_scalar(at, zt, tap_, None, ALU.mult)
                    elif w < TAPS:
                        ins = dve.scalar_tensor_tensor(at, zt, tap_, at, ALU.mult, ALU.add)
                    else:
                        ins = dve.tensor_tensor(acc[:, t, :], acc[:, t, :], te[:], ALU.add)
                    ins.then_inc(tap_done, 1)

                for p, cuts in ((0, (0, 6, 11, 16)), (1, (16, 22, 27, TAPS + 1))):
                    head(c + 4 * p, j + 4 * p, n + p, lambda k: [tap(w) for w in range(cuts[k], cuts[k + 1])])

            lower(phase("heads")[0] + 2)
            with dve.Fori(0, CT - 1) as i:
                two_heads(*phase("heads", 8, 8, i), i, Idx(0, 2, i))
            c, j = phase("heads")
            two_heads(c + 8 * (CT - 1), j + 8 * (CT - 1), CT - 1, Idx(2 * (CT - 1)))

            dve.wait_ge(mean_ready, 1)
            dve.wait_ge(tap_done, CT * (TAPS + 1))
            for t in range(CT):
                dve.scalar_tensor_tensor(acc[:, t, :], sc[0][:], -1.0 / CONV, acc[:, t, :], ALU.mult, ALU.add)\
                    .then_inc(centred, 1)
                low(ol[:, t, :], sc[1 + t % 2][:], oh[:, t, :], o_high, t + 1, o_low)
            c, j = phase("mla_out")

            def mla_out(f):
                g = gates[:, DT + f, :]
                freed(dve.scalar_tensor_tensor(g, g, 1.0, read(j + f)[:], ALU.add, ALU.mult), j + f)

            mla_out(0)
            lower(c + 3)
            lower(c + 4)
            mla_out(1)
            norm_diag("conv")
            mla_out(2)
            mla_out(3)
            dve.wait_ge(centred, CT)
            dve.wait_ge(bc_ready, BC_NO["conv"] + 1)
            for t in range(CT):
                dve.scalar_tensor_tensor(acc[:, t, :], acc[:, t, :], col("conv_ln_g", t), tr[0][:], ALU.mult, ALU.mult)\
                    .then_inc(y_norm, 1)
                if t % 2:
                    mla_out(4 + t // 2)

            def branch_low(t):
                low(yl[:, t, :], (tc, td)[t % 2][:], yh[:, t, :], y_high, t + 1, y_low)

            for t in range(CT):
                dve.wait_ge(y_tanh, t + 1)
                wait(dve, y_low, t - 1)
                dve.scalar_tensor_tensor((tc, td)[t % 2][:], (ta, tb)[t % 2][:], 1.0, (qt, kt)[t % 2][:], ALU.add,
                                         ALU.mult).then_inc(y_made, 1)
                if t:
                    branch_low(t - 1)
                if t == 2:
                    mla_out(6)
            branch_low(CT - 1)
            mla_out(7)
            lower(c + 5)

            def merge(f, j, mine, other, base):
                freed(dve.scalar_tensor_tensor(mine[:, f, :], mine[:, f, :], 1.0, read(j)[:], ALU.add, ALU.mult), j)
                evacuated(dve, j)
                wait(dve, m_low, base + f - 1)
                dve.tensor_tensor((tc, td)[f % 2][:], mine[:, f, :], other[:, f, :], ALU.add).then_inc(m_made, 1)
                if f:
                    merge_low(f - 1, base)

            def merge_low(f, base):
                low(ul[:, f, :], (tc, td)[f % 2][:], uh[:, f, :], m_high, base + f + 1, m_low)

            def add_to_h(f, j, scale=None):
                at = h[:, f, :]
                if scale is None:
                    freed(dve.tensor_tensor(at, read(j)[:], at, ALU.add), j)
                else:
                    freed(dve.scalar_tensor_tensor(at, read(j)[:], scale, at, ALU.mult, ALU.add), j)

            c, j = phase("conv_out")
            for m in range(4):
                lower(c + (m + 2))
                for f in (2 * m, 2 * m + 1):
                    merge(f, j + f, gates, gates[:, DT:2 * DT, :], 0)
            merge_low(DT - 1, 0)

            c, j = phase("w_out")
            for m in range(DT):
                lower(c + (m + 2))
                add_to_h(m, j + m, 0.5)
                dve.wait_ge(mem_high, m + 1)
                dve.scalar_tensor_tensor(meml[:, m, :], sc[m % 3][:, 0:MEM], col("norm_mem_g", m),
                                         memh[:, m, :].bitcast(F32), ALU.mult, ALU.subtract).then_inc(mem_low, 1)
                if m:
                    evacuated(dve, j + (m - 1))
                    gain_low(xul[:, m - 1, :], h[:, m - 1, :], col("norm_xattn_g", m - 1), xuh[:, m - 1, :],
                             U0["xattn"] + m)
            evacuated(dve, j + (DT - 1))
            gain_low(xul[:, DT - 1, :], h[:, DT - 1, :], col("norm_xattn_g", DT - 1), xuh[:, DT - 1, :],
                     U0["xattn"] + DT)
            norm_rstd("mem", mem_rstd)
            diagonal("mem", mem_rstd)
            c, j = phase("xkv")

            def place_values(hd):
                dve.wait_ge(xvt_ready, hd + 1)
                dve.tensor_tensor(xv[:, :, hd * XD:(hd + 1) * XD], ob[:, 0:256].rearrange("p (q d) -> p q d", q=2),
                                  mem_rstd.unsqueeze(2).broadcast_to([P, 2, XD]), ALU.mult).then_inc(xv_placed, 1)

            for m in range(8):
                lower(c + (m + 2))
                if m == 0:
                    dve.wait_ge(bc_ready, BC_NO["mem"] + 1)
                    dve.tensor_copy(mem_scale, tr[0][:, 0:MEM]).then_inc(mem_scaled, 1)
                    dve.wait_ge(mem_scaled, 1)
                if m < XH:
                    freed(dve.tensor_tensor(xk[:, m, :], read(j + m)[:, 0:MEM], mem_scale, ALU.mult), j + m)
                if m >= 6:
                    place_values(m - 6)
            norm_rstd("xattn")
            dve.tensor_scalar(minus_rstd, rstd, -1.0, None, ALU.mult).then_inc(minus_made, 1)
            def x_maxima(hd):
                for b in range(2):
                    dve.wait_ge(xs_ready, 2 * hd + b + 1)
                    s_, k = ((sc[0], sc[1]), (sc[2], ob))[hd % 2][b], 4 * (hd % 2) + 2 * b
                    dve.tensor_reduce(xnmax[:, k:k + 2], s_[:].rearrange("p (q k) -> p q k", q=2), AX_X, ALU.min)\
                        .then_inc(xmin_made, 1)
                    dve.wait_ge(xmin_made, 2 * hd + b + 1)
                    dve.tensor_tensor(xnmax[:, k:k + 2], xnmax[:, k:k + 2], rstd[:, 2 * b:2 * b + 2], ALU.mult)\
                        .then_inc(xmax_made, 1)

            def x_scale(hd):
                for b in range(2):
                    k = 4 * (hd % 2) + 2 * b
                    dve.wait_ge(xp_made, 4 * hd + 2 * b + 2)
                    dve.reciprocal(xrden[:, k:k + 2], xden[:, k:k + 2]).then_inc(xrden_made, 1)
                    dve.wait_ge(xrden_made, 2 * hd + b + 1)
                    p_ = xp[:, hd % 2, 2 * b:2 * b + 2, :]
                    dve.tensor_tensor(p_, p_, xrden[:, k:k + 2].unsqueeze(2).broadcast_to([P, 2, MEM]), ALU.mult)\
                        .then_inc(xp_scaled, 1)

            def x_copied(hd):
                dve.wait_ge(xpt_ready, 2 * hd + 2)
                dve.tensor_copy(xpt[:, hd % 2, :, 256:512], tr[1][:].rearrange("p (k q) -> p k q", k=2))\
                    .then_inc(xpt_dve, 1)

            def x_low(hd):
                dve.wait_ge(xo_ready, hd + 1)
                low(xol[:, hd, :], sc[2 * (hd % 2)][:], xoh[:, hd, :], xo_high, hd + 1, xo_low)

            c, _ = phase("xq")
            for m in range(XH):
                lower(c + (m + 2))
                if m < 2:
                    place_values(m + 2)
                if m:
                    x_maxima(m - 1)
                if m >= 2:
                    x_copied(m - 2)
                if m:
                    x_scale(m - 1)
                if m >= 2:
                    x_low(m - 2)
            x_copied(2)
            x_maxima(3)
            x_scale(3)
            x_low(2)
            x_copied(3)
            x_low(3)
            c, j = phase("xo")
            for m in range(4):
                lower(c + (m + 2))
                for f in (2 * m, 2 * m + 1):
                    add_to_h(f, j + f)
                    evacuated(dve, j + f)
                    gain_low(ul[:, f, :], h[:, f, :], col("norm_mlp_g", f), uh[:, f, :], U0["mlp"] + f + 1)

            def up(half, trip):
                c, j = phase(f"up{half}", 4, 4, trip)
                f = Idx(16 * half, 4, trip)
                for m in range(4):
                    lower(c + (m + 2))
                    evacuated(dve, j + m)
                    r_ = (ta, tb)[m % 2][:]
                    wait(dve, f_low, f.times(1, m))
                    dve.tensor_tensor((tc, td)[m % 2][:], r_, r_, ALU.mult).then_inc(f_sq, 1)
                    low(fl[:, 4 * trip + m, :], (tc, td)[m % 2][:], fh[:, 4 * trip + m, :], f_high,
                        f.times(1, m + 1), f_low)

            up(0, 0)
            norm_rstd("mlp")
            diagonal("mlp", rstd, squared=True)
            for half in range(2):
                with dve.Fori(1 - half, 4) as i:
                    up(half, i)
                if half == 0:
                    dve.wait_ge(bc_ready, BC_NO["mlp"] + 1)
                    dve.tensor_copy(mlp_scale, tr[0][:]).then_inc(mlp_scaled, 1)
                    dve.wait_ge(mlp_scaled, 1)
                with dve.Fori(0, 4) as i:
                    c, j = phase(f"down{half}", 4, 2, i)
                    for m in range(2):
                        lower(c + (2 * m + 2))
                        lower(c + (2 * m + 3))
                        f, part = Idx(m, 2, i), (tc, td)[m]
                        freed(dve.tensor_tensor(part[:], read(j + m)[:], mlp_scale, ALU.mult), j + m)
                        evacuated(dve, j + m)
                        at = h[:, f.v(), :]
                        dve.tensor_tensor(at, part[:], at, ALU.add).then_inc(h_added, 1)
                        if half == 1:
                            dve.wait_ge(u_high, f.times(1, U0["raw"] + 1))
                            dve.scalar_tensor_tensor(ul[:, f.v(), :], at, both[:, bass.ds(f.v(), 1)],
                                                     uh[:, f.v(), :].bitcast(F32), ALU.mult, ALU.subtract)\
                                .then_inc(u_low, 1)
                if half == 0:
                    dve.wait_ge(pool_made, 3)
                    dint = atok[:].rearrange("p a b -> p (a b)").bitcast(I32)
                    tint = rbc[:].bitcast(I32)
                    step(dve.tensor_scalar(tint, dint, 3, None, ALU.bitwise_and))
                    step(dve.tensor_scalar(nlog[:], tint, 0.0, None, ALU.is_equal))
                    step(dve.tensor_scalar(tint, dint, 15, None, ALU.bitwise_and))
                    step(dve.tensor_scalar(bias[:], tint, 0.0, None, ALU.is_equal))
                    step(dve.tensor_tensor(nlog[:], nlog[:], bias[:], ALU.add))
                    step(dve.tensor_scalar(bias[:], dist[:], 128.0, None, ALU.is_le))
                    step(dve.tensor_tensor(nlog[:], nlog[:], bias[:], ALU.add))
                    step(dve.tensor_scalar(rbc[:], nlog[:], 2.0, -float(np.log(2.0)), ALU.is_equal, ALU.mult))
                    step(dve.tensor_scalar(bias[:], nlog[:], 3.0, -float(np.log(3.0)), ALU.is_equal, ALU.mult))
                    step(dve.tensor_tensor(rbc[:], rbc[:], bias[:], ALU.add))
                    step(dve.tensor_scalar(bias[:], nlog[:], 0.0, BIG, ALU.is_equal, ALU.mult))
                    dve.tensor_tensor(nlog[:], rbc[:], bias[:], ALU.add).then_inc(table_made, 1)

            c, j = phase("av")
            lower(c + 2)
            k = NORM_NO["second"]
            dve.wait_ge(std_made, k + 1)
            step(dve.reciprocal(final_rstd, std))
            step(dve.scalar_tensor_tensor(final_sq, tr[1][:, 4:8], 1.0 / D, final_rstd, ALU.mult, ALU.mult))
            dve.tensor_tensor(final_sq, final_sq, final_rstd, ALU.mult).then_inc(rstd_made, 1)
            norm_rstd("final")
            step(dve.tensor_tensor(rstd, rstd, final_rstd, ALU.mult))
            diagonal("second", rstd)
            dve.wait_ge(bc_ready, BC_NO["second"] + 1)
            dve.tensor_copy(rbc[:], tr[0][:]).then_inc(rbc_made, 1)
            dve.wait_ge(rbc_made, 1)

            def gelu(j, k, dst):
                dve.wait_ge(g_square, k)
                dve.scalar_tensor_tensor(tb[:], ta[:], 1.0 / GELU_A, read(j)[:], ALU.add, ALU.mult).then_inc(g_poly, 1)
                dve.wait_ge(g_tanh, k)
                freed(dve.scalar_tensor_tensor(dst, ta[:], 1.0, read(j)[:], ALU.add, ALU.mult), j)

            def normed_input(f):
                u = U0["second"] + f
                wait(dve, u_low, u - 1)
                dve.scalar_tensor_tensor((tc, td)[u % 2][:], h[:, f, :], both[:, f:f + 1], rbc[:], ALU.mult, ALU.mult)\
                    .then_inc(u_made, 1)

            def normed_low(f):
                u = U0["second"] + f
                dve.wait_ge(u_made, NORMED0["second"] + f + 1)
                low(vl[:, f, :], (tc, td)[u % 2][:], vh[:, f, :], u_high, u + 1, u_low)

            for m in range(PAIRS):
                if m:
                    lower(c + (m + 2))
                freed(dve.tensor_tensor(scaled, read(j + m)[:], rbc[:], ALU.mult), j + m)
                evacuated(dve, j + m)
                for f in NORMED_IN[m][0:1]:
                    normed_input(f)
                dve.wait_ge(g_square, m + 1)
                dve.scalar_tensor_tensor(tb[:], ta[:], 1.0 / GELU_A, scaled, ALU.add, ALU.mult).then_inc(g_poly, 1)
                for f in NORMED_IN[m][0:1]:
                    normed_low(f)
                dve.wait_ge(g_tanh, m + 1)
                dve.scalar_tensor_tensor(av[:, m, :], ta[:], 1.0, scaled, ALU.add, ALU.mult).then_inc(gating_made, 1)
                for f in NORMED_IN[m][1:]:
                    normed_input(f)
                    normed_low(f)
                dve.wait_ge(gating_made, m + 1)
            dve.wait_ge(pool_made, 4)

            def mask(n, k):
                dve.wait_ge(logits_made, n.times(4, 1))
                dve.scalar_tensor_tensor(bias[:], dist[:], consts[:, bass.ds(4 + k, 1)], nlog[:], ALU.mult, ALU.add)\
                    .then_inc(bias_made, 1)
                dve.wait_ge(bias_made, (n + (1 - HEADS)).v())

            lower(phase("pairs")[0] + 2)
            norm_rstd("gate_v")
            with dve.Fori(0, PAIRS) as i:
                c, j = phase("pairs", 8, 8, i)
                g, n0, n1 = Idx(0, 1, i), Idx(HEADS, 2, i), Idx(HEADS + 1, 2, i)
                lower(c + 3)
                freed(dve.tensor_copy(kt[:], read(j + 1)[:]), j + 1)
                lower(c + 4)
                dve.wait_ge(yb_low, g.times(1, 1))
                dve.tensor_scalar(tc[:], av[:, i, :], cols[:, bass.ds(COL["g_v_2"] + i, 1)], None, ALU.mult)\
                    .then_inc(gv_made, 1)
                mask(n0, 2 * i)
                lower(c + 5)
                maxima(n0)
                dve.wait_ge(vtr_ready, g.times(1, HEADS + 1))
                dve.tensor_copy(vtok[:].rearrange("p q d -> p (q d)"), tr[0][:]).then_inc(vtok_placed, 1)
                gelu(j + 3, g.times(1, PAIRS + 1), tb[:])
                mask(n1, 2 * i + 1)
                middle(n0)
                outputs(n0, otp[:, :, 0:VD])
                lower(c + 6)
                maxima(n1)
                dve.wait_ge(silu_tanh, g.times(2, 1))
                freed(dve.scalar_tensor_tensor(te[:], ta[:], 1.0, read(j + 4)[:], ALU.add, ALU.mult), j + 4)
                evacuated(dve, j + 4)
                evacuated(dve, j + 3)
                dve.scalar_tensor_tensor(tb[:], tb[:], 0.25, te[:], ALU.mult, ALU.mult).then_inc(gate_prod, 1)
                dve.wait_ge(gvt_ready, g.times(1, 1))
                dve.tensor_tensor(atok[:], tr[1][:].rearrange("p (q d) -> p q d", q=QT),
                                  rstd.unsqueeze(2).broadcast_to([P, QT, P]), ALU.mult).then_inc(atok_placed, 1)
                lower(c + 7)
                dve.wait_ge(gate_prod, g.times(1, 1))
                dve.wait_ge(silu_tanh, g.times(2, 2))
                freed(dve.scalar_tensor_tensor(te[:], ta[:], 1.0, read(j + 5)[:], ALU.add, ALU.mult), j + 5)
                middle(n1)
                outputs(n1, otp[:, :, VD:P])
                lower(c + 8)
                dve.wait_ge(ob_ready, g.times(1, 1))
                evacuated(dve, j + 5)
                dve.scalar_tensor_tensor(tc[:], tr[0][:], 0.5, te[:], ALU.mult, ALU.mult).then_inc(yb_made, 1)
                dve.wait_ge(mix_ready, g.times(1, 1))
                dve.tensor_tensor(ta[:].rearrange("p (q t) -> p q t", q=QT), tr[1][:].rearrange("p (q t) -> p q t", q=QT),
                                  bsb.unsqueeze(1).broadcast_to([P, QT, P]), ALU.add).then_inc(mix_read, 1)
                dve.wait_ge(mix_read, g.times(1, 2))
                dve.wait_ge(gate_prod, g.times(1, 1))
                dve.tensor_tensor(ya[:, i, :], ta[:], tb[:], ALU.mult).then_inc(ya_made, 1)
                low(ybl[:, i, :], tc[:], ybh[:, i, :], yb_high, g.times(1, 1), yb_low)
                lower(c + 9)
                lower(c + 10)

            dve.wait_ge(yb_made, PAIRS)
            diagonal("final", final_rstd)
            c, j = phase("proj_b")
            for m in range(DT):
                if m:
                    lower(c + (m + 2))
                at = gb[:, m, :]
                freed(dve.scalar_tensor_tensor(at, at, 1.0, read(j + m)[:], ALU.add, ALU.mult), j + m)
                low(vl[:, m, :], ya[:, m, :], vh[:, m, :], ya_high, m + 1, ya_low)
                dve.wait_ge(bc_ready, BC_NO["final"] + 1)
                dve.scalar_tensor_tensor(h[:, m, :], h[:, m, :], col("final_norm_g", m), tr[0][:], ALU.mult,
                                         ALU.mult).then_inc(x1_made, 1)
            evacuated(dve, j + (DT - 1))
            c, j = phase("proj_a")
            for m in range(DT):
                lower(c + (m + 2))
                merge(m, j + m, av, gb, DT)
            merge_low(DT - 1, DT)
            c, j = phase("w_out2")
            dve.wait_ge(x1_made, DT)
            for m in range(DT):
                lower(c + (m + 2))
                add_to_h(m, j + m, 0.5)
                evacuated(dve, j + m)
                wait(dve, fin_ready, m - 1)
                dve.tensor_scalar((tc, td)[m % 2][:], h[:, m, :], col("g_final_2", m), None, ALU.mult).then_inc(fin_made, 1)
            norm_rstd("out")
            dve.wait_ge(fin_copied, DT)
            for q in range(2):
                dve.tensor_scalar(fin[:, q, :], fin[:, q, :], rstd[:, q:q + 1], None, ALU.mult).then_inc(fin_scaled_vector, 1)


USED = ["x", "mem", "positions", "norm_mix_g", "w_in", "conv_w", "conv_b", "conv_ln_g", "conv_ln_b", "w_conv_out",
        "q_norm_g", "w_uq", "kv_norm_g", "w_ukv", "w_mla_out", "w_out", "norm_xattn_g", "norm_mem_g", "w_xq", "w_xkv",
        "w_xo", "norm_mlp_g", "w_mlp1", "w_mlp2", "final_norm_g", "g_norm_2", "w_in_2", "w_s_2", "b_s_2", "g_v_2",
        "w_proj_a_2", "w_proj_b_2", "w_out_2", "g_final_2"]


def shape_consts():
    c = np.zeros((P, NCONST), np.float32)
    half = ROPE // 2
    freq = np.float32(10000.0) ** (-np.arange(half, dtype=np.float32) / np.float32(half))
    c[64:, 0] = np.tile(freq, 4)
    c[64:96, 2], c[64:96, 3] = -1.0, np.float32(np.pi / 2)
    c[96:112, 1], c[112:, 1] = -1.0, 1.0
    c[:, 4:] = np.float32(2.0) ** (np.float32(-0.5) * np.arange(1, 17, dtype=np.float32))
    return c


def kernel(**inputs):
    import concourse.bacc as bacc
    from concourse.bass_utils import run_bass_kernel_spmd

    nc = bacc.Bacc("TRN2", target_bir_lowering=False, num_devices=1)
    arrays = {f"in_{n}_dram": np.ascontiguousarray(inputs[n]) for n in USED}
    arrays["in_shape_consts_dram"] = shape_consts()
    aps = {}
    for name, v in arrays.items():
        aps[name[3:-5]] = nc.dram_tensor(name, v.shape, mybir.dt.from_np(v.dtype), kind="ExternalInput").ap()
    out = nc.dram_tensor("out_0_dram", (1, S, D), F32, kind="ExternalOutput").ap()
    build(nc, aps, out)
    r = run_bass_kernel_spmd(nc, [arrays], core_ids=[0])
    return r.results[0]["out_0_dram"]
```
